# Optimizing a Trainium2 kernel written in Bass

```python
import math
import jax, jax.numpy as jnp
from jax import lax
import numpy as np
import jax
import jax.numpy as jnp

D_MODEL = 1024
BATCH = 1
SEQ = 256
DEPTH = 1

N_MEM = 256
D_MIX = D_MODEL
D_MLSTM = D_MIX // 2
N_MLSTM_HEADS = 4
MLSTM_HEAD_DIM = D_MLSTM // N_MLSTM_HEADS
MLSTM_CHUNK = 128
CONV_WIDTH = 5
D_GMLP = D_MIX - D_MLSTM
N_GMLP_GROUPS = 4
GMLP_GROUP_DIM = D_GMLP // N_GMLP_GROUPS
GMLP_CHUNK = 128
N_GATES = 4 * N_MLSTM_HEADS
PROJ_COLS = 4 * D_MLSTM + N_GATES + 2 * D_GMLP
N_XATTN_HEADS = 4
XATTN_HEAD_DIM = D_MODEL // N_XATTN_HEADS
N_EXPERT_GROUPS = 4
EXPERTS_PER_GROUP = 8
N_EXPERTS = N_EXPERT_GROUPS * EXPERTS_PER_GROUP
TOP_K_IN_GROUP = 2
D_EXPERT = D_MODEL // 2
MOE_BLOCK = 128
RMS_EPS = 1e-6
LN_EPS = 1e-5
NEG_INIT = -1e30


def rms_norm(x, g):
    xf = x.astype(jnp.float32)
    y = xf * lax.rsqrt(jnp.mean(xf * xf, axis=-1, keepdims=True) + RMS_EPS)
    return (y * g.astype(jnp.float32)).astype(x.dtype)

def layer_norm(x, g, b):
    xf = x.astype(jnp.float32)
    mu = jnp.mean(xf, axis=-1, keepdims=True)
    xc = xf - mu
    y = xc * lax.rsqrt(jnp.mean(xc * xc, axis=-1, keepdims=True) + LN_EPS)
    return (y * g.astype(jnp.float32) + b.astype(jnp.float32)).astype(x.dtype)

def mlstm_chunkwise(q, k, v, i_pre, f_pre):
    Bq, H, S, dh = q.shape
    L = MLSTM_CHUNK
    NC = S // L
    q = q.reshape(Bq, H, NC, L, dh)
    k = k.reshape(Bq, H, NC, L, dh) * (dh ** -0.5)
    v = v.reshape(Bq, H, NC, L, dh)
    ig = i_pre.reshape(Bq, H, NC, L)
    b = jnp.cumsum(jax.nn.log_sigmoid(f_pre.reshape(Bq, H, NC, L)), axis=-1)
    F = b[..., -1]
    a = F[..., None] - b + ig
    m_loc = jnp.max(a, axis=-1)
    kw = k * jnp.exp(a - m_loc[..., None])[..., None]
    C_loc = jnp.einsum('bhcsd,bhcse->bhcde', kw, v)
    n_loc = jnp.sum(kw, axis=-2)

    def step(carry, inp):
        C, n, m = carry
        F_c, m_c, C_c, n_c = inp
        m_new = jnp.maximum(F_c + m, m_c)
        s_old = jnp.exp(F_c + m - m_new)
        s_new = jnp.exp(m_c - m_new)
        C_new = s_old[..., None, None] * C + s_new[..., None, None] * C_c
        n_new = s_old[..., None] * n + s_new[..., None] * n_c
        return (C_new, n_new, m_new), (C, n, m)

    init = (jnp.zeros((Bq, H, dh, dh), jnp.float32),
            jnp.zeros((Bq, H, dh), jnp.float32),
            jnp.full((Bq, H), NEG_INIT, jnp.float32))
    xs = (jnp.moveaxis(F, 2, 0), jnp.moveaxis(m_loc, 2, 0),
          jnp.moveaxis(C_loc, 2, 0), jnp.moveaxis(n_loc, 2, 0))
    _, (C_prev, n_prev, m_prev) = lax.scan(step, init, xs)
    C_prev = jnp.moveaxis(C_prev, 0, 2)
    n_prev = jnp.moveaxis(n_prev, 0, 2)
    m_prev = jnp.moveaxis(m_prev, 0, 2)

    mask = jnp.tril(jnp.ones((L, L), dtype=bool))
    Dm = jnp.where(mask, b[..., :, None] - b[..., None, :] + ig[..., None, :], -jnp.inf)
    inter = b + m_prev[..., None]
    m_t = jnp.maximum(inter, jnp.max(Dm, axis=-1))
    Wqk = jnp.exp(Dm - m_t[..., None]) * jnp.einsum('bhctd,bhcsd->bhcts', q, k)
    s_inter = jnp.exp(inter - m_t)
    num = (jnp.einsum('bhcts,bhcse->bhcte', Wqk, v)
           + s_inter[..., None] * jnp.einsum('bhctd,bhcde->bhcte', q, C_prev))
    den = jnp.sum(Wqk, axis=-1) + s_inter * jnp.einsum('bhctd,bhcd->bhct', q, n_prev)
    h = num / jnp.maximum(jnp.abs(den), jnp.exp(-m_t))[..., None]
    return h.reshape(Bq, H, S, dh)

def parallel_mixer(h, w_in, conv_w, conv_b, gate_b, g_head, ln_v_g, ln_v_b, w_s, b_s, w_out):
    Bq, S, _ = h.shape
    z = h @ w_in
    cuts = [D_MLSTM, 2 * D_MLSTM, 3 * D_MLSTM, 4 * D_MLSTM,
            4 * D_MLSTM + N_GATES, 4 * D_MLSTM + N_GATES + D_GMLP]
    q, k, v, o, gates, gu, gv = jnp.split(z, cuts, axis=-1)

    qk = lax.conv_general_dilated(jnp.concatenate([q, k], axis=-1), conv_w, (1,), 'SAME',
                                  dimension_numbers=('NWC', 'WIO', 'NWC'),
                                  feature_group_count=2 * D_MLSTM)
    qk = jax.nn.silu(qk + conv_b)
    q, k = qk[..., :D_MLSTM], qk[..., D_MLSTM:]

    def heads(t):
        return t.reshape(Bq, S, N_MLSTM_HEADS, MLSTM_HEAD_DIM).transpose(0, 2, 1, 3).astype(jnp.float32)

    qh, kh, vh = heads(q), heads(k), heads(v)
    g = (gates.astype(jnp.float32) + gate_b.astype(jnp.float32)).reshape(Bq, S, 4, N_MLSTM_HEADS)
    g = g.transpose(2, 0, 3, 1)
    i_f, f_f, i_b, f_b = g[0], g[1], g[2], g[3]

    def flip(t):
        return jnp.flip(t, axis=2)

    h_fwd = mlstm_chunkwise(qh, kh, vh, i_f, f_f)
    h_bwd = flip(mlstm_chunkwise(flip(qh), flip(kh), flip(vh), flip(i_b), flip(f_b)))
    hs = h_fwd + h_bwd
    gh = g_head.astype(jnp.float32).reshape(N_MLSTM_HEADS, 1, MLSTM_HEAD_DIM)
    hs = hs * lax.rsqrt(jnp.mean(hs * hs, axis=-1, keepdims=True) + RMS_EPS) * gh
    hs = hs.transpose(0, 2, 1, 3).reshape(Bq, S, D_MLSTM)
    y_mlstm = (jax.nn.sigmoid(o.astype(jnp.float32)) * hs).astype(h.dtype)

    gu = jax.nn.gelu(gu)
    gv = layer_norm(jax.nn.gelu(gv), ln_v_g, ln_v_b)
    NC = S // GMLP_CHUNK
    gv = gv.reshape(Bq, NC, GMLP_CHUNK, N_GMLP_GROUPS, GMLP_GROUP_DIM)
    sp = jnp.einsum('gts,bcsgd->bctgd', w_s, gv) + b_s.T[:, :, None]
    y_gmlp = gu * sp.reshape(Bq, S, D_GMLP)

    return jnp.concatenate([y_mlstm, y_gmlp], axis=-1) @ w_out

def memory_cross_attention(h, hm, w_q, w_kv, w_o):
    Bq, S, _ = h.shape
    M = hm.shape[1]
    q = (h @ w_q).reshape(Bq, S, N_XATTN_HEADS, XATTN_HEAD_DIM)
    kv = (hm @ w_kv).reshape(Bq, M, 2, N_XATTN_HEADS, XATTN_HEAD_DIM)
    k, v = kv[:, :, 0], kv[:, :, 1]
    s = jnp.einsum('bshd,bmhd->bhsm', q, k).astype(jnp.float32) * (XATTN_HEAD_DIM ** -0.5)
    p = jax.nn.softmax(s, axis=-1).astype(h.dtype)
    o = jnp.einsum('bhsm,bmhd->bshd', p, v).reshape(Bq, S, N_XATTN_HEADS * XATTN_HEAD_DIM)
    return o @ w_o

def hier_moe(h, w_rg, b_rg, w_re, b_re, w_gate, w_up, w_down):
    T, D = h.shape
    g_logits = (h @ w_rg).astype(jnp.float32) + b_rg.astype(jnp.float32)
    p_group = jax.nn.softmax(g_logits, axis=-1)
    p_top, g_idx = lax.top_k(p_group, 1)
    e_logits = ((h @ w_re).astype(jnp.float32) + b_re.astype(jnp.float32)).reshape(
        T, N_EXPERT_GROUPS, EXPERTS_PER_GROUP)
    e_logits = jnp.take_along_axis(e_logits, g_idx[:, :, None], axis=1)[:, 0]
    e_top, e_local = lax.top_k(e_logits, TOP_K_IN_GROUP)
    weights = p_top * jax.nn.softmax(e_top, axis=-1)
    expert_id = g_idx * EXPERTS_PER_GROUP + e_local

    A = T * TOP_K_IN_GROUP
    e_flat = expert_id.reshape(A)
    t_flat = jnp.repeat(jnp.arange(T), TOP_K_IN_GROUP)
    w_flat = weights.reshape(A)
    order = jnp.argsort(e_flat)
    e_sorted, t_sorted, w_sorted = e_flat[order], t_flat[order], w_flat[order]
    counts = jnp.bincount(e_flat, length=N_EXPERTS)
    padded = ((counts + MOE_BLOCK - 1) // MOE_BLOCK) * MOE_BLOCK
    start = jnp.cumsum(counts) - counts
    pend = jnp.cumsum(padded)
    pstart = pend - padded
    dest = pstart[e_sorted] + (jnp.arange(A) - start[e_sorted])
    NB = A // MOE_BLOCK + N_EXPERTS
    P = NB * MOE_BLOCK
    x_disp = jnp.zeros((P, D), h.dtype).at[dest].set(h[t_sorted])
    blk_e = jnp.clip(jnp.searchsorted(pend, jnp.arange(NB) * MOE_BLOCK, side='right'), 0, N_EXPERTS - 1)

    def expert_block(args):
        xb, e = args
        return (jax.nn.silu(xb @ w_gate[e]) * (xb @ w_up[e])) @ w_down[e]

    y_disp = lax.map(expert_block, (x_disp.reshape(NB, MOE_BLOCK, D), blk_e)).reshape(P, D)
    contrib = (w_sorted[:, None] * y_disp[dest].astype(jnp.float32))
    out = jnp.zeros((T, D), jnp.float32).at[t_sorted].add(contrib)
    return out.astype(h.dtype)

def first_inputs(seed: int = 0) -> dict:
    key = jax.random.key(seed)
    ks = jax.random.split(key, 32)

    def nrm(k, shape, scale):
        return jax.random.normal(k, shape, jnp.float32) * scale

    def gain(k, shape):
        return 1.0 + 0.1 * jax.random.normal(k, shape, jnp.float32)

    H = N_MLSTM_HEADS
    f_bias = jnp.linspace(3.0, 6.0, H, dtype=jnp.float32)
    gk = jax.random.split(ks[6], 4)
    gate_b = jnp.concatenate([
        nrm(gk[0], (DEPTH, H), 0.1),
        f_bias + nrm(gk[1], (DEPTH, H), 0.1),
        nrm(gk[2], (DEPTH, H), 0.1),
        f_bias + nrm(gk[3], (DEPTH, H), 0.1)], axis=-1)
    return {
        'x': nrm(ks[0], (BATCH, SEQ, D_MODEL), 1.0),
        'mem': nrm(ks[1], (BATCH, N_MEM, D_MODEL), 1.0),
        'g_mix': gain(ks[2], (DEPTH, D_MODEL)),
        'w_in': nrm(ks[3], (DEPTH, D_MODEL, PROJ_COLS), D_MODEL ** -0.5),
        'conv_w': nrm(ks[4], (DEPTH, CONV_WIDTH, 1, 2 * D_MLSTM), CONV_WIDTH ** -0.5),
        'conv_b': nrm(ks[5], (DEPTH, 2 * D_MLSTM), 0.01),
        'gate_b': gate_b,
        'g_head': gain(ks[7], (DEPTH, D_MLSTM)),
        'ln_v_g': gain(ks[8], (DEPTH, D_GMLP)),
        'ln_v_b': nrm(ks[9], (DEPTH, D_GMLP), 0.01),
        'w_s': nrm(ks[10], (DEPTH, N_GMLP_GROUPS, GMLP_CHUNK, GMLP_CHUNK), GMLP_CHUNK ** -0.5),
        'b_s': gain(ks[11], (DEPTH, N_GMLP_GROUPS, GMLP_CHUNK)),
        'w_out': nrm(ks[12], (DEPTH, D_MIX, D_MODEL), D_MIX ** -0.5),
        'g_xattn': gain(ks[13], (DEPTH, D_MODEL)),
        'g_mem': gain(ks[14], (DEPTH, D_MODEL)),
        'w_q_x': nrm(ks[15], (DEPTH, D_MODEL, N_XATTN_HEADS * XATTN_HEAD_DIM), D_MODEL ** -0.5),
        'w_kv_x': nrm(ks[16], (DEPTH, D_MODEL, 2 * N_XATTN_HEADS * XATTN_HEAD_DIM), D_MODEL ** -0.5),
        'w_o_x': nrm(ks[17], (DEPTH, N_XATTN_HEADS * XATTN_HEAD_DIM, D_MODEL), D_MODEL ** -0.5),
        'g_moe': gain(ks[18], (DEPTH, D_MODEL)),
        'w_rg': nrm(ks[19], (DEPTH, D_MODEL, N_EXPERT_GROUPS), D_MODEL ** -0.5),
        'b_rg': nrm(ks[20], (DEPTH, N_EXPERT_GROUPS), 0.01),
        'w_re': nrm(ks[21], (DEPTH, D_MODEL, N_EXPERTS), D_MODEL ** -0.5),
        'b_re': nrm(ks[22], (DEPTH, N_EXPERTS), 0.01),
        'w_gate': nrm(ks[23], (DEPTH, N_EXPERTS, D_MODEL, D_EXPERT), D_MODEL ** -0.5),
        'w_up': nrm(ks[24], (DEPTH, N_EXPERTS, D_MODEL, D_EXPERT), D_MODEL ** -0.5),
        'w_down': nrm(ks[25], (DEPTH, N_EXPERTS, D_EXPERT, D_MODEL), D_EXPERT ** -0.5),
        'g_final': gain(ks[26], (D_MODEL,)),
    }

def first_block(x, mem, g_mix, w_in, conv_w, conv_b, gate_b, g_head, ln_v_g, ln_v_b, w_s, b_s, w_out,
              g_xattn, g_mem, w_q_x, w_kv_x, w_o_x, g_moe, w_rg, b_rg, w_re, b_re,
              w_gate, w_up, w_down, g_final):
    Bq, S, D = x.shape
    for l in range(DEPTH):
        x = x + parallel_mixer(rms_norm(x, g_mix[l]), w_in[l], conv_w[l], conv_b[l], gate_b[l],
                               g_head[l], ln_v_g[l], ln_v_b[l], w_s[l], b_s[l], w_out[l])
        x = x + memory_cross_attention(rms_norm(x, g_xattn[l]), rms_norm(mem, g_mem[l]),
                                       w_q_x[l], w_kv_x[l], w_o_x[l])
        x = x + hier_moe(rms_norm(x, g_moe[l]).reshape(Bq * S, D), w_rg[l], b_rg[l], w_re[l], b_re[l],
                         w_gate[l], w_up[l], w_down[l]).reshape(Bq, S, D)
    return rms_norm(x, g_final)


DEPTH_2 = 2

N_BRANCHES = 3
NORM_EPS = 1e-6
D_HYENA = 512
HYENA_EMB_DIM = 33
HYENA_FILTER_ORDER = 64
HYENA_FAST_DECAY_PCT = 0.3
HYENA_SLOW_DECAY_PCT = 1.5
HYENA_DECAY_TARGET = 1e-2
GLA_HEADS = 4
GLA_KEY_DIM = 512
GLA_VALUE_DIM = 512
GLA_HEAD_K = GLA_KEY_DIM // GLA_HEADS
GLA_HEAD_V = GLA_VALUE_DIM // GLA_HEADS
GLA_GATE_RANK = 16
GLA_GATE_NORMALIZER = 16.0
GLA_LOG_GATE_MIN = -1.0
GLA_CHUNK = 64
D_POOL = 512
POOL_WINDOWS = (2, 4, 8, 16)
POOL_GROUP = D_POOL // len(POOL_WINDOWS)
D_FF = 2816
IN_SPLITS = (3 * D_HYENA, GLA_KEY_DIM, GLA_KEY_DIM, GLA_VALUE_DIM, GLA_VALUE_DIM,
             2 * GLA_GATE_RANK, D_POOL, N_BRANCHES * D_MODEL)
D_IN = 3 * D_HYENA + 2 * GLA_KEY_DIM + 2 * GLA_VALUE_DIM + 2 * GLA_GATE_RANK + D_POOL + N_BRANCHES * D_MODEL


def _split(t, sizes):
    out, off = [], 0
    for s in sizes:
        out.append(t[..., off:off + s])
        off += s
    return out

def _rms_norm(x, g):
    xf = x.astype(jnp.float32)
    y = xf * lax.rsqrt(jnp.mean(xf * xf, axis=-1, keepdims=True) + NORM_EPS)
    return (y * g.astype(jnp.float32)).astype(x.dtype)

def _dwconv3_centred(x, w, b):
    L = x.shape[1]
    xp = jnp.pad(x, ((0, 0), (1, 1), (0, 0)))
    return xp[:, :L] * w[0] + xp[:, 1:L + 1] * w[1] + xp[:, 2:] * w[2] + b

def _hyena_positional_features(L):
    t = jnp.linspace(0.0, 1.0, L, dtype=jnp.float32)[:, None]
    bands = (HYENA_EMB_DIM - 1) // 2
    w = 2.0 * math.pi * jnp.arange(L, dtype=jnp.float32)[:, None] / L
    f = jnp.linspace(1e-4, bands - 1, bands, dtype=jnp.float32)[None, :]
    ang = f * w
    z = jnp.concatenate([t, jnp.cos(ang), -jnp.sin(ang)], axis=-1)
    return t, z

def _hyena_filter(t, z, w1, b1, fr1, w2, b2, fr2, w3):
    L = t.shape[0]
    h = jnp.sin(fr1 * (z @ w1 + b1))
    h = jnp.sin(fr2 * (h @ w2 + b2))
    h = (h @ w3).astype(jnp.float32)
    max_decay = math.log(HYENA_DECAY_TARGET) / HYENA_FAST_DECAY_PCT
    min_decay = math.log(HYENA_DECAY_TARGET) / HYENA_SLOW_DECAY_PCT
    deltas = jnp.linspace(min_decay, max_decay, D_HYENA, dtype=jnp.float32)
    decay = jnp.exp(-t * jnp.abs(deltas))
    h_fwd = h[:, :D_HYENA] * decay
    h_bwd = h[:, D_HYENA:] * decay
    zero = jnp.zeros((1, D_HYENA), jnp.float32)
    return jnp.concatenate([h_fwd, zero, h_bwd[:0:-1]], axis=0)

def _hyena_mixer(u, conv_w, conv_b, t, z, w1, b1, fr1, w2, b2, fr2, w3, bias):
    B, L, _ = u.shape
    u = _dwconv3_centred(u, conv_w, conv_b)
    x0, x1, v = _split(u, (D_HYENA, D_HYENA, D_HYENA))
    zv = (x1 * v).astype(jnp.float32)
    k = _hyena_filter(t, z, w1, b1, fr1, w2, b2, fr2, w3)
    Zf = jnp.fft.rfft(zv, n=2 * L, axis=1)
    Kf = jnp.fft.rfft(k, n=2 * L, axis=0)
    y = jnp.fft.irfft(Zf * Kf[None], n=2 * L, axis=1)[:, :L]
    y = y + zv * bias.astype(jnp.float32)
    return (x0.astype(jnp.float32) * y).astype(u.dtype)

def _gla_direction(q, k, v, log_a, include_diag):
    B, L, H, DK = q.shape
    DV = v.shape[-1]
    C = GLA_CHUNK
    N = L // C
    q = q.reshape(B, N, C, H, DK)
    k = k.reshape(B, N, C, H, DK)
    v = v.reshape(B, N, C, H, DV)
    b = jnp.cumsum(log_a.reshape(B, N, C, H, DK), axis=2)
    b_last = b[:, :, -1]
    q_e = q * jnp.exp(b)
    k_e = k * jnp.exp(-b)
    scores = jnp.einsum('bnthd,bnshd->bnhts', q_e, k_e)
    mask = jnp.tril(jnp.ones((C, C), dtype=bool), k=0 if include_diag else -1)
    scores = jnp.where(mask, scores, 0.0)
    o_intra = jnp.einsum('bnhts,bnshe->bnthe', scores, v)
    k_dec = k * jnp.exp(b_last[:, :, None] - b)
    U = jnp.einsum('bnshd,bnshe->bnhde', k_dec, v)
    decay = jnp.exp(b_last)

    def step(S, inp):
        dec, inc = inp
        return dec[..., None] * S + inc, S

    S0 = jnp.zeros((B, H, DK, DV), U.dtype)
    _, S_prev = lax.scan(step, S0, (jnp.moveaxis(decay, 1, 0), jnp.moveaxis(U, 1, 0)))
    S_prev = jnp.moveaxis(S_prev, 0, 1)
    o_inter = jnp.einsum('bnthd,bnhde->bnthe', q_e, S_prev)
    return (o_intra + o_inter).reshape(B, L, H, DV)

def _gla_mixer(q, k, v, g, gate_lr, gate_w2, gate_b, norm_g):
    B, L, _ = q.shape
    q = q.reshape(B, L, GLA_HEADS, GLA_HEAD_K) * (GLA_HEAD_K ** -0.5)
    k = k.reshape(B, L, GLA_HEADS, GLA_HEAD_K)
    v = v.reshape(B, L, GLA_HEADS, GLA_HEAD_V)
    lr = gate_lr.reshape(B, L, 2, GLA_GATE_RANK)
    gk = jnp.einsum('blzr,zrd->blzd', lr, gate_w2) + gate_b
    log_a = jnp.maximum(jax.nn.log_sigmoid(gk.astype(jnp.float32)) / GLA_GATE_NORMALIZER,
                        GLA_LOG_GATE_MIN).reshape(B, L, 2, GLA_HEADS, GLA_HEAD_K)
    o_fwd = _gla_direction(q, k, v, log_a[:, :, 0], True)
    fl = lambda a: jnp.flip(a, axis=1)
    o_bwd = fl(_gla_direction(fl(q), fl(k), fl(v), fl(log_a[:, :, 1]), False))
    o = _rms_norm(o_fwd + o_bwd, norm_g)
    return o.reshape(B, L, GLA_VALUE_DIM).astype(g.dtype) * jax.nn.silu(g)

def _pool_mixer(u, pool_w, pool_scale):
    B, L, _ = u.shape
    pos = jnp.arange(L)
    groups = []
    for gi, w in enumerate(POOL_WINDOWS):
        xg = u[..., gi * POOL_GROUP:(gi + 1) * POOL_GROUP].astype(jnp.float32)
        half = w // 2
        xp = jnp.pad(xg, ((0, 0), (half, half), (0, 0)))
        cs = jnp.pad(jnp.cumsum(xp, axis=1), ((0, 0), (1, 0), (0, 0)))
        wsum = cs[:, w:w + L] - cs[:, :L]
        count = (jnp.minimum(pos + half, L) - jnp.maximum(pos - half, 0)).astype(jnp.float32)
        groups.append(wsum / count[None, :, None] - xg)
    d = jnp.stack(groups, axis=2)
    y = jnp.einsum('blgc,gcd->blgd', d, pool_w.astype(jnp.float32)).reshape(B, L, D_POOL)
    return (y * pool_scale.astype(jnp.float32)).astype(u.dtype)

def second_inputs(seed: int = 0) -> dict:
    key = jax.random.key(seed)
    ks = iter(jax.random.split(key, 40))
    f32 = jnp.float32
    n = DEPTH_2
    FO = HYENA_FILTER_ORDER

    def nrm(shape, scale):
        return jax.random.normal(next(ks), shape, f32) * scale

    def gain(shape, noise=0.05):
        return 1.0 + nrm(shape, noise)

    return {
        "x": nrm((BATCH, SEQ, D_MODEL), 1.0),
        "norm_mix_pre": gain((n, D_MODEL)),
        "norm_mix_post": gain((n, D_MODEL)),
        "norm_ffn_pre": gain((n, D_MODEL)),
        "norm_ffn_post": gain((n, D_MODEL)),
        "w_in": nrm((n, D_MODEL, D_IN), D_MODEL ** -0.5),
        "hy_conv_w": nrm((n, 3, 3 * D_HYENA), 3 ** -0.5),
        "hy_conv_b": nrm((n, 3 * D_HYENA), 0.02),
        "hy_filt_w1": nrm((n, HYENA_EMB_DIM, FO), HYENA_EMB_DIM ** -0.5),
        "hy_filt_b1": nrm((n, FO), 0.1),
        "hy_filt_freq1": gain((n, FO), 0.01),
        "hy_filt_w2": nrm((n, FO, FO), FO ** -0.5),
        "hy_filt_b2": nrm((n, FO), 0.1),
        "hy_filt_freq2": gain((n, FO), 0.01),
        "hy_filt_w3": nrm((n, FO, 2 * D_HYENA), 0.005),
        "hy_bias": nrm((n, D_HYENA), 1.0),
        "gla_gate_w2": nrm((n, 2, GLA_GATE_RANK, GLA_KEY_DIM), GLA_GATE_RANK ** -0.5),
        "gla_gate_b": nrm((n, 2, GLA_KEY_DIM), 0.1),
        "gla_norm": gain((n, GLA_HEAD_V), 0.01),
        "pool_w": nrm((n, len(POOL_WINDOWS), POOL_GROUP, POOL_GROUP), POOL_GROUP ** -0.5),
        "pool_scale": gain((n, D_POOL), 0.1),
        "w_br_hyena": nrm((n, D_HYENA, D_MODEL), D_HYENA ** -0.5),
        "w_br_gla": nrm((n, GLA_VALUE_DIM, D_MODEL), GLA_VALUE_DIM ** -0.5),
        "w_br_pool": nrm((n, D_POOL, D_MODEL), D_POOL ** -0.5),
        "w_out": nrm((n, D_MODEL, D_MODEL), D_MODEL ** -0.5),
        "ffn_w_up": nrm((n, D_MODEL, 2 * D_FF), D_MODEL ** -0.5),
        "ffn_conv_w": nrm((n, 3, D_FF), 3 ** -0.5),
        "ffn_conv_b": nrm((n, D_FF), 0.02),
        "ffn_w_down": nrm((n, D_FF, D_MODEL), D_FF ** -0.5),
    }

def second_block(x, norm_mix_pre, norm_mix_post, norm_ffn_pre, norm_ffn_post, w_in,
              hy_conv_w, hy_conv_b, hy_filt_w1, hy_filt_b1, hy_filt_freq1, hy_filt_w2,
              hy_filt_b2, hy_filt_freq2, hy_filt_w3, hy_bias, gla_gate_w2, gla_gate_b,
              gla_norm, pool_w, pool_scale, w_br_hyena, w_br_gla, w_br_pool, w_out,
              ffn_w_up, ffn_conv_w, ffn_conv_b, ffn_w_down):
    B, L, _ = x.shape
    t_pos, z_pos = _hyena_positional_features(L)
    for i in range(DEPTH_2):
        h = _rms_norm(x, norm_mix_pre[i])
        proj = h @ w_in[i]
        u_hy, q, k, v, g_out, gate_lr, u_pool, gate_logits = _split(proj, IN_SPLITS)
        y_hy = _hyena_mixer(u_hy, hy_conv_w[i], hy_conv_b[i], t_pos, z_pos,
                            hy_filt_w1[i], hy_filt_b1[i], hy_filt_freq1[i], hy_filt_w2[i],
                            hy_filt_b2[i], hy_filt_freq2[i], hy_filt_w3[i], hy_bias[i])
        y_gla = _gla_mixer(q, k, v, g_out, gate_lr, gla_gate_w2[i], gla_gate_b[i], gla_norm[i])
        y_pool = _pool_mixer(u_pool, pool_w[i], pool_scale[i])
        gates = jax.nn.sigmoid(gate_logits).reshape(B, L, N_BRANCHES, D_MODEL)
        merged = (gates[:, :, 0] * (y_hy @ w_br_hyena[i])
                  + gates[:, :, 1] * (y_gla @ w_br_gla[i])
                  + gates[:, :, 2] * (y_pool @ w_br_pool[i]))
        x = x + _rms_norm(merged @ w_out[i], norm_mix_post[i])
        h = _rms_norm(x, norm_ffn_pre[i])
        a, b = _split(h @ ffn_w_up[i], (D_FF, D_FF))
        a = _dwconv3_centred(a, ffn_conv_w[i], ffn_conv_b[i])
        y = (jax.nn.gelu(a, approximate=False) * b) @ ffn_w_down[i]
        x = x + _rms_norm(y, norm_ffn_post[i])
    return x


_first_inputs = second_inputs


def second_inputs(seed=0):
    import zlib

    import numpy as np

    out = dict(_first_inputs(seed))
    spreads = {}
    factors = {'hy_filt_b1': 3.546,
     'hy_filt_freq1': 8.0,
     'hy_filt_b2': 3.724,
     'hy_filt_freq2': 8.0,
     'gla_norm': 8.0,
     'ffn_conv_b': 3.271}
    for name, (base, spread) in spreads.items():
        noise = np.random.default_rng([zlib.crc32(name.encode()), seed]).standard_normal(out[name].shape)
        drawn = base * np.exp(spread * noise) if base else spread * noise
        out[name] = jnp.asarray(drawn.astype(out[name].dtype))
    for name, factor in factors.items():
        out[name] = (out[name] * factor).astype(out[name].dtype)
    return out


_narrow_inputs = second_inputs


def second_inputs(seed=0):
    out = dict(_narrow_inputs(seed))
    wider = {'hy_conv_b': 7.08, 'hy_filt_freq1': 3.99, 'hy_filt_freq2': 12.0, 'gla_norm': 5.1}
    for name, times in wider.items():
        mean = out[name].mean()
        out[name] = (mean + times * (out[name] - mean)).astype(out[name].dtype)
    return out


def setup_inputs(seed=0):
    out = dict(first_inputs(seed))
    for name, value in second_inputs(seed + 1).items():
        if name != "x":
            out[name + "_2"] = value
    return out


def reference(
    x, mem, g_mix, w_in, conv_w, conv_b, gate_b, g_head, ln_v_g, ln_v_b, w_s, b_s, w_out,
    g_xattn, g_mem, w_q_x, w_kv_x, w_o_x, g_moe, w_rg, b_rg, w_re, b_re, w_gate, w_up, w_down,
    g_final, norm_mix_pre_2, norm_mix_post_2, norm_ffn_pre_2, norm_ffn_post_2, w_in_2,
    hy_conv_w_2, hy_conv_b_2, hy_filt_w1_2, hy_filt_b1_2, hy_filt_freq1_2, hy_filt_w2_2,
    hy_filt_b2_2, hy_filt_freq2_2, hy_filt_w3_2, hy_bias_2, gla_gate_w2_2, gla_gate_b_2,
    gla_norm_2, pool_w_2, pool_scale_2, w_br_hyena_2, w_br_gla_2, w_br_pool_2, w_out_2,
    ffn_w_up_2, ffn_conv_w_2, ffn_conv_b_2, ffn_w_down_2,
):
    x = first_block(
        x, mem, g_mix, w_in, conv_w, conv_b, gate_b, g_head, ln_v_g, ln_v_b, w_s, b_s, w_out,
        g_xattn, g_mem, w_q_x, w_kv_x, w_o_x, g_moe, w_rg, b_rg, w_re, b_re, w_gate, w_up,
        w_down, g_final,
    )
    return second_block(
        x, norm_mix_pre_2, norm_mix_post_2, norm_ffn_pre_2, norm_ffn_post_2, w_in_2,
        hy_conv_w_2, hy_conv_b_2, hy_filt_w1_2, hy_filt_b1_2, hy_filt_freq1_2, hy_filt_w2_2,
        hy_filt_b2_2, hy_filt_freq2_2, hy_filt_w3_2, hy_bias_2, gla_gate_w2_2, gla_gate_b_2,
        gla_norm_2, pool_w_2, pool_scale_2, w_br_hyena_2, w_br_gla_2, w_br_pool_2, w_out_2,
        ffn_w_up_2, ffn_conv_w_2, ffn_conv_b_2, ffn_w_down_2,
    )


_drawn_inputs = setup_inputs


def setup_inputs(seed=0):
    import zlib

    import numpy as np

    out = dict(_drawn_inputs(seed))
    spreads = {}
    factors = {'conv_b': 4.993, 'b_rg': 8.0, 'ln_v_b': 5.698}
    for name, (base, spread) in spreads.items():
        noise = np.random.default_rng([zlib.crc32(name.encode()), seed]).standard_normal(out[name].shape)
        drawn = base * np.exp(spread * noise) if base else spread * noise
        out[name] = jnp.asarray(drawn.astype(out[name].dtype))
    for name, factor in factors.items():
        out[name] = (out[name] * factor).astype(out[name].dtype)
    return out
```

```python
import concourse.bass as bass
from concourse import mybir
import numpy as np

F32 = mybir.dt.float32
F32R = mybir.dt.float32r
BF16 = mybir.dt.bfloat16
I32 = mybir.dt.int32
ALU = mybir.AluOpType
ACT = mybir.ActivationFunctionType
AX = mybir.AxisListType

T = 256
D = 1024
EPS = 1e-6
NEG = -1e30

FIRST_CHUNKS = 65
U_MOE = 33
GROUPS = 16
UNITS_PER_GROUP = 12
U_B2 = U_MOE + GROUPS * UNITS_PER_GROUP
LAYER = [("v", 4), ("g", 4), ("pool", 4), ("q", 4), ("k", 4), ("lr", 1), ("hy", 12), ("pb", 12), ("gb", 12),
         ("hb", 12), ("wo", 8), ("ffn", 66)]
L_AT, _n = {}, 0
for _name, _w in LAYER:
    L_AT[_name] = _n
    _n += _w
L_CHUNKS = _n
N_UNITS = U_B2 + (2 * L_CHUNKS + 1) // 2

PAR = {}
_n = 0
for _name, _w in [("g_mix", 8), ("g_mem", 8), ("g_xattn", 8), ("g_moe", 8), ("conv_w", 40),
                  ("conv_b", 8), ("g_head", 4), ("gate_b", 1), ("br", 1),
                  ("mix_pre0", 8), ("mix_pre1", 8), ("ffn_pre0", 8), ("ffn_pre1", 8),
                  ("hcw0", 36), ("hcw1", 36), ("hcb0", 12), ("hcb1", 12),
                  ("hf0", 4), ("hf1", 4), ("gla_norm0", 1), ("gla_norm1", 1),
                  ("pool_s0", 4), ("pool_s1", 4), ("fcw0", 66), ("fcw1", 66),
                  ("fcb0", 22), ("fcb1", 22)]:
    PAR[_name] = _n
    _n += _w
N_PAR = _n

CON = {}
_n = 0
for _name, _w in [("ident", 128), ("ones", 128), ("le", 128), ("ge", 128), ("lt", 128),
                  ("mf", 128), ("mb", 128), ("onehot", 512), ("iota", 64), ("cf", 130), ("cb", 130),
                  ("m1", 128), ("m2", 64), ("edge", 64), ("lrone", 1)]:
    CON[_name] = _n
    _n += _w
N_CON = _n


def constants():
    s = np.arange(128)[:, None]
    t = np.arange(128)[None, :]
    c = np.zeros((128, N_CON), np.float32)

    def put(name, a):
        c[:a.shape[0], CON[name]:CON[name] + a.shape[1]] = a

    put("ident", (s == t).astype(np.float32))
    put("ones", np.ones((128, 128), np.float32))
    put("le", (s <= t).astype(np.float32))
    put("ge", (s >= t).astype(np.float32))
    put("lt", (s < t).astype(np.float32))
    put("mf", np.where(s <= t, 0.0, NEG).astype(np.float32))
    put("mb", np.where(s >= t, 0.0, NEG).astype(np.float32))
    oh = np.zeros((4, 4, 128), np.float32)
    for h in range(4):
        oh[h, h, :] = 1.0
    put("onehot", oh.reshape(4, 512))
    put("iota", np.broadcast_to(np.arange(64, dtype=np.float32)[None], (128, 64)))
    le = (s <= t).astype(np.float32)
    cf = np.concatenate([le - le[:, 63:64], le[:, 63:64], 1.0 - le[:, 63:64]], axis=1)
    ge = (s >= t).astype(np.float32)
    cb = np.concatenate([ge - ge[:, 64:65], ge[:, 64:65], 1.0 - ge[:, 64:65]], axis=1)
    put("cf", cf.astype(np.float32))
    put("cb", cb.astype(np.float32))
    m1 = np.ones((128, 128), np.float32)
    for a in (0, 64):
        m1[a:a + 64, a:a + 64] = le[:64, :64]
    put("m1", m1)
    put("m2", np.concatenate([(s > t).astype(np.float32)[:64, :64]] * 2, axis=0))
    edge = np.ones((4, 16), np.float32)
    for g, w in enumerate((2, 4, 8, 16)):
        half = w // 2
        for i in range(8):
            edge[g, i] = w / min(w, i + half)
            edge[g, 8 + i] = w / min(w, 8 - i + half)
    put("lrone", ((s == 16) | (s == 48)).astype(np.float32))
    put("edge", np.broadcast_to(edge.reshape(1, 64), (128, 64)))
    return c


def dft_tables():
    s = np.arange(256, dtype=np.float64)[:, None]
    w = 2.0 * np.pi * (np.arange(256, dtype=np.float64)[None, :] + 0.5) / 512.0
    a = s * w
    out = np.zeros((128, 4, 2, 256), np.float32)
    out[:, 0] = np.cos(a).reshape(2, 128, 256).transpose(1, 0, 2)
    out[:, 1] = np.sin(a).reshape(2, 128, 256).transpose(1, 0, 2)
    out[:, 2] = (np.cos(a).T / 256.0).reshape(2, 128, 256).transpose(1, 0, 2)
    out[:, 3] = (np.sin(a).T / 256.0).reshape(2, 128, 256).transpose(1, 0, 2)
    return out.reshape(128, 2048)


def filter_tables():
    L = T
    t = np.linspace(0.0, 1.0, L, dtype=np.float32)[:, None]
    w = (2.0 * np.pi * np.arange(L, dtype=np.float32)[:, None] / L).astype(np.float32)
    f = np.linspace(1e-4, 15, 16, dtype=np.float32)[None, :]
    ang = (f * w).astype(np.float32)
    z = np.concatenate([t, np.cos(ang), -np.sin(ang)], axis=-1).astype(np.float32)
    mx, mn = np.log(1e-2) / 0.3, np.log(1e-2) / 1.5
    deltas = np.linspace(mn, mx, 512, dtype=np.float32)
    decay = np.exp(-t * np.abs(deltas)).astype(np.float32)
    return np.ascontiguousarray(z.T), np.ascontiguousarray(decay.reshape(2, 128, 512).transpose(1, 0, 2).reshape(128, 1024))


class Eng:

    def __init__(self, sem):
        self.sem = sem
        self.n = 0
        self.q = []
        self.seen = {}

    def wait(self, *toks):
        for t in toks:
            if t is None:
                continue
            if isinstance(t, list):
                self.wait(*t)
                continue
            if self.seen.get(t[0].name, 0) < t[1]:
                self.seen[t[0].name] = t[1]
                self.q.append(lambda e, t=t: e.wait_ge(t[0], t[1]))

    def __call__(self, fn, *toks, sig=True):
        self.wait(*toks)
        if not sig:
            self.q.append(fn)
            return None
        self.n += 1
        sem = self.sem
        self.q.append(lambda e: fn(e).then_inc(sem, 1))
        return (sem, self.n)

    def last(self):
        return (self.sem, self.n)


def program(nc, A):
    ctx_sems = []

    def sem(name):
        s = nc.alloc_semaphore(name)
        ctx_sems.append(s)
        return s

    PE, AC, DV, PO, SP = (Eng(sem(f"s_{n}")) for n in ("pe", "act", "dve", "pool", "sp"))

    BASE = 16896
    R = 7

    def at(name, shape, off, dt=F32):
        return nc.alloc_sbuf_tensor_at(name, shape, dt, offset=off)

    class Region:

        def __init__(self, start, end):
            self.o, self.end = start, end

        def __call__(self, name, shape, dt=F32, keep=True):
            n = 4
            for w in shape[1:]:
                n *= w
            t = at(name, shape, self.o, dt)
            if keep:
                self.o += (n + 31) // 32 * 32
            assert self.o <= self.end, (name, self.o, self.end)
            return t

    NH = 6
    fix = Region(BASE, 229344)
    X = fix("X", [128, 2, 1024])
    HA_AT = fix.o
    HA = fix("HA", [128, 8, 256], F32R)
    LA_AT = fix.o
    LA = fix("LA", [128, 8, 256], F32R)
    HB_AT = fix.o
    HB = fix("HB", [128, 8, 256], F32R)
    LB_AT = fix.o
    LB = fix("LB", [128, 8, 256], F32R)
    WH_AT = fix.o
    WH = fix("WH", [128, NH, 1024], F32R)
    PARS = fix("PARS", [128, N_PAR])
    CONS = fix("CONS", [128, N_CON])
    SM = fix("SM", [128, 240])
    CNT = fix("CNT", [128, 8], I32)
    JNK = fix("JNK", [128, 2, 512], BF16)
    DIAG = fix("DIAG", [128, 2, 128])
    RING = fix("RING", [128, R, 2048], keep=False)
    RINGL = fix("RINGL", [128, R, 2048], F32R)
    Z, ZEND = fix.o, fix.end

    P = [nc.alloc_psum_tensor(f"P{i}", [128, 512], F32) for i in range(8)]
    pfree = [None] * 8

    def con(name, a=0, b=None, p=128):
        c = CON[name]
        w = {"iota": 64, "onehot": 512, "cf": 130, "cb": 130, "m2": 64, "edge": 64, "lrone": 1}.get(name, 128)
        return CONS[0:p, c + a:c + (w if b is None else b)]

    def par(name, i=0, p=128, p0=0):
        return PARS[p0:p0 + p, PAR[name] + i:PAR[name] + i + 1]

    IDENT = con("ident")

    def tt(E, out, a, b, op, *d):
        return E(lambda e: e.tensor_tensor(out, a, b, op), *d)

    def ts(E, out, a, s1, s2, op0, op1, *d):
        if op1 is None:
            return E(lambda e: e.tensor_scalar(out, a, s1, None, op0), *d)
        return E(lambda e: e.tensor_scalar(out, a, s1, s2, op0, op1), *d)

    def stt(E, out, a, s, b, op0, op1, *d):
        return E(lambda e: e.scalar_tensor_tensor(out, a, s, b, op0, op1), *d)

    def cp(E, out, a, *d):
        return E(lambda e: e.tensor_copy(out, a), *d)

    def act(out, a, func, *d, bias=0.0, scale=1.0, accum=None):
        if accum is None:
            return AC(lambda e: e.activation(out, a, func, bias=bias, scale=scale), *d)
        return AC(lambda e: e.activation(out, a, func, bias=bias, scale=scale, accum_out=accum), *d)

    def table(name):
        AC(lambda e: e.preload_act_table_set(name), sig=False)

    def mm(out, lhsT, rhs, start, stop, *d, sig=False):
        return PE(lambda e: e.matmul(out, lhsT, rhs, start=start, stop=stop), *d, sig=sig)

    def tr(out, a, *d, sig=False, n=128):
        return PE(lambda e: e.transpose(out, a, IDENT if n == 128 else CONS[0:n, 0:n]), *d, sig=sig)

    def memset(E, ap, v, *d):
        return E(lambda e: e.memset(ap, v), *d)

    def f(ap):
        return ap.bitcast(F32)

    pool_sems = [[sem(f"s_ld{i}"), 0, None] for i in range(24)]
    pool_at = [0]

    def load(out, src, *d):
        r = pool_sems[pool_at[0] % len(pool_sems)]
        pool_at[0] += 1
        SP.wait(*d)
        if r[1]:
            SP.wait((r[0], r[1]))
        r[1] += 16
        s = r[0]
        SP.q.append(lambda e: e.dma_start(out, src).then_inc(s, 16))
        return (r[0], r[1])

    class Slot:

        def __init__(self, raw, lo, name, until):
            self.raw, self.lo, self.sem, self.n, self.until, self.freed = raw, lo, sem(name), 0, until, None

    slots = [Slot(RING[:, i, :], RINGL[:, i, :], f"s_w{i}", N_UNITS) for i in range(R)]
    unit_n = [0]
    units = {}
    vacant = [(s_, None) for s_ in slots]

    def load_units(n=None):
        while vacant and unit_n[0] < N_UNITS and (n is None or n > 0):
            u = unit_n[0]
            fit = [i for i, v in enumerate(vacant) if v[0].lo is not None or u >= U_MOE]
            if not fit:
                break
            s_, d = vacant.pop(fit[0])
            if u >= s_.until:
                s_.freed = d
                continue
            unit_n[0] += 1
            if n is not None:
                n -= 1
            SP.wait(d)
            s_.n += 16
            SP.q.append(lambda e, s_=s_, u=u: e.dma_start(s_.raw, A["ws"][u]).then_inc(s_.sem, 16))
            units[u] = [s_, (s_.sem, s_.n), 0, []]

    def free_unit(u, *toks):
        vacant.append((units.pop(u)[0], list(toks)))
        load_units()

    LAHEAD = 2
    st = {"split": 0, "chunk": 0, "end": FIRST_CHUNKS, "bg": 0}
    his = [(WH[:, i, :], None) for i in range(NH)]
    halves = {}

    def split_chunks(end):
        while st["split"] < min(end, st["end"]) and his:
            c = st["split"]
            st["split"] += 1
            hi, free = his.pop(0)
            s_, tok = units[c // 2][:2]
            w = slice((c % 2) * 1024, (c % 2) * 1024 + 1024)
            t1 = act(hi, s_.raw[:, w], ACT.Copy, tok, free)
            t2 = tt(DV, s_.lo[:, w], s_.raw[:, w], f(hi), ALU.subtract, t1)
            halves[c] = (hi, s_.lo[:, w], t1, t2)

    def take():
        c = st["chunk"]
        st["chunk"] += 1
        split_chunks(c + 1 + LAHEAD)
        return c, halves[c]

    def give(c, done):
        his.append((halves.pop(c)[0], done))
        u = units[c // 2]
        u[2] += 1
        u[3].append(done)
        if u[2] == 2 or c == st["end"] - 1:
            free_unit(c // 2, *u[3])

    behind = []

    def bg(n=1):
        for _ in range(n):
            while behind:
                try:
                    next(behind[0])
                    break
                except StopIteration:
                    behind.pop(0)

    def bg_all(*gens):
        while behind and (not gens or any(g in behind for g in gens)):
            bg()

    sbank = [0]
    held = set()

    def stream_bank(hold=False):
        while sbank[0] % 4 in held:
            sbank[0] += 1
        b = sbank[0] % 4
        sbank[0] += 1
        if hold:
            held.add(b)
        return b

    def t_out(hi_a, lo_a, a_tok, evac, kt=8, parts=1):
        c, (hi, lo, t1, t2) = take()
        b = stream_bank()
        for q in range(parts):
            out = P[b][:, q * 256:(q + 1) * 256]
            for k in range(kt):
                w = slice((q * kt + k) * 128, (q * kt + k + 1) * 128)
                (h0, l0), (h1, l1) = a_tok(k, 0), a_tok(k, 1)
                mm(out, hi[:, w], hi_a[:, k, :], k == 0, False, t1, h0, h1, pfree[b])
                mm(out, lo[:, w], hi_a[:, k, :], False, False, t2)
                done = mm(out, hi[:, w], lo_a[:, k, :], False, k == kt - 1, l0, l1,
                          sig=(k == kt - 1 and q == parts - 1))
        give(c, done)
        pfree[b] = evac(P[b], done)
        bg(st["bg"])

    def n_out(hi_a, lo_a, a_tok, evac, pairs=(0, 1, 2, 3)):
        banks = []

        def step(j):
            c, (hi, lo, t1, t2) = take()
            if j == 0:
                banks.extend([stream_bank(True), stream_bank(True)])
            ends = []
            for i in range(2):
                k = 2 * pairs[j] + i
                w = slice(i * 512, (i + 1) * 512)
                for t in range(2):
                    out = P[banks[t]][:, :]
                    ta = slice(t * 128, (t + 1) * 128)
                    first, last = j == 0 and i == 0, j == 3 and i == 1
                    th, tl = a_tok(k, t)
                    mm(out, hi_a[:, k, ta], hi[:, w], first, False, t1, th, pfree[banks[t]] if first else None)
                    mm(out, hi_a[:, k, ta], lo[:, w], False, False, t2)
                    done = mm(out, lo_a[:, k, ta], hi[:, w], False, last, tl, sig=(last or (i == 1 and t == 1)))
                    if last:
                        ends.append((t, done))
            give(c, done)
            for t, d in ends:
                held.discard(banks[t])
                pfree[banks[t]] = evac(t, P[banks[t]], d)
            bg(st["bg"])
        return [lambda j=j: step(j) for j in range(4)]

    def n_tiles(hi_a, lo_a, a_tok, evac, mid, pairs=(0, 1, 2, 3)):
        got = [take() for _ in range(4)]
        for t in range(2):
            ta = slice(t * 128, (t + 1) * 128)
            b = stream_bank()
            for j in range(4):
                if j == 3:
                    mid(t)
                c, (hi, lo, t1, t2) = got[j]
                for i in range(2):
                    k = 2 * pairs[j] + i
                    w = slice(i * 512, (i + 1) * 512)
                    th, tl = a_tok(k, t)
                    first, last = j == 0 and i == 0, j == 3 and i == 1
                    mm(P[b][:, :], hi_a[:, k, ta], hi[:, w], first, False, t1, th, pfree[b])
                    mm(P[b][:, :], hi_a[:, k, ta], lo[:, w], False, False, t2)
                    done = mm(P[b][:, :], lo_a[:, k, ta], hi[:, w], False, last, tl, sig=(last or (t == 1 and i == 1)))
                if t == 1:
                    give(c, done)
                    if j == 2:
                        split_chunks(st["chunk"] + LAHEAD + 1)
            pfree[b] = evac(t, P[b], done)

    todo = []

    def fill(n):
        for _ in range(n):
            if todo:
                todo.pop(0)()

    def now():
        return [E.last() for E in (PE, AC, DV, PO) if E.n]

    def rstd_of(ss, n, scale, eps, *d):
        m = SM[:, 64:64 + n]
        y = SM[:, 96:96 + n]
        a = SM[:, 128:128 + n]
        t0 = ts(DV, m, ss, scale, eps, ALU.mult, ALU.add, *d)
        t1 = act(y, m, ACT.Ln, t0)
        t1 = act(y, y, ACT.Exp, t1, scale=-0.5)
        t2 = tt(DV, a, y, y, ALU.mult, t1)
        t2 = stt(DV, a, a, -0.5, m, ALU.mult, ALU.mult, t2)
        return stt(DV, ss, a, 1.5, y, ALU.add, ALU.mult, t2)

    jnk = [0, [None, None]]

    def square(E, x, acc, scale, *d):
        i = jnk[0] % 2
        jnk[0] += 1
        if E is AC:
            v = act(JNK[:, i, :], x, ACT.Square, jnk[1][i], *d, scale=scale ** 0.5, accum=acc)
        else:
            v = DV(lambda e: e.tensor_tensor_reduce(JNK[:, i, :], x, x, scale, 0.0, ALU.mult, ALU.add, acc), jnk[1][i], *d)
        jnk[1][i] = v
        return v

    def ms(t, n, x, *d, E=None):
        c = 200 + 2 * t + n
        return square(E or AC, x, SM[:, c:c + 1], 1.0 / D, *d)

    def rstd_tile(t, *d, base=200):
        o_ = base + 8 + 4 * t
        m, y, a, r = (SM[:, o_ + i:o_ + i + 1] for i in range(4))
        v = ts(DV, m, SM[:, base + 2 * t:base + 1 + 2 * t], SM[:, base + 1 + 2 * t:base + 2 + 2 * t], EPS, ALU.add,
               ALU.add, *d)
        v = act(y, m, ACT.Ln, v)
        v = act(y, y, ACT.Exp, v, scale=-0.5)
        v = stt(DV, a, y, m, y, ALU.mult, ALU.mult, v)
        return r, stt(DV, r, a, -3.0, y, ALU.add, ALU.mult, v)

    class Norm:

        def __init__(self, x, g, hi, lo):
            self.x, self.g, self.hi, self.lo, self.toks = x, g, hi, lo, {}

        def tok(self, k, t):
            return self.toks[k, t]

        def a(self, t, *d):
            self.r, v = rstd_tile(t, *d)
            self.d = ts(DV, DIAG[:, t, :], IDENT, self.r, -0.5, ALU.mult, ALU.mult, v, diag_used[t])
            self.rt = v
            return v

        def b(self, t):
            self.done = []
            for i in range(2):
                bk = 4 + 2 * t + i
                for q in range(4):
                    k = 4 * i + q
                    dn = mm(P[bk][:, q * 128:(q + 1) * 128], self.x[:, t, k * 128:(k + 1) * 128], DIAG[:, t, :],
                            True, True, self.d, pfree[bk], sig=(q == 3))
                self.done.append(dn)
            diag_used[t] = dn

        def c(self, t, *w):
            for _ in self.c_steps(t, *w):
                pass

        def c_steps(self, t, *w):
            ta = slice(t * 128, (t + 1) * 128)
            for i in range(2):
                bk = 4 + 2 * t + i
                hs = []
                for q in range(4):
                    k = 4 * i + q
                    hs.append(act(self.hi[:, k, ta], P[bk][:, q * 128:(q + 1) * 128], ACT.Copy, self.done[i], *w,
                                  scale=par(self.g, k)))
                    if q == 1:
                        yield
                for q in range(4):
                    k = 4 * i + q
                    v = stt(DV, self.lo[:, k, ta], P[bk][:, q * 128:(q + 1) * 128], par(self.g, k), f(self.hi[:, k, ta]),
                            ALU.mult, ALU.subtract, hs[3], *w)
                    self.toks[k, t] = (hs[q], v)
                    if q == 1:
                        yield
                pfree[bk] = v
                yield

    diag_used = [None, None]

    def finish():
        for E in (PE, AC, DV, PO):
            if E.n:
                SP.wait(E.last())
        for r in pool_sems:
            if r[1]:
                SP.wait((r[0], r[1]))
        for u in units.values():
            SP.wait(u[1])
        with nc.Block() as block:
            @block.sync
            def _(e):
                for g in SP.q:
                    g(e)

            @block.scalar
            def _(e):
                for g in AC.q:
                    g(e)

            @block.vector
            def _(e):
                for g in DV.q:
                    g(e)

            @block.gpsimd
            def _(e):
                for g in PO.q:
                    g(e)

            @block.tensor
            def _(e):
                for g in PE.q:
                    g(e)

    z = Region(Z, ZEND)
    KT = z("KT", [128, 8, 256])
    MEM = z("MEM", [128, 2, 1024], keep=False)
    VN = z("VN", [128, 2, 1024])
    IG = z("IG", [4, 2, 256])
    FG = z("FG", [4, 2, 256])
    RT1 = z("RT1", [4, 2, 256])
    NC = z("NC", [4, 2, 256])
    SI = z("SI", [4, 2, 128])
    KWR = z("KWR", [4, 2, 128])
    ONEROW = z("ONEROW", [4, 128])
    za = Region(z.o, ZEND)
    QP = z("QP", [128, 2, 260])
    QK = z("QK", [128, 8, 256])
    V1 = z("V1", [128, 2, 4, 130])
    SO = z("SO", [128, 2, 512])
    GV = z("GV", [128, 2, 512], keep=False)
    HS = z("HS", [128, 2, 512])
    GU = z("GU", [128, 4, 256])
    LNG = z("LNG", [128, 512])
    LNB = z("LNB", [128, 512])
    BS = z("BS", [1, 4, 128])
    WST = z("WST", [128, 4, 128])
    COLS = z("COLS", [128, 12, 4])
    MN = z("MN", [128, 2, 512])
    KW = z("KW", [128, 2, 2, 128])
    CA = z("CA", [128, 2, 2, 130])
    T1 = z("T1", [128, 2, 130])
    DN = z("DN", [128, 4])
    QX = za("QX", [128, 8, 256])
    PX = za("PX", [128, 2, 2, 256])
    PTX = za("PTX", [128, 2, 2, 256])
    K1_AT = ZEND - 8192
    zslots = [Slot(at(f"ZR{i}", [128, 2048], K1_AT - 8192 * i)[:, :], None, f"s_z{i}", U_B2 if i else U_MOE + 6 * UNITS_PER_GROUP)
              for i in range(2)]

    i0 = CON["ident"]
    x_tok = [load(X[:, 0, :], A["x"][0])]
    i_tok = load(CONS[:, i0:i0 + 128], A["con"][:, i0:i0 + 128])
    p_tok = load(PARS[:, :], A["par"])
    load_units(1)
    x_tok.append(load(X[:, 1, :], A["x"][1]))
    load_units(2)
    mem_tok = [load(MEM[:, t, :], A["mem"][t]) for t in range(2)]
    load_units(1)
    assert i0 == 0
    c_tok = load(CONS[:, 128:], A["con"][:, 128:])
    load_units(R - 4)
    ln_tok = [load(LNG[:, :], A["ln_g"].partition_broadcast(128)), load(LNB[:, :], A["ln_b"].partition_broadcast(128))]
    bs_tok = load(BS[:, :, :], A["b_s"])
    wst_tok = load(WST[:, :, :], A["w_sT"])

    table("natural_log_exp_and_others")
    sm0 = memset(DV, SM[:, :], 0.0)
    qpz = memset(PO, QP[:, :, :], 0.0)
    v1one = memset(PO, V1[:, :, :, 128:130], 1.0)
    onerow = memset(PO, ONEROW[:, :], 1.0)
    AC.wait(sm0)
    DV.wait(sm0)

    nA = Norm(X, "g_mix", HA, LA)
    tA = nA.tok
    s0 = [ms(0, 0, X[:, 0, 0:512], x_tok[0]), ms(0, 1, X[:, 0, 512:1024], x_tok[0], E=DV)]
    DV.wait(i_tok)
    AC.wait(p_tok)
    nA.a(0, s0)
    nA.b(0)
    DV.wait(p_tok)
    nA.c(0)
    split_chunks(LAHEAD)
    s1 = [ms(1, 0, X[:, 1, 0:512], x_tok[1]), ms(1, 1, X[:, 1, 512:1024], x_tok[1], E=DV)]
    nA.a(1, s1)
    v_tok = [None, None]

    def v_evac(t, bank, done):
        v_tok[t] = act(V1[:, t, :, 0:128], bank[:, :].rearrange("p (h d) -> p h d", h=4), ACT.Copy, done)
        return v_tok[t]

    def v_mid(t):
        if t == 0:
            nA.b(1)
            nA.c(1)

    n_tiles(HA, LA, tA, v_evac, v_mid)

    g_in = [None] * 4

    def gate_evac(bank, done):
        for kind in range(4):
            dst = (IG if kind < 2 else FG)[:, kind % 2, :]
            g_in[kind] = act(dst, bank[32 * kind:32 * kind + 4, 0:256], ACT.Identity, done,
                             bias=par("gate_b", p=4, p0=32 * kind))
        return g_in[3]

    t_out(HA, LA, tA, gate_evac)
    for E in (PE, AC, DV, PO):
        E.wait(c_tok)

    def order(d, t):
        return slice(t * 128, t * 128 + 128) if d == 0 else slice(t * 128 + 127, (t * 128 - 1) if t else None, -1)

    def at_end(ap, d, t):
        i = t * 128 + (127 if d == 0 else 0)
        return ap[:, d, i:i + 1]

    gt = {}

    def scan(out, a, b, init, op0, op1, *d):
        return DV(lambda e: e.tensor_tensor_scan(out, a, b, init, op0, op1), *d)

    def rows():
        a = act(RT1[:, :, :], FG[:, :, :], ACT.Abs, g_in[3])
        a = act(RT1[:, :, :], RT1[:, :, :], ACT.Exp, a, scale=-1.0)
        a = act(RT1[:, :, :], RT1[:, :, :], ACT.Ln, a, bias=1.0)
        yield
        lf = stt(DV, FG[:, :, :], FG[:, :, :], 0.0, RT1[:, :, :], ALU.min, ALU.subtract, a)
        yield
        bt = []
        for d in range(2):
            for t in range(2):
                o_ = order(d, t)
                bt.append(scan(RT1[:, d, o_], ONEROW[:, :], FG[:, d, o_], 0.0, ALU.mult, ALU.add, lf, onerow))
            yield
        gt["u"] = u_t = tt(DV, IG[:, :, :], IG[:, :, :], RT1[:, :, :], ALU.subtract, bt)
        yield
        mA = []
        for d in range(2):
            o_ = order(d, d)
            mA.append(scan(FG[:, d, o_], IG[:, d, o_], IG[:, d, o_], -3e38, ALU.max, ALU.max, u_t))
        yield
        mp_t = [tt(DV, SM[0:4, 16 + d:17 + d], at_end(FG, d, d), at_end(RT1, d, d), ALU.add, mA[d]) for d in range(2)]
        yield
        for d in range(2):
            o_ = order(d, 1 - d)
            mB = scan(FG[:, d, o_], IG[:, d, o_], IG[:, d, o_], SM[0:4, 16 + d:17 + d], ALU.max, ALU.max, mp_t[d])
        yield
        gt["nc"] = nc_t = ts(DV, NC[:, :, :], FG[:, :, :], -1.0, None, ALU.mult, None, mB)
        bc_t = tt(DV, RT1[:, :, :], RT1[:, :, :], FG[:, :, :], ALU.add, mB)
        yield
        for d in range(2):
            ta, tb = slice(d * 128, d * 128 + 128), slice((1 - d) * 128, (1 - d) * 128 + 128)
            kw_t = act(KWR[:, d, :], IG[:, d, ta], ACT.Exp, nc_t, bias=at_end(NC, d, d))
            si_t = act(SI[:, d, :], NC[:, d, tb], ACT.Exp, nc_t, bias=SM[0:4, 16 + d:17 + d])
        em_t = act(RT1[:, :, :], RT1[:, :, :], ACT.Exp, bc_t, scale=-1.0)
        yield
        src = [(IG, 0, 0), (IG, 0, 1), (IG, 1, 0), (IG, 1, 1), (RT1, 0, 0), (RT1, 0, 1), (RT1, 1, 1), (RT1, 1, 0)]
        for i, (a, d, t) in enumerate(src):
            done = tr(P[7][:, 4 * i:4 * i + 4], a[:, d, t * 128:(t + 1) * 128], u_t, em_t, pfree[7], n=4)
        for i, a in enumerate((SI, SI, KWR, KWR)):
            done = tr(P[7][:, 32 + 4 * i:36 + 4 * i], a[:, i % 2, :], sig=(i == 3), n=4)
        gt["cols"] = pfree[7] = cp(DV, COLS[:, :, :], P[7][:, 0:48].rearrange("p (k h) -> p k h", h=4), done)

    nB = Norm(MEM, "g_mem", HB, LB)
    tB = nB.tok

    def mem_norm():
        s = [[ms(t, n, MEM[:, t, n * 512:(n + 1) * 512], mem_tok[t]) for n in range(2)] for t in range(2)]
        yield
        for t in range(2):
            nB.a(t, s[t])
            yield
            yield
            nB.b(t)
            yield
            yield from nB.c_steps(t)

    qk_tok = [None] * 8
    qk_act = [None] * 8
    conv_tok = [None, None]

    def qk_evac(i):
        def ev(bank, done):
            r = i % 2
            t0 = act(QP[:, r, 2:258], bank[:, 0:256], ACT.Copy, done, qpz, conv_tok[r])
            acc = QK[:, i, :]
            v = t1 = act(acc, bank[:, 0:256], ACT.Identity, done, bias=par("conv_b", i), scale=par("conv_w", 16 + i))
            for j in (0, 1, 3, 4):
                v = stt(DV, acc, QP[:, r, j:j + 256], par("conv_w", 8 * j + i), acc, ALU.mult, ALU.add, v, t0)
            conv_tok[r] = qk_tok[i] = v
            return t1
        return ev

    so_t = [None, None]

    def o_evac(t, bank, done):
        so_t[t] = act(SO[:, t, :], bank[:, :], ACT.Copy, done)
        return so_t[t]

    kx_t = [None] * 8

    def kx_evac(i):
        def ev(bank, done):
            kx_t[i] = act(KT[:, i, :], bank[:, 0:256], ACT.Copy, done)
            return kx_t[i]
        return ev

    behind.extend([mem_norm(), rows()])
    st["bg"] = 2
    os_ = n_out(HA, LA, tA, o_evac)
    for i in range(4):
        t_out(HA, LA, tA, qk_evac(i))
        os_[i]()
    mem_left = behind[:1]
    bg_all(*mem_left)
    for i in range(4):
        t_out(HA, LA, tA, qk_evac(4 + i))
        t_out(HB, LB, tB, kx_evac(i))
    bg_all()

    table("silu_and_others")
    for i in (0, 4, 2, 6):
        qk_act[i] = qk_act[i + 1] = act(QK[:, i:i + 2, :], QK[:, i:i + 2, :], ACT.Silu, qk_tok[i], qk_tok[i + 1])
    table("sigmoid_and_others")
    so = act(SO[:, :, :], SO[:, :, :], ACT.Sigmoid, so_t)
    table("gelu_apprx_tanh_and_others")
    gelu_t = [None, None]

    def gv_evac(t, bank, done):
        gelu_t[t] = act(GV[:, t, :], bank[:, :], ACT.Gelu_apprx_tanh, done)
        return gelu_t[t]

    gu_t = [None] * 4

    def gu_evac(i):
        def ev(bank, done):
            gu_t[i] = act(GU[:, i, :], bank[:, 0:256], ACT.Gelu_apprx_tanh, done)
            return gu_t[i]
        return ev

    def layer_norm():
        ln_done = []
        for t in range(2):
            b0 = DV(lambda e, t=t: e.bn_stats(SM[:, 32 + 6 * t:38 + 6 * t], GV[:, t, :]), gelu_t[t])
            ln_done.append(DV(lambda e, t=t: e.bn_aggr(SM[:, 24 + 2 * t:26 + 2 * t], SM[:, 32 + 6 * t:38 + 6 * t]), b0))
        yield
        r = cp(DV, SM[:, 2:4], SM[:, 25:29:2], ln_done)
        while gu_t[3] is None:
            yield
        table("natural_log_exp_and_others")
        r = rstd_of(SM[:, 2:4], 2, 1.0, 1e-5, r)
        yield
        for t in range(2):
            a = ts(DV, GV[:, t, :], GV[:, t, :], SM[:, 24 + 2 * t:25 + 2 * t], SM[:, 2 + t:3 + t],
                   ALU.subtract, ALU.mult, r)
            a = tt(PO, GV[:, t, :], GV[:, t, :], LNG[:, :], ALU.mult, a, ln_tok[0])
            gv_t[t] = tt(PO, GV[:, t, :], GV[:, t, :], LNB[:, :], ALU.add, a, ln_tok[1])
            yield

    gv_t = [None, None]
    for s in n_out(HA, LA, tA, gv_evac):
        s()
    behind.append(layer_norm())
    for i in range(4):
        t_out(HA, LA, tA, gu_evac(i))
    hA_free = PE.last()
    bg_all()
    st["bg"] = 0

    SC = 128 ** -0.5
    hd = [{} for _ in range(4)]
    cols_t, nc_t = gt["cols"], gt["nc"]

    def col(kind, h):
        return COLS[:, kind, h:h + 1]

    def m1_products(h):
        s = hd[h]
        for t in range(2):
            ta = slice(t * 128, (t + 1) * 128)
            mm(P[4][:, ta], QK[:, 4 + h, ta], QK[:, h, ta], True, True, qk_act[h], qk_act[4 + h], pfree[4])
        for d in range(2):
            s["s"] = tr(P[4][:, 256 + d * 128:384 + d * 128], QK[:, 4 + h, d * 128:(d + 1) * 128], sig=(d == 1))
        for d in range(2):
            s["bc"] = mm(P[5][:, d * 256:(d + 1) * 256], con("onehot", h * 128, h * 128 + 128, p=4), NC[:, d, :],
                         True, True, nc_t, pfree[5], sig=(d == 1))

    def m2_weights(h):
        s, r = hd[h], h % 2
        a = []
        for d in range(2):
            for t in range(2):
                c = d * 256 + t * 128
                a.append(stt(DV, MN[:, r, c:c + 128], P[5][:, c:c + 128], col(2 * d + t, h),
                             con("mf" if d == 0 else "mb"), ALU.add, ALU.min, s["bc"], cols_t,
                             hd[h - 2]["num"] if h >= 2 else None))
        pfree[5] = a[3]
        x_ = act(MN[:, r, :], MN[:, r, :], ACT.Exp, a[3])
        for d in range(2):
            k_ = ts(DV, KW[:, r, d, :], P[4][:, 256 + d * 128:384 + d * 128], col(10 + d, h), None, ALU.mult, None,
                    s["s"], hd[h - 2]["caug"] if h >= 2 else None)
        s["kw"] = k_
        for d in range(2):
            c = slice(d * 256, d * 256 + 256)
            s["p"] = stt(DV, MN[:, r, c], P[4][:, 0:256], SC, MN[:, r, c], ALU.mult, ALU.mult, x_)
        pfree[4] = s["p"]

    def v_aug(t, h):
        return V1[:, t, h, 0:129]

    def m3_numerators(h):
        s, r = hd[h], h % 2
        for d in range(2):
            s["caug"] = mm(P[5][:, d * 130:d * 130 + 129], KW[:, r, d, :], v_aug(d, h), True, True,
                           s["kw"], pfree[5], v_tok[d], v1one, sig=(d == 1))
        for i, (d, t) in enumerate(((0, 0), (0, 1), (1, 1))):
            s["x"] = mm(P[6][:, i * 130:i * 130 + 129], MN[:, r, d * 256 + t * 128:d * 256 + t * 128 + 128], v_aug(t, h),
                        True, True, s["p"], pfree[6], sig=(i == 2))
        s["num"] = mm(P[7][:, 0:129], MN[:, r, 256:384], v_aug(0, h), True, True, pfree[7], sig=True)
        pfree[5] = s["ca"] = act(CA[:, r, :, 0:129], P[5][:, 0:260].rearrange("p (d c) -> p d c", d=2)[:, :, 0:129],
                                 ACT.Copy, s["caug"], hd[h - 2]["int"] if h >= 2 else None, scale=SC)

    def m4_inter(h):
        s, r = hd[h], h % 2
        for d in range(2):
            tb = slice((1 - d) * 128, (1 - d) * 128 + 128)
            s["int"] = mm(P[7][:, 130 + d * 130:259 + d * 130], QK[:, h, tb], CA[:, r, d, 0:129], True, True, s["ca"],
                          sig=(d == 1))
        for d in range(2):
            a = act(T1[:, d, 0:129], P[7][:, 130 + d * 130:259 + d * 130], ACT.Copy, s["int"],
                    hd[h - 1]["out"] if h else None, scale=col(8 + d, h))
        b = act(DN[:, 0:3], P[6][:, 128:389:130], ACT.Abs, s["x"], hd[h - 1]["out"] if h else None)
        s["a"], s["b"] = a, b

    def m5_out(h):
        s = hd[h]
        f1 = tt(DV, T1[:, 0, 0:129], P[6][:, 130:259], T1[:, 0, 0:129], ALU.add, s["a"], s["b"])
        b0 = tt(DV, T1[:, 1, 0:129], P[7][:, 0:129], T1[:, 1, 0:129], ALU.add)
        pfree[7] = b0
        dn = stt(DV, DN[:, 1:4:2], T1[:, :, 128], -1.0, T1[:, :, 128], ALU.mult, ALU.max, b0)
        dn = tt(DV, DN[:, :], DN[:, :], COLS[:, 4:8, h], ALU.max, dn)
        dn = DV(lambda e: e.reciprocal(DN[:, :], DN[:, :]), dn)
        hs = [HS[:, t, h * 128:(h + 1) * 128] for t in range(2)]
        w = [gv_free[0], dn]
        a0 = ts(DV, hs[0], P[6][:, 0:128], DN[:, 0:1], None, ALU.mult, None, *w)
        a1 = ts(DV, hs[1], P[6][:, 260:388], DN[:, 2:3], None, ALU.mult, None)
        pfree[6] = a1
        a0 = stt(DV, hs[0], T1[:, 1, 0:128], DN[:, 3:4], hs[0], ALU.mult, ALU.add, a0)
        a1 = stt(DV, hs[1], T1[:, 0, 0:128], DN[:, 1:2], hs[1], ALU.mult, ALU.add, a1)
        s["out"] = a1
        for t in range(2):
            i = jnk[0] % 2
            jnk[0] += 1
            jnk[1][i] = s["ss"] = act(JNK[:, i, 0:128], hs[t], ACT.Square, a1, jnk[1][i],
                                      accum=SM[:, 4 + h * 2 + t:5 + h * 2 + t])

    ya = [[None] * 2 for _ in range(8)]

    def y_heads(p):
        r = rstd_of(SM[:, 4 + 4 * p:8 + 4 * p], 4, 1.0 / 128, EPS, hd[2 * p + 1]["ss"])
        for h in (2 * p, 2 * p + 1):
            for t in range(2):
                v = HS[:, t, h * 128:(h + 1) * 128]
                y_t = stt(DV, v, v, SM[:, 4 + h * 2 + t:5 + h * 2 + t], SO[:, t, h * 128:(h + 1) * 128],
                          ALU.mult, ALU.mult, r, so)
        fill(1)
        b = stream_bank()
        for h in (2 * p, 2 * p + 1):
            for t in range(2):
                v = HS[:, t, h * 128:(h + 1) * 128]
                done = tr(P[b][:, (h % 2) * 256 + t * 128:(h % 2) * 256 + t * 128 + 128], v, y_t, pfree[b],
                          sig=(t == 1))
        for q in (2 * p, 2 * p + 1):
            ya[q][0] = act(HA[:, q, :], P[b][:, (q % 2) * 256:(q % 2) * 256 + 256], ACT.Copy, done, hA_free,
                           scale=par("g_head", q))
        for q in (2 * p, 2 * p + 1):
            pfree[b] = ya[q][1] = stt(DV, LA[:, q, :], P[b][:, (q % 2) * 256:(q % 2) * 256 + 256], par("g_head", q),
                                      f(HA[:, q, :]), ALU.mult, ALU.subtract, ya[2 * p + 1][0])

    def spatial(half):
        b = 6 + half
        for g in (2 * half, 2 * half + 1):
            for c in range(2):
                out = P[b][:, (g % 2) * 256 + c * 128:(g % 2) * 256 + c * 128 + 128]
                mm(out, GV[:, c, g * 128:(g + 1) * 128], WST[:, g, :], True, False, gv_t[c], wst_tok, pfree[b])
                done = mm(out, con("ones", p=1), BS[:, g, :], False, True, bs_tok, sig=True)
        gv_free[0] = done
        sp = []
        for g in (2 * half, 2 * half + 1):
            v = pfree[b] = tt(DV, GU[:, g, :], P[b][:, (g % 2) * 256:(g % 2) * 256 + 256], GU[:, g, :], ALU.mult, done, gu_t[g])
            sp.append(v)
        for g in (2 * half, 2 * half + 1):
            a = act(HA[:, 4 + g, :], GU[:, g, :], ACT.Copy, sp[g % 2], hA_free)
            ya[4 + g] = [a, tt(DV, LA[:, 4 + g, :], GU[:, g, :], f(HA[:, 4 + g, :]), ALU.subtract, a)]

    gv_free = [None]
    for i in range(4, 8):
        todo.append(lambda i=i: t_out(HB, LB, tB, kx_evac(i)))
    vx_t = [None] * 4

    def vx_evac(h):
        def ev(t, bank, done):
            vx_t[2 * h + t] = act(VN[:, t, h * 512:(h + 1) * 512], bank[:, :], ACT.Copy, done)
            return vx_t[2 * h + t]
        return ev

    todo.extend(n_out(HB, LB, tB, vx_evac(0)))
    m1_products(0)
    spatial(0)
    m2_weights(0)
    spatial(1)
    m1_products(1)
    for i in range(2, 6):
        if i < 5:
            m2_weights(i - 1)
        m3_numerators(i - 2)
        if i < 4:
            m1_products(i)
        fill(1)
        m4_inter(i - 2)
        fill(1)
        m5_out(i - 2)
        if i == 3:
            y_heads(0)
    while todo:
        fill(1)

    def residual(half, x_t, nrm, after=None):
        def ev(t, bank, done):
            v = X[:, t, half * 512:(half + 1) * 512]
            a = tt(DV, v, bank[:, :], v, ALU.add, done)
            x_t[2 * t + half] = ms(t, half, v, a)
            if half == 1:
                nrm.a(t, x_t[2 * t:2 * t + 2])
            return a
        return ev

    x1 = [None] * 4
    nQ = Norm(X, "g_xattn", HA, LA)
    tY = lambda k, t: ya[k]
    steps = n_out(HA, LA, tY, residual(0, x1, nQ), pairs=(2, 3, 0, 1))
    todo.extend(steps)
    fill(1)
    y_heads(1)
    while todo:
        fill(1)

    def wo_mid(t):
        if t == 1:
            nQ.b(0)
            nQ.c(0, t0_done[0])
    t0_done = [None]

    def r1(t, bank, done, ev=residual(1, x1, nQ)):
        if t == 0:
            t0_done[0] = done
        return ev(t, bank, done)

    n_tiles(HA, LA, tY, r1, wo_mid, pairs=(2, 3, 0, 1))
    wo_done = PE.last()
    prev = now()
    for i in range(2):
        vacant.append((zslots[i], prev))
    load_units()

    vs = n_out(HB, LB, tB, vx_evac(1))
    vs[0]()
    nQ.b(1)
    nQ.c(1, wo_done)
    for s in vs[1:]:
        s()
    q_t = [None] * 8
    hB_free = PE.last()

    def qx_evac(i):
        def ev(bank, done):
            q_t[i] = act(QX[:, i, :], bank[:, 0:256], ACT.Copy, done, prev)
            return q_t[i]
        return ev

    XS = 256 ** -0.5
    xa = [{} for _ in range(4)]
    yx = [None] * 8

    def a1_scores(h):
        s, b = xa[h], 4 + h % 2
        for t in range(2):
            for k in range(2):
                s["s"] = mm(P[b][:, t * 256:(t + 1) * 256], QX[:, 2 * h + k, t * 128:(t + 1) * 128], KT[:, 2 * h + k, :],
                            k == 0, k == 1, q_t[2 * h + k], kx_t[2 * h + k], pfree[b], sig=(t == 1 and k == 1))

    def a2_softmax(h):
        s, b, r = xa[h], 4 + h % 2, h % 2
        sm = SM[:, 160 + 8 * r:168 + 8 * r]
        m = DV(lambda e: e.tensor_reduce(sm[:, 0:2], P[b][:, :].rearrange("p (t m) -> p t m", t=2), AX.X, ALU.max),
               s["s"], xa[h - 2]["p"] if h >= 2 else None)
        m = ts(DV, sm[:, 2:4], sm[:, 0:2], -XS, None, ALU.mult, None, m)
        for t in range(2):
            e_ = act(PX[:, r, t, :], P[b][:, t * 256:(t + 1) * 256], ACT.Exp, m,
                     xa[h - 2]["tr"] if h >= 2 else prev, bias=sm[:, 2 + t:3 + t], scale=XS, accum=sm[:, 4 + t:5 + t])
        pfree[b] = e_
        m = DV(lambda e: e.reciprocal(sm[:, 6:8], sm[:, 4:6]), e_)
        for t in range(2):
            s["p"] = ts(DV, PX[:, r, t, :], PX[:, r, t, :], sm[:, 6 + t:7 + t], None, ALU.mult, None, m)

    def a3_transpose(h):
        s, r = xa[h], h % 2
        for m in range(2):
            for t in range(2):
                s["tr"] = tr(P[6][:, m * 256 + t * 128:m * 256 + t * 128 + 128], PX[:, r, t, m * 128:(m + 1) * 128],
                             s["p"], pfree[6], sig=(m == 1 and t == 1))
        pfree[6] = s["pt"] = cp(DV, PTX[:, r, :, :], P[6][:, :].rearrange("p (m t) -> p m t", m=2), s["tr"],
                                xa[h - 2]["o"] if h >= 2 else prev)

    def a4_out(h):
        s, r = xa[h], h % 2
        for k in range(2):
            for m in range(2):
                s["o"] = mm(P[7][:, k * 256:(k + 1) * 256], VN[:, m, h * 256 + k * 128:h * 256 + k * 128 + 128],
                            PTX[:, r, m, :], m == 0, m == 1, s["pt"], vx_t, pfree[7], sig=(k == 1 and m == 1))
        a = [act(HB[:, 2 * h + k, :], P[7][:, k * 256:(k + 1) * 256], ACT.Copy, s["o"], hB_free) for k in range(2)]
        for k in range(2):
            l = tt(DV, LB[:, 2 * h + k, :], P[7][:, k * 256:(k + 1) * 256], f(HB[:, 2 * h + k, :]), ALU.subtract, a[1])
            yx[2 * h + k] = [a[k], l]
        pfree[7] = l

    t_out(HA, LA, nQ.tok, qx_evac(0))
    t_out(HA, LA, nQ.tok, qx_evac(1))
    for h in range(4):
        a1_scores(h)
        a2_softmax(h)
        if h:
            a4_out(h - 1)
        if h < 3:
            t_out(HA, LA, nQ.tok, qx_evac(2 * h + 2))
            a3_transpose(h)
            t_out(HA, LA, nQ.tok, qx_evac(2 * h + 3))
    qx_done = PE.last()
    x2 = [None] * 4
    nM = Norm(X, "g_moe", HB, LB)
    tX = lambda k, t: yx[k]
    steps = n_out(HB, LB, tX, residual(0, x2, nM))
    steps[0]()
    a3_transpose(3)
    steps[1]()
    a4_out(3)
    steps[2]()
    steps[3]()

    z = Region(Z, K1_AT - 8192)
    XT_AT = z.o
    XT = z("XT", [128, 2, 8, 256])
    SWT = z("SWT", [128, 2, 2, 256])
    GS_AT = z.o
    GS = z("GS", [128, 512])
    HT = z("HT", [128, 4, 128])
    YS = z("YS", [128, 1024])
    SS = z("SS", [128, 2, 256], F32R)
    SW = z("SW", [128, 2, 256])
    RS = z("RS", [128, 12, 64])
    MB = z("MB", [128, 2, 32], BF16)
    WF_AT = z.o
    GF2 = z("GF2", [128, 1024], keep=False)
    HF = z("HF", [128, 2, 2, 512])
    HBI = z("HBI", [128, 512])
    XTMP = z("XTMP", [128, 512])
    W3_AT = z.o
    W3 = z("W3", [64, 1024])
    ZP = z("ZP", [33, 256])
    W1 = z("W1", [33, 64])
    W2 = z("W2", [64, 64])
    FA = z("FA", [64, 256])
    FB = z("FB", [64, 256])
    zr = Region(W3_AT, z.o)
    WR = zr("WR", [128, 8, 36])
    WRH = zr("WRH", [128, 8, 36], F32R)
    WRL = zr("WRL", [128, 8, 36], F32R)
    LGT = zr("LGT", [36, 256])
    LTB = zr("LTB", [128, 128], BF16)
    ONB = zr("ONB", [128, 128], BF16)
    assert W3_AT >= za.o, (W3_AT, za.o)
    NHI = at("NHI", [128, 2, 1024], HA_AT, F32R)
    NLO = at("NLO", [128, 2, 1024], LA_AT, F32R)
    H32 = at("H32", [128, 8, 256], LB_AT)
    WF = at("WF", [128, 4, 1024], WF_AT)
    GF = at("GF", [128, 2, 512], GS_AT)
    HTF = at("HTF", [128, 4, 256], GS_AT + 4096)
    CAP = 64

    wr_t = load(WR[:, :, :], A["wr"], prev)
    wrh = act(WRH[:, :, :], WR[:, :, :], ACT.Copy, wr_t)
    wrl = tt(DV, WRL[:, :, :], WR[:, :, :], f(WRH[:, :, :]), ALU.subtract, wrh)
    ltb = act(LTB[:, :], con("lt"), ACT.Copy, prev)
    onb = act(ONB[:, :], con("ones"), ACT.Copy)

    def ox_mid(t):
        if t == 1:
            nM.b(0)
            nM.c(0, t0_done[0])

    nh, nl = [None, None], [None, None]

    def r2(t, bank, done, ev=residual(1, x2, nM)):
        if t == 0:
            t0_done[0] = done
        v = ev(t, bank, done)
        c = SM[:, 12 + t:13 + t]
        rc = ts(DV, c, nM.r, -0.5, None, ALU.mult, None, nM.rt)
        return v

    n_tiles(HB, LB, tX, r2, ox_mid)
    ox_done = PE.last()
    wslots = [Slot(at(f"WS{i}", [128, 2048], WH_AT + 8192 * i)[:, :], None, f"s_h{i}", U_B2) for i in range(NH // 2)]
    for w_ in wslots:
        vacant.append((w_, ox_done))
    load_units()
    nM.b(1)
    nM.c(1, ox_done)

    for k in range(8):
        out = P[0][0:36, 0:256]
        (h0, l0), (h1, l1) = nM.tok(k, 0), nM.tok(k, 1)
        mm(out, WRH[:, k, :], HB[:, k, :], k == 0, False, h0, h1, wrl, pfree[0])
        mm(out, WRL[:, k, :], HB[:, k, :], False, False)
        done = mm(out, WRH[:, k, :], LB[:, k, :], False, k == 7, l0, l1, sig=(k == 7))
    lg = pfree[0] = act(LGT[:, :], P[0][0:36, 0:256], ACT.Identity, done, bias=par("br", p=36))
    for t in range(2):
        done = tr(P[1][:, t * 36:(t + 1) * 36], LGT[:, t * 128:(t + 1) * 128], lg, pfree[1], n=36, sig=(t == 1))
    rc = DV.last()
    for t in range(2):
        c = SM[:, 12 + t:13 + t]
        nh[t] = act(NHI[:, t, :], X[:, t, :], ACT.Copy, rc, qx_done, scale=c)
        nl[t] = stt(DV, NLO[:, t, :], X[:, t, :], c, f(NHI[:, t, :]), ALU.mult, ALU.subtract, nh[t])

    def rs(i, n=64, w=None):
        a = RS[:, i, 0:n]
        return a if w is None else a.rearrange("p (t c) -> p t c", t=2)

    def bc(ap, *shape):
        return ap.unsqueeze(len(ap.shape)).broadcast_to(list(shape))

    def red(out, a, op, *d):
        return DV(lambda e: e.tensor_reduce(out, a, AX.X, op), *d)

    def first_max(a, n, mx, ix, oh, tmp, v):
        v = red(mx, a, ALU.max, v)
        v = tt(DV, tmp, a, bc(mx, 128, 2, n), ALU.not_equal, v)
        io = con("iota", 0, n).unsqueeze(1).broadcast_to([128, 2, n])
        v = stt(DV, tmp, tmp, 100.0, io, ALU.mult, ALU.add, v)
        v = red(ix, tmp, ALU.min, v)
        return tt(DV, oh, io, bc(ix, 128, 2, n), ALU.is_equal, v)

    LG = P[1][:, 0:72].rearrange("p (t c) -> p t c", t=2)
    LGG, LGE = LG[:, :, 0:4], LG[:, :, 4:36].rearrange("p t (g e) -> p t g e", g=4)
    gm, gx, ohg, tm = rs(0, 2), rs(0, 4)[:, 2:4], rs(1, 8, 1), rs(2, 8, 1)
    v = first_max(LGG, 4, gm, gx, ohg, tm, [done, ox_done])
    el, el3 = rs(4, 16, 1), rs(5, 64).rearrange("p (t g e) -> p t g e", t=2, g=4)
    v = tt(DV, el3, LGE, bc(ohg, 128, 2, 4, 8), ALU.mult, v)
    tmg = rs(7, 24)[:, 16:24].rearrange("p (t c) -> p t c", t=2)
    tg = pfree[1] = tt(DV, tmg, LGG, bc(gm, 128, 2, 4), ALU.subtract)
    tg = act(tmg, tmg, ACT.Exp, tg)
    v = red(el, el3.rearrange("p t g e -> p t e g"), ALU.add, v)
    m1, i1, oh1, t8 = rs(0, 6)[:, 4:6], rs(0, 8)[:, 6:8], rs(6, 16, 1), rs(7, 16, 1)
    v = first_max(el, 8, m1, i1, oh1, t8, v)
    v = stt(DV, el, oh1, -3e38, el, ALU.mult, ALU.add, v)
    m2, i2, oh2 = rs(0, 10)[:, 8:10], rs(0, 12)[:, 10:12], rs(8, 16, 1)
    v = first_max(el, 8, m2, i2, oh2, t8, v)
    one, two = rs(9, 64, 1), rs(10, 64, 1)
    g4 = lambda a: a.rearrange("p t (g e) -> p t g e", g=4)
    for dst, oh in ((one, oh1), (two, oh2)):
        v = tt(DV, g4(dst), bc(ohg, 128, 2, 4, 8), oh.unsqueeze(2).broadcast_to([128, 2, 4, 8]), ALU.mult, v)
    W_, POS, WOV = rs(5, 64, 1), rs(1, 64, 1), rs(2, 64, 1)
    m_t = v = tt(DV, MB[:, :, :], one, two, ALU.add, v, ox_done)
    mm(P[1][:, 128:160], LTB[:, :], MB[:, 0, :], True, True, m_t, ltb, onb, pfree[1])
    mm(P[1][:, 160:192], LTB[:, :], MB[:, 1, :], True, False)
    mm(P[1][:, 160:192], ONB[:, :], MB[:, 0, :], False, True)
    mm(P[1][:, 192:224], ONB[:, :], MB[:, 0, :], True, False)
    done = mm(P[1][:, 192:224], ONB[:, :], MB[:, 1, :], False, True, sig=True)
    v = ts(DV, POS, MB[:, :, :], 1000.0, -1000.0, ALU.mult, ALU.add, v)
    cmax = rs(11, 1)
    c_ = red(cmax, P[1][:, 192:224], ALU.max, done)
    v = tt(DV, POS, P[1][:, 128:192].rearrange("p (t c) -> p t c", t=2), POS, ALU.add, v)
    pos_t = pfree[1] = v
    cnt_t = cp(DV, CNT[:, 0:1], cmax, c_)
    w_t = []

    def weights():
        pt, qd, w1, w2 = rs(3, 2), rs(3, 4)[:, 2:4], rs(3, 6)[:, 4:6], rs(3, 8)[:, 6:8]
        u = tt(DV, qd, m2, m1, ALU.subtract)
        u = act(qd, qd, ACT.Exp, u)
        p_ = red(pt, tmg, ALU.add, tg)
        p_ = DV(lambda e: e.reciprocal(pt, pt), p_)
        u = ts(DV, w1, qd, 1.0, None, ALU.add, None, u)
        u = DV(lambda e: e.reciprocal(w1, w1), u)
        u = tt(DV, w1, w1, pt, ALU.mult, u, p_)
        u = tt(DV, w2, w1, qd, ALU.mult, u)
        for t in range(2):
            u = ts(DV, W_[:, t, :], one[:, t, :], w1[:, t:t + 1], None, ALU.mult, None, u)
            u = stt(DV, W_[:, t, :], two[:, t, :], w2[:, t:t + 1], W_[:, t, :], ALU.mult, ALU.add, u)
        w_t.append(stt(DV, WOV, POS, float(CAP), W_, ALU.is_ge, ALU.mult, u, pos_t))

    engines = (PE, AC, DV, PO, SP)
    fsem = [sem(f"s_f{n}") for n in range(6)]

    def general_path():
        fd = [0]
        entry = now()
        held = [(E.sem, E.n, E.q, E.seen) for E in engines]
        for E, s in zip(engines, fsem):
            E.sem, E.n, E.q, E.seen = s, 0, [], dict(E.seen)
            E.wait(entry)

        def fload(out, src, *d):
            SP.wait(*d)
            fd[0] += 16
            SP.q.append(lambda e: e.dma_start(out, src).then_inc(fsem[5], 16))
            return (fsem[5], fd[0])

        h_t = tt(DV, H32[:, :, :], f(HB[:, :, :]), f(LB[:, :, :]), ALU.add)
        free = None
        y_t = None
        for ex in range(32):
            u = U_MOE + (ex // 2) * UNITS_PER_GROUP
            parts = A["ws"][u:u + 12].rearrange("k p (e c) -> p k e c", e=2)[:, :, ex % 2, :]
            for m in range(2):
                w_t = fload(WF[:, :, :], parts[:, 4 * m:4 * m + 4, :], free)
                for t in range(2):
                    for k in range(8):
                        free = mm(P[2 * m + t][:, :], H32[:, k, t * 128:(t + 1) * 128],
                                  WF[:, k // 2, (k % 2) * 512:(k % 2) * 512 + 512], k == 0, k == 7,
                                  w_t, h_t, y_t, sig=(k == 7))
            g_t = [act(GF[:, t, :], P[t][:, :], ACT.Silu, free, y_t) for t in range(2)]
            hh = [tt(DV, GF[:, t, :], P[2 + t][:, :], GF[:, t, :], ALU.mult, g_t[t]) for t in range(2)]
            for k in range(4):
                for t in range(2):
                    d = tr(P[4 + k // 2][:, (k % 2) * 256 + t * 128:(k % 2) * 256 + t * 128 + 128],
                           GF[:, t, k * 128:(k + 1) * 128], hh, y_t, sig=(k == 3 and t == 1))
            for i in range(2):
                ht = cp(DV, HTF[:, 2 * i:2 * i + 2, :], P[4 + i][:, :].rearrange("p (k t) -> p k t", k=2), d)
            w_t = fload(WF[:, :, :], parts[:, 8:12, :], free)
            for t in range(2):
                for n in range(2):
                    for k in range(4):
                        free = mm(P[2 * t + n][:, :], HTF[:, k, t * 128:(t + 1) * 128],
                                  WF[:, k, n * 512:(n + 1) * 512], k == 0, k == 3, w_t, ht, sig=(k == 3))
            for t in range(2):
                for n in range(2):
                    v = X[:, t, n * 512:(n + 1) * 512]
                    y_t = stt(DV, v, P[2 * t + n][:, :], WOV[:, t, ex:ex + 1], v, ALU.mult, ALU.add, free)
        ends = [(E.sem, E.n) for E in engines if E.n]
        for E, (s_, n_, q_, seen_) in zip(engines, held):
            E.wait(ends)
            body = E.q
            E.sem, E.n, E.q, E.seen = s_, n_, q_, seen_
            E.wait(cnt_t)

            def branch(e, body=body):
                c = e.value_load(CNT[0:1, 0:1], min_val=0, max_val=512)
                with e.If(c > CAP):
                    for g in body:
                        g(e)
            E.q.append(branch)

    table("silu_and_others")
    mbank = [0]

    def misc_bank():
        mbank[0] += 1
        return 4 + mbank[0] % 4

    ex_st = {"ht": None}
    grp = [{} for _ in range(GROUPS + 1)]
    four = [{} for _ in range(GROUPS // 2)]

    def prepare(G):
        s, r = four[G], G % 2
        back, back2 = (four[G - 1] if G else {}), (four[G - 2] if G >= 2 else {})
        for j in range(4):
            for t in range(2):
                a = ts(DV, SS[:, t, j * 64:(j + 1) * 64], con("iota"), POS[:, t, 4 * G + j:4 * G + j + 1], None,
                       ALU.is_equal, None, pos_t, back.get("xt_mm"))
        yield
        for q in range(4):
            bk = misc_bank()
            for k in (2 * q, 2 * q + 1):
                out = P[bk][:, (k % 2) * 256:(k % 2) * 256 + 256]
                kc = slice(k * 128, (k + 1) * 128)
                for t in range(2):
                    mm(out, NHI[:, t, kc], SS[:, t, :], t == 0, False, a, nh, pfree[bk])
                    s["xt_mm"] = mm(out, NLO[:, t, kc], SS[:, t, :], False, t == 1, nl, sig=(k % 2 == 1 and t == 1))
            s["xt"] = tt(DV, XT[:, r, 2 * q:2 * q + 2, :], P[bk][:, :].rearrange("p (k s) -> p k s", k=2),
                         bc(PARS[:, PAR["g_moe"] + 2 * q:PAR["g_moe"] + 2 * q + 2], 128, 2, 256),
                         ALU.mult, s["xt_mm"], back2.get("up"))
            pfree[bk] = s["xt"]
            yield
        for j in range(4):
            e_ = 4 * G + j
            for t in range(2):
                b = ts(DV, SW[:, t, j * 64:(j + 1) * 64], con("iota"), POS[:, t, e_:e_ + 1], W_[:, t, e_:e_ + 1],
                       ALU.is_equal, ALU.mult, back.get("sw_mm"), w_t)
        yield
        for p in range(2):
            bk = misc_bank()
            for t in range(2):
                s["sw_mm"] = tr(P[bk][:, t * 128:(t + 1) * 128], SW[:, t, p * 128:(p + 1) * 128], b, pfree[bk],
                                sig=(t == 1))
            pfree[bk] = s["swt"] = act(SWT[:, r, p, :], P[bk][:, 0:256], ACT.Copy, s["sw_mm"], back2.get("comb"))
            yield

    preps = []

    def prep(n=1):
        for _ in range(n):
            if preps:
                try:
                    next(preps[0])
                except StopIteration:
                    preps.pop(0)

    unit = [U_MOE]

    def in_products(g, bank, name):
        G, r, p = four[g // 2], (g // 2) % 2, g % 2
        for kp in range(4):
            u = unit[0]
            unit[0] += 1
            w, wt = units[u][0].raw, units[u][1]
            for q in range(2):
                k = 2 * kp + q
                for e_ in range(2):
                    c = p * 128 + e_ * 64
                    done = mm(P[bank][e_ * 64:(e_ + 1) * 64, :], XT[:, r, k, c:c + 64],
                              w[:, e_ * 1024 + q * 512:e_ * 1024 + q * 512 + 512], k == 0, k == 7,
                              wt, G["xt"], pfree[bank], sig=(q == 1 and e_ == 1))
            free_unit(u, done)
            if kp % 2:
                prep()
            else:
                bg()
        grp[g][name] = G[name] = done

    def hidden(g):
        s = grp[g]
        a = pfree[0] = act(GS[:, :], P[0][:, :], ACT.Silu, s["gate"], ex_st["ht"])
        a = pfree[1] = tt(DV, GS[:, :], P[1][:, :], GS[:, :], ALU.mult, a, s["up"])
        if g > 1:
            combine(g - 1)
        bk = misc_bank()
        for k in range(4):
            d = tr(P[bk][:, k * 128:(k + 1) * 128], GS[:, k * 128:(k + 1) * 128], a, pfree[bk], sig=(k == 3))
        ex_st["ht"] = d
        pfree[bk] = s["ht"] = act(HT[:, :, :], P[bk][:, :].rearrange("p (k s) -> p k s", k=4), ACT.Copy, d,
                                  grp[g - 1].get("down"))

    def down(g):
        s = grp[g]
        prep()
        for k in range(4):
            u = unit[0]
            unit[0] += 1
            w, wt = units[u][0].raw, units[u][1]
            for n in range(2):
                for e_ in range(2):
                    done = mm(P[2 + n][e_ * 64:(e_ + 1) * 64, :], HT[:, k, e_ * 64:(e_ + 1) * 64],
                              w[:, e_ * 1024 + n * 512:e_ * 1024 + n * 512 + 512], k == 0, k == 3,
                              wt, s["ht"], pfree[2 + n], sig=(n == 1 and e_ == 1))
            free_unit(u, done)
            if k % 2:
                bg()
        s["down"] = done
        s["y"] = [act(YS[:, 0:512], P[2][:, :], ACT.Copy, done, grp[g - 1].get("comb")),
                  cp(DV, YS[:, 512:1024], P[3][:, :], done, grp[g - 1].get("comb"))]
        pfree[2], pfree[3] = s["y"]

    def combine(g, after=None):
        s, r = grp[g], (g // 2) % 2
        for t in range(2):
            for n in range(2):
                bk = misc_bank()
                s["comb"] = mm(P[bk][:, :], SWT[:, r, g % 2, t * 128:(t + 1) * 128], YS[:, n * 512:(n + 1) * 512], True, True,
                               four[g // 2]["swt"], s["y"][n], pfree[bk], sig=True)
                v = X[:, t, n * 512:(n + 1) * 512]
                pfree[bk] = v = tt(DV, v, P[bk][:, :], v, ALU.add, s["comb"])
                if after:
                    after(t, n, v)
        four[g // 2]["comb"] = s["comb"]

    K0 = at("K0", [128, 2, 2, 512], HB_AT)
    z = Region(LB_AT, LB_AT + 8192)
    TF = z("TF", [128, 2, 2, 256])
    DEC = z("DEC", [128, 2, 512])
    K1 = at("K1", [128, 2, 2, 512], K1_AT)
    KS_ = (K0, K1)
    k_done = [None, None]
    MAGIC = 1.5 * 2.0 ** 23
    C1, C2 = 6.28125, float(np.float32(2 * np.pi - 6.28125))
    C3 = float(np.float32(2 * np.pi - 6.28125 - np.float64(np.float32(C2))))
    PI_LO = float(np.nextafter(np.float32(np.pi), np.float32(0)))
    fs = {}

    def filters():
        nl_done = nl[1]
        prev = now()
        fs["tf"] = load(TF[:, :, :, :], A["dft"][:, 0:1024], prev)
        fs["dec"] = load(DEC[:, :, :], A["decay"], prev)
        fs["zp"] = load(ZP[:, :], A["zpos"], prev)
        for l in range(2):
            w = prev if l == 0 else fs["end"]
            fs["w1"] = load(W1[:, :], A["hw1"][l], w)
            fs["w2"] = load(W2[:, :], A["hw2"][l], w)
            fs["w3"] = load(W3[:, :], A["hw3"][l], w)
            fs["bias"] = load(HBI[:, :], A["hbias"][l].partition_broadcast(128), w)
            for _ in range(4):
                yield
            hp = lambda i: PARS[0:64, PAR[f"hf{l}"] + i:PAR[f"hf{l}"] + i + 1]
            bk = misc_bank()
            d = mm(P[bk][0:64, 0:256], W1[:, :], ZP[:, :], True, True, fs["w1"], fs["zp"], pfree[bk], sig=True)
            yield from sine(bk, hp(0), hp(1), d)
            yield
            bk = misc_bank()
            d = mm(P[bk][0:64, 0:256], W2[:, :], FA[:, :], True, True, fs["w2"], fs["sin"], pfree[bk], sig=True)
            yield from sine(bk, hp(2), hp(3), d)
            yield
            for t in range(2):
                for n in range(2):
                    bk = misc_bank()
                    d = mm(P[bk][:, :], FA[:, t * 128:(t + 1) * 128], W3[:, n * 512:(n + 1) * 512], True, True,
                           fs["sin"], fs["w3"], pfree[bk], sig=True)
                    a = tt(DV, HF[:, n, t, :], P[bk][:, :], DEC[:, t, :], ALU.mult, d, fs["dec"])
                    pfree[bk] = a
                    yield
            z0 = memset(DV, HF[0:1, 1, 0, :], 0.0, a)
            for t in range(2):
                c = tt(DV, XTMP[:, :], HF[:, 0, t, :], HF[:, 1, t, :], ALU.add, z0, fs.get("c"))
                b_ = tt(DV, HF[:, 1, t, :], HF[:, 0, t, :], HF[:, 1, t, :], ALU.subtract, z0)
                fs["c"] = cp(DV, HF[:, 0, t, :], XTMP[:, :], c, b_)
                yield
            for kind in range(2):
                for m in range(2):
                    bk = misc_bank()
                    for t in range(2):
                        d = mm(P[bk][:, :], TF[:, kind, t, m * 128:(m + 1) * 128], HF[:, kind, t, :], t == 0, t == 1,
                               fs["c"], fs["tf"], pfree[bk], sig=(t == 1))
                    w = prev if l == 0 else zslots[0].freed
                    if kind == 0:
                        e_ = tt(DV, KS_[l][:, 0, m, :], P[bk][:, :], HBI[:, :], ALU.add, d, fs["bias"], w)
                    else:
                        e_ = act(KS_[l][:, 1, m, :], P[bk][:, :], ACT.Copy, d, w)
                    pfree[bk] = e_
                    yield
                fs["e", kind] = e_
            k_done[l] = fs["end"] = [d, fs["e", 0], e_]
        gf = load(GF2[:, :], A["g_final"].partition_broadcast(128), fs["end"])
        fs["gf"] = ts(DV, GF2[:, :], GF2[:, :], -0.5, None, ALU.mult, None, gf)

    def sine(bk, b, fr, d):
        v = ts(DV, FA[:, :], P[bk][0:64, 0:256], b, fr, ALU.add, ALU.mult, d, fs.get("end"))
        pfree[bk] = v
        yield
        v = ts(DV, FB[:, :], FA[:, :], 1.0 / (2 * np.pi), MAGIC, ALU.mult, ALU.add, v)
        yield
        v = ts(DV, FB[:, :], FB[:, :], -MAGIC, None, ALU.add, None, v)
        for c in (C1, C2, C3):
            yield
            v = stt(DV, FA[:, :], FB[:, :], -c, FA[:, :], ALU.mult, ALU.add, v)
        yield
        v = ts(DV, FA[:, :], FA[:, :], PI_LO, -PI_LO, ALU.min, ALU.max, v)
        fs["sin"] = act(FA[:, :], FA[:, :], ACT.Sin, v)
        yield

    def until_out(*gens):
        for g in gens:
            for _ in g:
                pass

    preps.append(prepare(0))
    prep(5)
    weights()
    for g in range(GROUPS):
        if g % 2 == 0 and g // 2 + 1 < GROUPS // 2:
            preps.append(prepare(g // 2 + 1))
        in_products(g, 0, "gate")
        in_products(g, 1, "up")
        hidden(g)
        if g % 2:
            prep(20)
        down(g)
        if g == 0:
            combine(0)
            general_path()
            behind.append(filters())
    b2 = Region(Z, K1_AT)
    MG = b2("MG", [128, 4, 512])
    GSB = b2("GSB", [128, 2, 2, 256])
    X0 = b2("X0", [128, 4, 256])
    ZV = b2("ZV", [128, 4, 256])
    QPC = b2("QPC", [128, 2, 260])
    CVT = b2("CVT", [128, 2, 256])
    QT_AT = b2.o
    QT = b2("QT", [128, 4, 256])
    KT_AT = b2.o
    KTT = b2("KTT", [128, 4, 256])
    VV_AT = b2.o
    VV = b2("VV", [128, 2, 512])
    LAB_AT = b2.o
    LAB = b2("LAB", [128, 2, 2, 512])
    QE_AT = b2.o
    QE = b2("QE", [128, 2, 2, 130])
    KE = b2("KE", [128, 2, 2, 128])
    QE2_AT = b2.o
    QE2 = b2("QE2", [128, 2, 2, 130])
    KE2 = b2("KE2", [128, 2, 2, 128])
    OO_AT = b2.o
    OO = b2("OO", [128, 2, 512])
    SM_AT = b2.o
    QI = b2("QI", [128, 2, 128])
    ATT = b2("ATT", [128, 2, 128])
    AT2 = b2("AT2", [128, 2, 64])
    PW = b2("PW", [128, 4, 128], keep=False)
    KN = b2("KN", [128, 2, 128])
    UU = b2("UU", [128, 2, 128])
    W2A = b2("W2A", [128, 512])
    LRT = b2("LRT", [128, 256])
    CVT4 = at("CVT4", [128, 8, 128], LAB_AT)
    SGT = at("SGT", [128, 2, 512], VV_AT)
    PXP = at("PXP", [128, 4, 272], QE_AT)
    PSA = at("PSA", [128, 4, 272], LAB_AT)
    PH = at("PH", [128, 4, 256], LB_AT, F32R)
    PL = at("PL", [128, 4, 256], LB_AT + 4096, F32R)
    GO = OO
    GH = at("GH", [128, 4, 256], LAB_AT, F32R)
    GL = at("GL", [128, 4, 256], LAB_AT + 4096, F32R)
    ZVN = at("ZVN", [128, 2, 512], KT_AT)
    TMP = at("TMP", [128, 2, 512], VV_AT)
    TAB = at("TAB", [128, 4, 2, 256], QE_AT)
    YY = at("YY", [128, 2, 2, 512], SM_AT)
    assert SM_AT + 8192 <= K1_AT
    HH = at("HH", [128, 4, 256], OO_AT, F32R)
    HL = at("HL", [128, 4, 256], QT_AT, F32R)
    GB = at("GB", [128, 1024], LAB_AT)
    YB = at("YB", [128, 2, 1024], Z)
    FH = at("FH", [128, 4, 256], HB_AT, F32R)
    FL = at("FL", [128, 4, 256], HB_AT + 4096, F32R)
    GEL = at("GEL", [128, 2, 256], QT_AT)

    po = {}

    def post_piece(t, n, psum, done, *w):
        q = square(AC, psum, SM[:, 224 + 2 * t + n:225 + 2 * t + n], 1.0 / D, done, *w)
        y = tt(DV, YB[:, t, n * 512:(n + 1) * 512], psum, GB[:, n * 512:(n + 1) * 512], ALU.mult, q, po["gb"], *w)
        po[t, n] = (q, y)
        return y

    def post_tile(t, nrm):
        r, v = rstd_tile(t, po[t, 0][0], po[t, 1][0], base=224)
        s_ = []
        for n in range(2):
            x = X[:, t, n * 512:(n + 1) * 512]
            a = po["x", t, n] = stt(DV, x, YB[:, t, n * 512:(n + 1) * 512], r, x, ALU.mult, ALU.add, v, po[t, n][1])
            if nrm:
                s_.append(ms(t, n, x, a))
        if nrm:
            nrm.a(t, s_)

    def load_gain(src, *d):
        g = load(GB[:, :], src.partition_broadcast(128), *d)
        po["gb"] = ts(DV, GB[:, :], GB[:, :], -0.5, None, ALU.mult, None, g)

    def second_layer(l, nL, nxt):
        KF = KS_[l]
        prev = now()
        w2_t = load(W2A[0:49, :], A["gw2"][l], prev)
        pw_t = load(PW[:, :, :], A["pool_w"][l], prev)
        qz = memset(PO, QPC[:, :, :], 0.0, prev)
        z2 = memset(PO, ATT[:, :, :], 0.0, prev)
        z0 = memset(PO, PXP[:, :, 0:8], 0.0, prev)
        z1 = memset(PO, PXP[:, :, 264:272], 0.0)
        tA = nL.tok
        v_t = [None] * 2

        def v_evac(t, bank, done):
            v_t[t] = act(VV[:, t, :], bank[:, :], ACT.Copy, done, prev)
            return v_t[t]

        def v_mid(t):
            if t == 0:
                nL.b(1)
                nL.c(1, prev)

        nL.b(0)
        nL.c(0, prev)
        n_tiles(HA, LA, tA, v_evac, v_mid)
        go = [None, None]

        def g_evac(t, bank, done):
            go[t] = act(GO[:, t, :], bank[:, :], ACT.Copy, done, prev)
            return go[t]

        for s in n_out(HA, LA, tA, g_evac):
            s()

        def px_evac(i):
            def ev(bank, done):
                px[i] = act(PXP[:, i, 8:264], bank[:, 0:256], ACT.Copy, done, prev)
                return px[i]
            return ev

        px = [None] * 4
        for i in range(4):
            t_out(HA, LA, tA, px_evac(i))
        pd = []
        for g in range(4):
            step = 1
            v = [px[g], z0, z1, pd[g - 2] if g >= 2 else None]
            n = 272
            for i in range(g + 1):
                n -= step
                v = tt(PO, PSA[:, 2 * (g % 2) + i % 2, 0:n], (PXP[:, g, 0:n] if i == 0 else PSA[:, 2 * (g % 2) + (i - 1) % 2, 0:n]),
                       (PXP[:, g, step:step + n] if i == 0 else PSA[:, 2 * (g % 2) + (i - 1) % 2, step:step + n]),
                       ALU.add, v)
                step *= 2
            w = 2 << g
            ws = PSA[:, 2 * (g % 2) + g % 2, 8 - w // 2:8 - w // 2 + 256]
            for e0, c0 in ((0, 0), (248, 8)):
                v = tt(PO, ws[:, e0:e0 + 8], ws[:, e0:e0 + 8], con("edge", 16 * g + c0, 16 * g + c0 + 8), ALU.mult, v)
            pd.append(stt(DV, PXP[:, g, 8:264], ws, 1.0 / w, PXP[:, g, 8:264], ALU.mult, ALU.subtract, v))

        q_t, k_t = [None] * 4, [None] * 4

        def q_evac(i):
            def ev(bank, done):
                q_t[i] = act(QT[:, i, :], bank[:, 0:256], ACT.Copy, done, prev, scale=128 ** -0.5)
                return q_t[i]
            return ev

        def k_evac(i):
            def ev(bank, done):
                k_t[i] = act(KTT[:, i, :], bank[:, 0:256], ACT.Copy, done)
                return k_t[i]
            return ev

        for i in range(4):
            t_out(HA, LA, tA, q_evac(i))
        for i in range(4):
            t_out(HA, LA, tA, k_evac(i))
        lr = {}

        def lr_evac(bank, done):
            lr["t"] = act(LRT[:, :], bank[:, 0:256], ACT.Identity, done, bias=con("lrone"))
            return lr["t"]

        t_out(HA, LA, tA, lr_evac)

        ph = [None] * 4
        for i in range(2):
            for g in (2 * i, 2 * i + 1):
                d = mm(P[4 + i][:, (g % 2) * 256:(g % 2) * 256 + 256], PW[:, g, :], PXP[:, g, 8:264], True, True,
                       pw_t, pd[g], pfree[4 + i], sig=(g % 2 == 1))
            for g in (2 * i, 2 * i + 1):
                a = act(PH[:, g, :], P[4 + i][:, (g % 2) * 256:(g % 2) * 256 + 256], ACT.Copy, d, prev,
                        scale=par(f"pool_s{l}", g))
                ph[g] = [a, None]
            for g in (2 * i, 2 * i + 1):
                pfree[4 + i] = ph[g][1] = stt(DV, PL[:, g, :], P[4 + i][:, (g % 2) * 256:(g % 2) * 256 + 256],
                                              par(f"pool_s{l}", g), f(PH[:, g, :]), ALU.mult, ALU.subtract, a)

        hy = {}

        def hy_evac(i):
            def ev(bank, done):
                r = i % 2
                t0 = act(QPC[:, r, 2:258], bank[:, 0:256], ACT.Copy, done, qz, hy.get(("c", i - 2)))
                out = X0[:, i, :] if i < 4 else ZV[:, i - 4, :] if i < 8 else CVT[:, r, :]
                v = t1 = act(out, bank[:, 0:256], ACT.Identity, prev, hy.get(("m", i - 2)), bias=par(f"hcb{l}", i),
                             scale=par(f"hcw{l}", 12 + i))
                for j in (0, 2):
                    v = stt(DV, out, QPC[:, r, j + 1:j + 257], par(f"hcw{l}", 12 * j + i), out, ALU.mult, ALU.add, v, t0)
                hy[("c", i)] = v
                if i >= 8:
                    v = tt(DV, ZV[:, i - 8, :], ZV[:, i - 8, :], out, ALU.mult, v)
                    hy[("m", i)] = v
                return t1
            return ev

        for i in range(12):
            todo.append(lambda i=i: t_out(HA, LA, tA, hy_evac(i)))
        table("natural_log_exp_and_others")
        la = []
        for t in range(2):
            for d in range(2):
                b = 4 + 2 * t + d
                dn = mm(P[b][:, :], LRT[32 * d:32 * d + 17, t * 128:(t + 1) * 128], W2A[32 * d:32 * d + 17, :], True, True,
                        lr["t"], w2_t, pfree[b], sig=True)
                pfree[b] = v = ts(DV, LAB[:, t, d, :], P[b][:, :], -20.0, None, ALU.max, None, dn, prev, pd)
            v = act(LAB[:, t, :, :], LAB[:, t, :, :], ACT.Exp, v, scale=-1.0)
            v = act(LAB[:, t, :, :], LAB[:, t, :, :], ACT.Ln, v, bias=1.0)
            la.append(ts(DV, LAB[:, t, :, :], LAB[:, t, :, :], -1.0 / 16.0, -1.0, ALU.mult, ALU.max, v))
            fill(1)

        ATM = {"o": ph[3][1], "s": None, "u": ph[3][1]}
        bufs = ((QE, KE), (QE2, KE2))
        for h in range(4):
            qe, ke = bufs[h % 2]
            hc = slice(h * 128, (h + 1) * 128)
            old = hy.get(("h", h - 2))
            for d in range(2):
                b = 4 + d
                for t in range(2):
                    dn = mm(P[b][:, t * 130:t * 130 + 130], LAB[:, t, d, hc], con("cf" if d == 0 else "cb"), True, True,
                            la[t], pfree[b], sig=(t == 1))
                pv = P[b][:, 0:260].rearrange("p (t c) -> p t c", t=2)
                e1 = act(qe[:, d, :, :], pv, ACT.Exp, dn, old, pd, ph[3][1])
                e2 = act(ke[:, d, :, :], pv[:, :, 0:128], ACT.Exp, dn, scale=-1.0)
                pfree[b] = e2
            for d in range(2):
                e1 = tt(DV, qe[:, d, :, 0:128], qe[:, d, :, 0:128], QT[:, h, :].rearrange("p (t c) -> p t c", t=2),
                        ALU.mult, e2, q_t[h])
                e2 = tt(DV, ke[:, d, :, :], ke[:, d, :, :], KTT[:, h, :].rearrange("p (t c) -> p t c", t=2),
                        ALU.mult, k_t[h])
            for d in range(2):
                e1 = ts(DV, QI[:, d, :], qe[:, d, 1 - d, 0:128], qe[:, d, 1 - d, 128:129], None, ALU.mult, None, e1,
                        ATM["o"])
            fill(1)
            for d in range(2):
                dn = tr(P[5][:, d * 128:(d + 1) * 128], ke[:, d, d, :], e2, pfree[5], sig=(d == 1))
            kn = act(KN[:, :, :], P[5][:, 0:256].rearrange("p (d c) -> p d c", d=2), ACT.Copy, dn, ATM["u"])
            for t in range(2):
                c0 = t * 192
                kf, kb, qf, qb = ke[:, 0, t, :], ke[:, 1, t, :], qe[:, 0, t, 0:128], qe[:, 1, t, 0:128]
                mm(P[4][0:64, c0:c0 + 128], kf[:, 0:64], qf, True, True, e1, e2, pfree[4])
                mm(P[4][64:128, c0 + 64:c0 + 128], kf[:, 64:128], qf[:, 64:128], True, True)
                mm(P[4][64:128, c0:c0 + 64], kb[:, 64:128], qb[:, 0:64], True, True)
                mm(P[4][0:64, c0 + 128:c0 + 192], kb[:, 0:64], qb[:, 0:64], True, True)
                dn = mm(P[4][64:128, c0 + 128:c0 + 192], kb[:, 64:128], qb[:, 64:128], True, True, sig=(t == 1))
            hy[("h", h)] = dn
            sv = P[4][:, 0:384].rearrange("p (t c) -> p t c", t=2)
            a1 = tt(DV, ATT[:, :, :], sv[:, :, 0:128], con("m1").unsqueeze(1).broadcast_to([128, 2, 128]), ALU.mult, dn,
                    ATM["o"], z2)
            a2 = tt(DV, AT2[:, :, :], sv[:, :, 128:192], con("m2").unsqueeze(1).broadcast_to([128, 2, 64]), ALU.mult,
                    ATM["s"])
            pfree[4] = a2
            for lo in (0, 64):
                ATM["s"] = tt(DV, ATT[lo:lo + 64, :, lo:lo + 64], ATT[lo:lo + 64, :, lo:lo + 64], AT2[lo:lo + 64, :, :],
                              ALU.add, a1, a2)
            fill(1)
            for d in range(2):
                dn = mm(P[5][:, 256 + d * 128:384 + d * 128], KN[:, d, :], VV[:, d, hc], True, True, kn, v_t[d],
                        sig=(d == 1))
            ATM["u"] = dn
            for d in range(2):
                u_ = act(UU[:, d, :], P[5][:, 256 + d * 128:384 + d * 128], ACT.Copy, dn, ATM["o"],
                         scale=qe[:, d, d, 129:130])
            pfree[5] = u_
            fill(1)
            for t in range(2):
                mm(P[6 + t][:, hc], ATT[:, t, :], VV[:, t, hc], True, False, ATM["s"], pfree[6 + t])
                ATM["o"] = mm(P[6 + t][:, hc], QI[:, 1 - t, :], UU[:, 1 - t, :], False, True, u_, sig=True)
            fill(1)
        hd_free = [ATM["o"], u_, ATM["s"]]
        r = None
        for t in range(2):
            for h in range(4):
                r = act(CVT4[:, 4 * t + h, :], P[6 + t][:, h * 128:(h + 1) * 128], ACT.Square, ATM["o"],
                        accum=SM[:, 4 + 4 * t + h:5 + 4 * t + h])
        fill(1)
        r = rstd_of(SM[:, 4:12], 8, 1.0 / 128, EPS, r)
        while todo:
            fill(1)
        tab_t = load(TAB[:, :, :, :], A["dft"], hd_free, now())
        table("sigmoid_and_others")

        mg = [None] * 4
        gs = {}
        state = {"last": None}

        def gate_evac(i, p):
            def ev(bank, done):
                gs[i] = act(GSB[:, p % 2, i % 2, :], bank[:, 0:256], ACT.Sigmoid, done, mg_used[p % 2], prev)
                return gs[i]
            return ev

        mg_used = [None, None]

        def br_evac(p, which):
            def ev(bank, done):
                g_ = GSB[:, p % 2, :, :].rearrange("p a b -> p (a b)")
                if which == 0:
                    mg[p] = mg_used[p % 2] = tt(DV, MG[:, p, :], bank[:, :], g_, ALU.mult, done, gs[2 * p + 1], prev)
                    return mg[p]
                v = tt(DV, g_, bank[:, :], g_, ALU.mult, done, gs[2 * p + 1])
                mg[p] = mg_used[p % 2] = tt(DV, MG[:, p, :], MG[:, p, :], g_, ALU.add, v)
                if which == 2:
                    for k in (2 * p, 2 * p + 1):
                        src = MG[:, p, (k % 2) * 256:(k % 2) * 256 + 256]
                        a = act(HB[:, k, :], src, ACT.Copy, mg[p], hy["k"])
                        ym[k] = [a, tt(DV, LB[:, k, :], src, f(HB[:, k, :]), ALU.subtract, a, state["last"])]
                return v
            return ev

        ym = [None] * 8

        def branch_steps(which, hi, lo, tok):
            out = []
            for p in range(4):
                for i in (2 * p, 2 * p + 1):
                    out.append(lambda i=i, p=p: t_out(HA, LA, tA, gate_evac(i, p)))
                out.append(lambda p=p: t_out(hi, lo, tok, br_evac(p, which), kt=4, parts=2))
            return out

        todo.extend(branch_steps(0, PH, PL, lambda k, t: ph[k]))
        yg = [None] * 4
        so = act(SGT[:, :, :], GO[:, :, :], ACT.Sigmoid, go, hd_free)
        so = tt(DV, GO[:, :, :], GO[:, :, :], SGT[:, :, :], ALU.mult, so)
        for t in range(2):
            for h in range(4):
                o_ = GO[:, t, h * 128:(h + 1) * 128]
                y_ = stt(DV, o_, P[6 + t][:, h * 128:(h + 1) * 128], SM[:, 4 + 4 * t + h:5 + 4 * t + h], o_,
                         ALU.mult, ALU.mult, r, so)
            pfree[6 + t] = y_
        fill(2)
        for i in range(2):
            for h in (2 * i, 2 * i + 1):
                for t in range(2):
                    dn = tr(P[4 + i][:, (h % 2) * 256 + t * 128:(h % 2) * 256 + t * 128 + 128],
                            GO[:, t, h * 128:(h + 1) * 128], y_, pfree[4 + i], sig=(t == 1))
            for h in (2 * i, 2 * i + 1):
                a = act(GH[:, h, :], P[4 + i][:, (h % 2) * 256:(h % 2) * 256 + 256], ACT.Copy, dn, hd_free,
                        scale=par(f"gla_norm{l}"))
                yg[h] = [a, None]
            for h in (2 * i, 2 * i + 1):
                pfree[4 + i] = yg[h][1] = stt(DV, GL[:, h, :], P[4 + i][:, (h % 2) * 256:(h % 2) * 256 + 256],
                                              par(f"gla_norm{l}"), f(GH[:, h, :]), ALU.mult, ALU.subtract, a)
        go_free = dn
        for t in range(2):
            for c in range(4):
                dn = tr(P[6 + t][:, c * 128:(c + 1) * 128], ZV[:, c, t * 128:(t + 1) * 128], hy[("m", 8 + c)],
                        pfree[6 + t], sig=(c == 3))
            pfree[6 + t] = zn = act(ZVN[:, t, :], P[6 + t][:, :], ACT.Copy, dn, hd_free)
        while len(todo):
            fill(1)
        todo.extend(branch_steps(1, GH, GL, lambda k, t: yg[k]))
        yv = None
        for m in range(2):
            mc = slice(m * 128, (m + 1) * 128)
            zb = []
            for kind in range(2):
                b = 4 + 2 * m + kind
                for t in range(2):
                    dn = mm(P[b][:, :], TAB[:, kind, t, mc], ZVN[:, t, :], t == 0, t == 1, tab_t, zn, pfree[b],
                            sig=(t == 1))
                zb.append(dn)
            zr, zs = P[4 + 2 * m][:, :], P[5 + 2 * m][:, :]
            a = tt(DV, YY[:, 0, m, :], zr, KF[:, 0, m, :], ALU.mult, zb[0], hd_free, k_done[l])
            b_ = tt(DV, TMP[:, 0, :], zs, KF[:, 1, m, :], ALU.mult, zb[1], yv)
            c_ = tt(DV, YY[:, 1, m, :], zs, KF[:, 0, m, :], ALU.mult)
            pfree[5 + 2 * m] = c_
            d_ = tt(DV, TMP[:, 1, :], zr, KF[:, 1, m, :], ALU.mult)
            pfree[4 + 2 * m] = d_
            y1 = tt(PO, YY[:, 0, m, :], YY[:, 0, m, :], TMP[:, 0, :], ALU.subtract, a, b_)
            yv = tt(PO, YY[:, 1, m, :], YY[:, 1, m, :], TMP[:, 1, :], ALU.add, c_, d_)
            fill(2)
        hy["k"] = d_
        fill(4)
        yh = [None] * 4
        for i in range(2):
            for c in (2 * i, 2 * i + 1):
                out = P[4 + i][:, (c % 2) * 256:(c % 2) * 256 + 256]
                for kind in range(2):
                    for m in range(2):
                        dn = mm(out, YY[:, kind, m, c * 128:(c + 1) * 128], TAB[:, 2 + kind, m, :],
                                kind == 0 and m == 0, kind == 1 and m == 1, yv, pfree[4 + i],
                                sig=(kind == 1 and m == 1))
            x0 = X0[:, 2 * i:2 * i + 2, :].rearrange("p a b -> p (a b)")
            v = tt(DV, x0, P[4 + i][:, :], x0, ALU.mult, dn)
            pfree[4 + i] = v
            for c in (2 * i, 2 * i + 1):
                a = act(HH[:, c, :], X0[:, c, :], ACT.Copy, v, go_free, hd_free)
                yh[c] = [a, tt(DV, HL[:, c, :], X0[:, c, :], f(HH[:, c, :]), ALU.subtract, a)]
        while todo:
            fill(1)
        state["last"] = PE.last()
        todo.extend(branch_steps(2, HH, HL, lambda k, t: yh[k]))
        while todo:
            fill(1)

        prev = now()
        load_gain(A["post"][l, 0], prev)
        table("natural_log_exp_and_others")
        nF = Norm(X, f"ffn_pre{l}", HA, LA)
        tM = lambda k, t: ym[k]
        for s in n_out(HB, LB, tM, lambda t, bank, done: post_piece(t, 0, bank[:, :], done, prev)):
            s()

        def y_evac(t, bank, done):
            v = post_piece(t, 1, bank[:, :], done, prev)
            post_tile(t, nF)
            return v

        n_tiles(HB, LB, tM, y_evac, lambda t: None)
        nF.b(0)
        nF.c(0, prev)
        nF.b(1)
        nF.c(1, prev)

        prev = now()
        load_gain(A["post"][l, 1], prev)
        qz = memset(PO, QPC[:, :, :], 0.0, prev)
        tA = nF.tok
        table("gelu_and_others")
        ff = {}

        def a_evac(i):
            def ev(bank, done):
                r = i % 2
                t0 = act(QPC[:, r, 2:258], bank[:, 0:256], ACT.Copy, done, qz, ff.get(("c", i - 2)))
                out = CVT[:, r, :]
                v = t1 = act(out, bank[:, 0:256], ACT.Identity, ff.get(("g", i - 2)), bias=par(f"fcb{l}", i),
                             scale=par(f"fcw{l}", 22 + i))
                for j in (0, 2):
                    v = stt(DV, out, QPC[:, r, j + 1:j + 257], par(f"fcw{l}", 22 * j + i), out, ALU.mult, ALU.add, v, t0)
                ff[("c", i)] = v
                ff[("g", i)] = act(GEL[:, r, :], out, ACT.Gelu, v, ff.get(("b", i - 2)), prev)
                return t1
            return ev

        def b_evac(i):
            def ev(bank, done):
                r = i % 2
                g_ = GEL[:, r, :]
                v = tt(DV, g_, bank[:, 0:256], g_, ALU.mult, done, ff[("g", i)])
                a = act(FH[:, i % 4, :], g_, ACT.Copy, v, ff.get(("d", i - 4)), prev)
                ff[("b", i)] = tt(DV, FL[:, i % 4, :], g_, f(FH[:, i % 4, :]), ALU.subtract, a)
                ff[("y", i)] = [a, ff[("b", i)]]
                return v
            return ev

        def down(i, parts, tiles):
            hi, lo, t1, t2 = parts
            y = ff[("y", i)]
            for t in tiles:
                ta = slice(t * 128, (t + 1) * 128)
                for n in range(2):
                    out = P[4 + 2 * t + n][:, :]
                    w = slice(n * 512, (n + 1) * 512)
                    mm(out, FH[:, i % 4, ta], hi[:, w], i == 0, False, t1, y[0], pfree[4 + 2 * t + n] if i == 0 else None)
                    mm(out, FL[:, i % 4, ta], hi[:, w], False, False, y[1])
                    dn = mm(out, FH[:, i % 4, ta], lo[:, w], False, i == 21, t2, sig=(n == 1))
            return dn

        for i in range(22):
            t_out(HA, LA, tA, a_evac(i))
            t_out(HA, LA, tA, b_evac(i))
            if 0 < i < 19:
                c, parts = take()
                ff[("d", i - 1)] = down(i - 1, parts, (0, 1))
                give(c, ff[("d", i - 1)])
        table("natural_log_exp_and_others")
        ab_done = PE.last()
        got = [take() for _ in range(4)]
        for t in range(2):
            for j in range(4):
                c, parts = got[j]
                dn = down(18 + j, parts, (t,))
                if t == 1:
                    give(c, dn)
                    if j == 1:
                        split_chunks(st["chunk"] + LAHEAD)
            for n in range(2):
                pfree[4 + 2 * t + n] = post_piece(t, n, P[4 + 2 * t + n][:, :], dn, prev)
            post_tile(t, nxt)

    nL = [Norm(X, "mix_pre0", HA, LA), Norm(X, "mix_pre1", HA, LA), None]
    bg_all()
    table("natural_log_exp_and_others")
    sq = {}

    def last_norm(t, n, v):
        sq[t, n] = ms(t, n, X[:, t, n * 512:(n + 1) * 512], v)
        if n == 0:
            return
        r, v = rstd_tile(t, sq[t, 0], sq[t, 1])
        s_ = []
        for m in range(2):
            x = X[:, t, m * 512:(m + 1) * 512]
            a = po["x", t, m] = stt(DV, x, x, r, GF2[:, m * 512:(m + 1) * 512], ALU.mult, ALU.mult, v, fs["gf"])
            s_.append(ms(t, m, x, a))
        nL[0].a(t, s_)

    combine(GROUPS - 1, last_norm)
    assert all(w_.freed for w_ in wslots)
    his[:] = [(WH[:, i, :], wslots[i // 2].freed) for i in range(NH)]
    st["split"] = st["chunk"] = 2 * U_B2
    st["end"] = 2 * U_B2 + 2 * L_CHUNKS
    split_chunks(2 * U_B2 + LAHEAD)
    for l in range(2):
        second_layer(l, nL[l], nL[l + 1])
    s_out = sem("s_out")
    for t in range(2):
        SP.wait(po["x", t, 0], po["x", t, 1])
        SP.q.append(lambda e, t=t: e.dma_start(A["out"][0, t * 128:(t + 1) * 128, :], X[:, t, :]).then_inc(s_out, 16))
    SP.q.append(lambda e: e.wait_ge(s_out, 32))
    return finish()


def host_arrays(I):
    ws = np.zeros((N_UNITS, 128, 2048), np.float32)
    flat = ws.reshape(N_UNITS, 128, 2, 1024)

    def put(c, a):
        flat[c // 2, :, c % 2, :] = a.reshape(128, 1024)

    def kt(w):
        return w.reshape(-1, 128, w.shape[1]).transpose(1, 0, 2)

    def t_cols(c, w, col, n):
        for i in range(n):
            put(c + i, kt(w[:, col + 128 * i:col + 128 * i + 128]))

    def n_cols(c, w, col, pairs=(0, 1, 2, 3)):
        a = kt(w[:, col:col + 512])
        for i, j in enumerate(pairs):
            put(c + i, a[:, 2 * j:2 * j + 2])

    w, kvx = I["w_in"][0], I["w_kv_x"][0]
    gates = np.zeros((1024, 128), np.float32)
    for i, kind in enumerate((0, 2, 1, 3)):
        gates[:, 32 * i:32 * i + 4] = w[:, 2048 + 4 * kind:2052 + 4 * kind]
    n_cols(0, w, 1024)
    t_cols(4, gates, 0, 1)
    for i in range(4):
        t_cols(5 + 2 * i, w, 128 * i, 1)
        put(6 + 2 * i, kt(w[:, 1536:2048])[:, 2 * i:2 * i + 2])
        t_cols(13 + 2 * i, w, 512 + 128 * i, 1)
        t_cols(14 + 2 * i, kvx, 128 * i, 1)
    n_cols(21, w, 2064 + 512)
    t_cols(25, w, 2064, 4)
    t_cols(29, kvx, 512, 4)
    n_cols(33, kvx, 1024)
    for h in range(2):
        n_cols(37 + 4 * h, I["w_out"][0], 512 * h, (2, 3, 0, 1))
        n_cols(57 + 4 * h, I["w_o_x"][0], 512 * h)
    n_cols(45, kvx, 1536)
    t_cols(49, I["w_q_x"][0], 0, 8)

    for g in range(GROUPS):
        u = U_MOE + g * UNITS_PER_GROUP
        for m, name in enumerate(("w_gate", "w_up")):
            a = I[name][0][2 * g:2 * g + 2].reshape(2, 4, 2, 128, 512)
            ws[u + 4 * m:u + 4 * m + 4] = a.transpose(1, 3, 0, 2, 4).reshape(4, 128, 2048)
        a = I["w_down"][0][2 * g:2 * g + 2].reshape(2, 4, 128, 1024)
        ws[u + 8:u + 12] = a.transpose(1, 2, 0, 3).reshape(4, 128, 2048)

    for l in range(2):
        c0 = 2 * U_B2 + l * L_CHUNKS
        at = lambda n: c0 + L_AT[n]
        w2 = I["w_in_2"][l]
        t_cols(at("pool"), w2, 3616, 4)
        t_cols(at("q"), w2, 1536, 4)
        t_cols(at("k"), w2, 2048, 4)
        n_cols(at("v"), w2, 2560)
        n_cols(at("g"), w2, 3072)
        lr = np.zeros((1024, 128), np.float32)
        lr[:, 0:16] = w2[:, 3584:3600]
        lr[:, 32:48] = w2[:, 3600:3616]
        t_cols(at("lr"), lr, 0, 1)
        t_cols(at("hy"), w2, 0, 12)
        for b, (n, src) in enumerate((("pb", "pool"), ("gb", "gla"), ("hb", "hyena"))):
            gate0 = 4128 + 1024 * {"hyena": 0, "gla": 1, "pool": 2}[src]
            br = I[f"w_br_{src}_2"][l]
            for p in range(4):
                t_cols(at(n) + 3 * p, w2, gate0 + 256 * p, 2)
                put(at(n) + 3 * p + 2, np.stack([kt(br[:, 256 * p + 128 * i:256 * p + 128 * i + 128]) for i in range(2)], axis=1))
        for h in range(2):
            n_cols(at("wo") + 4 * h, I["w_out_2"][l], 512 * h)
        up, dn = I["ffn_w_up_2"][l], kt(I["ffn_w_down_2"][l])
        c = at("ffn")
        for i in range(22):
            t_cols(c, up, 128 * i, 1)
            t_cols(c + 1, up, 2816 + 128 * i, 1)
            c += 2
            if 0 < i < 19:
                put(c, dn[:, i - 1])
                c += 1
        for i in range(4):
            put(c + i, dn[:, 18 + i])

    gw2 = np.zeros((2, 49, 512), np.float32)
    for l in range(2):
        for d in range(2):
            gw2[l, 32 * d:32 * d + 16] = I["gla_gate_w2_2"][l, d]
            gw2[l, 32 * d + 16] = I["gla_gate_b_2"][l, d]

    par = np.zeros((128, N_PAR), np.float32)

    def vec(name, v):
        v = v.reshape(-1, 128).T if v.size >= 128 else v.reshape(-1, 1)
        par[:v.shape[0], PAR[name]:PAR[name] + v.shape[1]] = v

    for n in ("g_mix", "g_mem", "g_xattn", "g_moe", "g_head", "conv_w", "conv_b"):
        vec(n, I[n][0])
    for i, kind in enumerate((0, 2, 1, 3)):
        par[32 * i:32 * i + 4, PAR["gate_b"]] = I["gate_b"][0][4 * kind:4 * kind + 4]
    par[0:36, PAR["br"]] = np.concatenate([I["b_rg"][0], I["b_re"][0]])
    for l in range(2):
        vec(f"mix_pre{l}", I["norm_mix_pre_2"][l])
        vec(f"ffn_pre{l}", I["norm_ffn_pre_2"][l])
        vec(f"hcw{l}", I["hy_conv_w_2"][l])
        vec(f"hcb{l}", I["hy_conv_b_2"][l])
        for i, n in enumerate(("b1", "freq1", "b2", "freq2")):
            par[0:64, PAR[f"hf{l}"] + i] = I[f"hy_filt_{n}_2"][l]
        vec(f"gla_norm{l}", I["gla_norm_2"][l])
        vec(f"pool_s{l}", I["pool_scale_2"][l])
        vec(f"fcw{l}", I["ffn_conv_w_2"][l])
        vec(f"fcb{l}", I["ffn_conv_b_2"][l])
    out = {
        "x": I["x"][0].reshape(2, 128, 1024), "mem": I["mem"][0].reshape(2, 128, 1024), "ws": ws, "par": par,
        "con": constants(), "ln_g": I["ln_v_g"][0], "ln_b": I["ln_v_b"][0], "b_s": I["b_s"],
        "w_sT": I["w_s"][0].transpose(2, 0, 1),
        "wr": kt(np.concatenate([I["w_rg"][0], I["w_re"][0]], axis=1)),
        "gw2": gw2, "pool_w": I["pool_w_2"].transpose(0, 2, 1, 3), "g_final": I["g_final"],
        "post": np.stack([I["norm_mix_post_2"], I["norm_ffn_post_2"]], axis=1),
        "dft": dft_tables(), "decay": filter_tables()[1], "zpos": filter_tables()[0],
        "hw1": I["hy_filt_w1_2"], "hw2": I["hy_filt_w2_2"], "hw3": I["hy_filt_w3_2"], "hbias": I["hy_bias_2"],
    }
    return {k: np.ascontiguousarray(v) for k, v in out.items()}


def kernel(**inputs):
    import numpy as _np
    import concourse.bacc as _bacc
    from concourse import mybir as _mybir
    from concourse.bass_utils import run_bass_kernel_spmd as _run

    nc = _bacc.Bacc("TRN2", target_bir_lowering=False, num_devices=1)
    arrays, args = {}, {}
    for name, a in host_arrays({k: _np.asarray(v) for k, v in inputs.items()}).items():
        arrays[f"in_{name}_dram"] = a
        args[name] = nc.dram_tensor(f"in_{name}_dram", a.shape, _mybir.dt.from_np(a.dtype), kind="ExternalInput").ap()
    args["out"] = nc.dram_tensor("out_0_dram", (1, 256, 1024), _mybir.dt.float32, kind="ExternalOutput").ap()
    program(nc, args)
    r = _run(nc, [arrays], core_ids=[0])
    return r.results[0]["out_0_dram"]
```

```python
import concourse.bass as bass
from concourse import mybir
import numpy as np

F32 = mybir.dt.float32
F32R = mybir.dt.float32r
BF16 = mybir.dt.bfloat16
I32 = mybir.dt.int32
ALU = mybir.AluOpType
ACT = mybir.ActivationFunctionType
AX = mybir.AxisListType

T = 256
D = 1024
EPS = 1e-6
NEG = -1e30

FIRST_CHUNKS = 65
U_MOE = 33
GROUPS = 16
UNITS_PER_GROUP = 12
U_B2 = U_MOE + GROUPS * UNITS_PER_GROUP
LAYER = [("v", 4), ("g", 4), ("pool", 4), ("qk0", 2), ("lr", 1), ("qk", 6), ("hy", 12), ("pb", 12), ("gb", 12),
         ("hb", 12), ("wo", 8), ("ffn", 66)]
L_AT, _n = {}, 0
for _name, _w in LAYER:
    L_AT[_name] = _n
    _n += _w
L_CHUNKS = _n
N_UNITS = U_B2 + (2 * L_CHUNKS + 1) // 2

PAR = {}
_n = 0
for _name, _w in [("g_mix", 8), ("g_mem", 8), ("g_xattn", 8), ("g_moe", 8), ("conv_w", 40),
                  ("conv_b", 8), ("g_head", 4), ("gate_b", 1), ("br", 1),
                  ("mix_pre0", 8), ("mix_pre1", 8), ("ffn_pre0", 8), ("ffn_pre1", 8),
                  ("hcw0", 36), ("hcw1", 36), ("hcb0", 12), ("hcb1", 12),
                  ("hf0", 4), ("hf1", 4), ("gla_norm0", 1), ("gla_norm1", 1),
                  ("pool_s0", 4), ("pool_s1", 4), ("fcw0", 66), ("fcw1", 66),
                  ("fcb0", 22), ("fcb1", 22), ("gfin", 8)]:
    PAR[_name] = _n
    _n += _w
N_PAR = _n

CON = {}
_n = 0
for _name, _w in [("ident", 128), ("ones", 128), ("le", 128), ("ge", 128), ("lt", 128),
                  ("mf", 128), ("mb", 128), ("onehot", 512), ("iota", 64), ("cf", 130), ("cb", 130),
                  ("m1", 128), ("m2", 64), ("edge", 64), ("lrone", 1)]:
    CON[_name] = _n
    _n += _w
N_CON = _n


def constants():
    s = np.arange(128)[:, None]
    t = np.arange(128)[None, :]
    c = np.zeros((128, N_CON), np.float32)

    def put(name, a):
        c[:a.shape[0], CON[name]:CON[name] + a.shape[1]] = a

    put("ident", (s == t).astype(np.float32))
    put("ones", np.ones((128, 128), np.float32))
    put("le", (s <= t).astype(np.float32))
    put("ge", (s >= t).astype(np.float32))
    put("lt", (s < t).astype(np.float32))
    put("mf", np.where(s <= t, 0.0, NEG).astype(np.float32))
    put("mb", np.where(s >= t, 0.0, NEG).astype(np.float32))
    oh = np.zeros((4, 4, 128), np.float32)
    for h in range(4):
        oh[h, h, :] = 1.0
    put("onehot", oh.reshape(4, 512))
    put("iota", np.broadcast_to(np.arange(64, dtype=np.float32)[None], (128, 64)))
    le = (s <= t).astype(np.float32)
    cf = np.concatenate([le - le[:, 63:64], le[:, 63:64], 1.0 - le[:, 63:64]], axis=1)
    ge = (s >= t).astype(np.float32)
    cb = np.concatenate([ge - ge[:, 64:65], ge[:, 64:65], 1.0 - ge[:, 64:65]], axis=1)
    put("cf", cf.astype(np.float32))
    put("cb", cb.astype(np.float32))
    m1 = np.ones((128, 128), np.float32)
    for a in (0, 64):
        m1[a:a + 64, a:a + 64] = le[:64, :64]
    put("m1", m1)
    put("m2", np.concatenate([(s > t).astype(np.float32)[:64, :64]] * 2, axis=0))
    edge = np.ones((4, 16), np.float32)
    for g, w in enumerate((2, 4, 8, 16)):
        half = w // 2
        for i in range(8):
            edge[g, i] = w / min(w, i + half)
            edge[g, 8 + i] = w / min(w, 8 - i + half)
    put("lrone", ((s == 16) | (s == 48)).astype(np.float32))
    put("edge", np.broadcast_to(edge.reshape(1, 64), (128, 64)))
    return c


def dft_tables():
    s = np.arange(256, dtype=np.float64)[:, None]
    w = 2.0 * np.pi * (np.arange(256, dtype=np.float64)[None, :] + 0.5) / 512.0
    a = s * w
    out = np.zeros((128, 4, 2, 256), np.float32)
    out[:, 0] = np.cos(a).reshape(2, 128, 256).transpose(1, 0, 2)
    out[:, 1] = np.sin(a).reshape(2, 128, 256).transpose(1, 0, 2)
    out[:, 2] = (np.cos(a).T / 256.0).reshape(2, 128, 256).transpose(1, 0, 2)
    out[:, 3] = (np.sin(a).T / 256.0).reshape(2, 128, 256).transpose(1, 0, 2)
    return out.reshape(128, 2048)


def filter_tables():
    L = T
    t = np.linspace(0.0, 1.0, L, dtype=np.float32)[:, None]
    w = (2.0 * np.pi * np.arange(L, dtype=np.float32)[:, None] / L).astype(np.float32)
    f = np.linspace(1e-4, 15, 16, dtype=np.float32)[None, :]
    ang = (f * w).astype(np.float32)
    z = np.concatenate([t, np.cos(ang), -np.sin(ang)], axis=-1).astype(np.float32)
    mx, mn = np.log(1e-2) / 0.3, np.log(1e-2) / 1.5
    deltas = np.linspace(mn, mx, 512, dtype=np.float32)
    decay = np.exp(-t * np.abs(deltas)).astype(np.float32)
    return np.ascontiguousarray(z.T), np.ascontiguousarray(decay.reshape(2, 128, 512).transpose(1, 0, 2).reshape(128, 1024))


class Eng:

    def __init__(self, sem):
        self.sem = sem
        self.n = 0
        self.q = []
        self.seen = {}

    def wait(self, *toks):
        for t in toks:
            if t is None:
                continue
            if isinstance(t, list):
                self.wait(*t)
                continue
            if self.seen.get(t[0].name, 0) < t[1]:
                self.seen[t[0].name] = t[1]
                self.q.append(lambda e, t=t: e.wait_ge(t[0], t[1]))

    def __call__(self, fn, *toks, sig=True):
        self.wait(*toks)
        if not sig:
            self.q.append(fn)
            return None
        self.n += 1
        sem = self.sem
        self.q.append(lambda e: fn(e).then_inc(sem, 1))
        return (sem, self.n)

    def last(self):
        return (self.sem, self.n)


def program(nc, A):
    ctx_sems = []

    def sem(name):
        s = nc.alloc_semaphore(name)
        ctx_sems.append(s)
        return s

    PE, AC, DV, PO, SP = (Eng(sem(f"s_{n}")) for n in ("pe", "act", "dve", "pool", "sp"))

    BASE = 16896
    R = 7

    def at(name, shape, off, dt=F32):
        return nc.alloc_sbuf_tensor_at(name, shape, dt, offset=off)

    class Region:

        def __init__(self, start, end):
            self.o, self.end = start, end

        def __call__(self, name, shape, dt=F32, keep=True):
            n = 2 if dt == BF16 else 4
            for w in shape[1:]:
                n *= w
            t = at(name, shape, self.o, dt)
            if keep:
                self.o += (n + 31) // 32 * 32
            assert self.o <= self.end, (name, self.o, self.end)
            return t

    NH = 6
    fix = Region(BASE, 229344)
    X = fix("X", [128, 2, 1024])
    HA_AT = fix.o
    HA = fix("HA", [128, 8, 256], F32R)
    LA_AT = fix.o
    LA = fix("LA", [128, 8, 256], F32R)
    HB_AT = fix.o
    HB = fix("HB", [128, 8, 256], F32R)
    LB_AT = fix.o
    LB = fix("LB", [128, 8, 256], F32R)
    WH_AT = fix.o
    WH = fix("WH", [128, NH, 1024], F32R)
    PARS = fix("PARS", [128, N_PAR])
    CONS = fix("CONS", [128, N_CON])
    SM = fix("SM", [128, 240])
    CNT = fix("CNT", [128, 8], I32)
    JNK = fix("JNK", [128, 2, 512], BF16)
    DIAG = fix("DIAG", [128, 2, 128])
    RING = fix("RING", [128, R, 2048], keep=False)
    RINGL = fix("RINGL", [128, R, 2048], F32R)
    Z, ZEND = fix.o, fix.end

    P = [nc.alloc_psum_tensor(f"P{i}", [128, 512], F32) for i in range(8)]
    pfree = [None] * 8

    def con(name, a=0, b=None, p=128):
        c = CON[name]
        w = {"iota": 64, "onehot": 512, "cf": 130, "cb": 130, "m2": 64, "edge": 64, "lrone": 1}.get(name, 128)
        return CONS[0:p, c + a:c + (w if b is None else b)]

    def par(name, i=0, p=128, p0=0):
        return PARS[p0:p0 + p, PAR[name] + i:PAR[name] + i + 1]

    IDENT = con("ident")

    def tt(E, out, a, b, op, *d):
        return E(lambda e: e.tensor_tensor(out, a, b, op), *d)

    def ts(E, out, a, s1, s2, op0, op1, *d):
        if op1 is None:
            return E(lambda e: e.tensor_scalar(out, a, s1, None, op0), *d)
        return E(lambda e: e.tensor_scalar(out, a, s1, s2, op0, op1), *d)

    def stt(E, out, a, s, b, op0, op1, *d):
        return E(lambda e: e.scalar_tensor_tensor(out, a, s, b, op0, op1), *d)

    def cp(E, out, a, *d):
        return E(lambda e: e.tensor_copy(out, a), *d)

    def act(out, a, func, *d, bias=0.0, scale=1.0, accum=None):
        if accum is None:
            return AC(lambda e: e.activation(out, a, func, bias=bias, scale=scale), *d)
        return AC(lambda e: e.activation(out, a, func, bias=bias, scale=scale, accum_out=accum), *d)

    def table(name):
        AC(lambda e: e.preload_act_table_set(name), sig=False)

    def mm(out, lhsT, rhs, start, stop, *d, sig=False):
        return PE(lambda e: e.matmul(out, lhsT, rhs, start=start, stop=stop), *d, sig=sig)

    def tr(out, a, *d, sig=False, n=128):
        return PE(lambda e: e.transpose(out, a, IDENT if n == 128 else CONS[0:n, 0:n]), *d, sig=sig)

    def memset(E, ap, v, *d):
        return E(lambda e: e.memset(ap, v), *d)

    def f(ap):
        return ap.bitcast(F32)

    pool_sems = [[sem(f"s_ld{i}"), 0, None] for i in range(24)]
    pool_at = [0]

    def load(out, src, *d):
        r = pool_sems[pool_at[0] % len(pool_sems)]
        pool_at[0] += 1
        SP.wait(*d)
        if r[1]:
            SP.wait((r[0], r[1]))
        r[1] += 16
        s = r[0]
        SP.q.append(lambda e: e.dma_start(out, src).then_inc(s, 16))
        return (r[0], r[1])

    class Slot:

        def __init__(self, raw, lo, name, until, own=None):
            self.raw, self.lo, self.sem, self.n, self.until, self.freed = raw, lo, sem(name), 0, until, None
            self.own = own
            if own is not None:
                reserved.add(own)

    reserved = set()
    slots = [Slot(RING[:, i, :], RINGL[:, i, :], f"s_w{i}", N_UNITS) for i in range(R)]
    unit_n = [0]
    units = {}
    vacant = [(s_, None) for s_ in slots]

    def load_units(n=None):
        while vacant and unit_n[0] < N_UNITS and (n is None or n > 0):
            u = unit_n[0]
            fit = [i for i, v in enumerate(vacant) if v[0].lo is not None or u >= U_MOE]
            if not fit:
                break
            s_, d = vacant.pop(fit[0])
            if s_.own is not None:
                u, s_.own = s_.own, None
            elif u >= s_.until:
                s_.freed = d
                continue
            else:
                unit_n[0] += 2 if u + 1 in reserved else 1
            if n is not None:
                n -= 1
            SP.wait(d)
            s_.n += 16
            SP.q.append(lambda e, s_=s_, u=u: e.dma_start(s_.raw, A["ws"][u]).then_inc(s_.sem, 16))
            units[u] = [s_, (s_.sem, s_.n), 0, []]

    def free_unit(u, *toks):
        vacant.append((units.pop(u)[0], list(toks)))
        load_units()

    LAHEAD = 4
    st = {"split": 0, "chunk": 0, "end": FIRST_CHUNKS, "bg": 0}
    his = [(WH[:, (i + 1) % NH, :], None) for i in range(NH)]
    halves = {}

    by_pool = {1, 3} | {2 * U_B2 + l * L_CHUNKS + L_AT[n] + i for l, n, i in
               ((0, "v", 0), (0, "v", 3), (0, "g", 0), (0, "g", 2),
                (1, "v", 0), (1, "v", 1), (1, "v", 3), (1, "g", 0), (1, "g", 2),
                (0, "ffn", 12), (1, "ffn", 12))}

    def split_chunks(end):
        while st["split"] < min(end, st["end"]) and his:
            c = st["split"]
            st["split"] += 1
            hi, free = his.pop(0)
            s_, tok = units[c // 2][:2]
            w = slice((c % 2) * 1024, (c % 2) * 1024 + 1024)
            t1 = act(hi, s_.raw[:, w], ACT.Copy, tok, free)
            t2 = tt(PO if c in by_pool else DV, s_.lo[:, w], s_.raw[:, w], f(hi), ALU.subtract, t1)
            halves[c] = (hi, s_.lo[:, w], t1, t2)

    def take(split=True):
        c = st["chunk"]
        st["chunk"] += 1
        if split:
            split_chunks(c + 1 + LAHEAD)
        return c, halves[c]

    def give(c, done):
        his.append((halves.pop(c)[0], done))
        u = units[c // 2]
        u[2] += 1
        u[3].append(done)
        if u[2] == 2 or c == st["end"] - 1:
            free_unit(c // 2, *u[3])

    behind = []

    def bg(n=1):
        for _ in range(n):
            while behind:
                try:
                    next(behind[0])
                    break
                except StopIteration:
                    behind.pop(0)

    def bg_all(*gens):
        while behind and (not gens or any(g in behind for g in gens)):
            bg()

    sbank = [0]
    held = set()

    def stream_bank(hold=False):
        while sbank[0] % 4 in held:
            sbank[0] += 1
        b = sbank[0] % 4
        sbank[0] += 1
        if hold:
            held.add(b)
        return b

    def t_out(hi_a, lo_a, a_tok, evac, kt=8, parts=1, split=True):
        c, (hi, lo, t1, t2) = take(split)
        b = stream_bank()
        for q in range(parts):
            out = P[b][:, q * 256:(q + 1) * 256]
            for k in range(kt):
                w = slice((q * kt + k) * 128, (q * kt + k + 1) * 128)
                (h0, l0), (h1, l1) = a_tok(k, 0), a_tok(k, 1)
                mm(out, hi[:, w], hi_a[:, k, :], k == 0, False, t1, h0, h1, pfree[b])
                mm(out, lo[:, w], hi_a[:, k, :], False, False, t2)
                done = mm(out, hi[:, w], lo_a[:, k, :], False, k == kt - 1, l0, l1,
                          sig=(k == kt - 1 and q == parts - 1))
        give(c, done)
        pfree[b] = evac(P[b], done)
        bg(st["bg"])

    def n_out(hi_a, lo_a, a_tok, evac, pairs=(0, 1, 2, 3)):
        banks = []

        def step(j):
            c, (hi, lo, t1, t2) = take(False)
            if j == 0:
                banks.extend([stream_bank(True), stream_bank(True)])
            ends = []
            for i in range(2):
                k = 2 * pairs[j] + i
                w = slice(i * 512, (i + 1) * 512)
                for t in range(2):
                    out = P[banks[t]][:, :]
                    ta = slice(t * 128, (t + 1) * 128)
                    first, last = j == 0 and i == 0, j == 3 and i == 1
                    th, tl = a_tok(k, t)
                    mm(out, hi_a[:, k, ta], hi[:, w], first, False, t1, th, pfree[banks[t]] if first else None)
                    mm(out, hi_a[:, k, ta], lo[:, w], False, False, t2)
                    done = mm(out, lo_a[:, k, ta], hi[:, w], False, last, tl, sig=(last or (i == 1 and t == 1)))
                    if last:
                        ends.append((t, done))
            give(c, done)
            for t, d in ends:
                held.discard(banks[t])
                pfree[banks[t]] = evac(t, P[banks[t]], d)
            split_chunks(c + 1 + LAHEAD)
            bg(st["bg"])
        return [lambda j=j: step(j) for j in range(4)]

    def n_tiles(hi_a, lo_a, a_tok, evac, mids, pairs=(0, 1, 2, 3), ahead=LAHEAD + 1, split=True):
        got = [take(split) for _ in range(4)]
        for t in range(2):
            ta = slice(t * 128, (t + 1) * 128)
            b = stream_bank()
            for j in range(4):
                if (t, j) in mids:
                    mids[t, j]()
                c, (hi, lo, t1, t2) = got[j]
                for i in range(2):
                    k = 2 * pairs[j] + i
                    w = slice(i * 512, (i + 1) * 512)
                    th, tl = a_tok(k, t)
                    first, last = j == 0 and i == 0, j == 3 and i == 1
                    mm(P[b][:, :], hi_a[:, k, ta], hi[:, w], first, False, t1, th, pfree[b])
                    mm(P[b][:, :], hi_a[:, k, ta], lo[:, w], False, False, t2)
                    done = mm(P[b][:, :], lo_a[:, k, ta], hi[:, w], False, last, tl, sig=(last or (t == 1 and i == 1)))
                if t == 1:
                    give(c, done)
                    if j == 2:
                        split_chunks(st["chunk"] + ahead)
            pfree[b] = evac(t, P[b], done)

    todo = []

    def fill(n):
        for _ in range(n):
            if todo:
                todo.pop(0)()

    def now():
        return [E.last() for E in (PE, AC, DV, PO) if E.n]

    def rstd_of(ss, n, scale, eps, *d):
        m = SM[:, 64:64 + n]
        y = SM[:, 96:96 + n]
        a = SM[:, 128:128 + n]
        t0 = ts(DV, m, ss, scale, eps, ALU.mult, ALU.add, *d)
        t1 = act(y, m, ACT.Ln, t0)
        t1 = act(y, y, ACT.Exp, t1, scale=-0.5)
        t2 = tt(DV, a, y, y, ALU.mult, t1)
        t2 = stt(DV, a, a, -0.5, m, ALU.mult, ALU.mult, t2)
        return stt(DV, ss, a, 1.5, y, ALU.add, ALU.mult, t2)

    jnk = [0, [None, None]]

    def square(E, x, acc, scale, *d):
        i = jnk[0] % 2
        jnk[0] += 1
        if E is AC:
            v = act(JNK[:, i, :], x, ACT.Square, jnk[1][i], *d, scale=scale ** 0.5, accum=acc)
        else:
            v = DV(lambda e: e.tensor_tensor_reduce(JNK[:, i, :], x, x, scale, 0.0, ALU.mult, ALU.add, acc), jnk[1][i], *d)
        jnk[1][i] = v
        return v

    def ms(t, n, x, *d, E=None):
        c = 200 + 2 * t + n
        return square(E or AC, x, SM[:, c:c + 1], 1.0 / D, *d)

    def rstd_steps(t, *d, base=200):
        o_ = base + 8 + 4 * t
        m, y, a, r = (SM[:, o_ + i:o_ + i + 1] for i in range(4))
        v = ts(DV, m, SM[:, base + 2 * t:base + 1 + 2 * t], SM[:, base + 1 + 2 * t:base + 2 + 2 * t], EPS, ALU.add,
               ALU.add, *d)
        yield
        v = act(y, m, ACT.Ln, v)
        yield
        v = act(y, y, ACT.Exp, v, scale=-0.5)
        yield
        v = stt(DV, a, y, m, y, ALU.mult, ALU.mult, v)
        yield
        return r, stt(DV, r, a, -3.0, y, ALU.add, ALU.mult, v)

    def run(gen, n=1000):
        for _ in range(n):
            try:
                next(gen)
            except StopIteration:
                return

    def weave(chain, split, plan):
        for n, m in plan:
            run(chain, n)
            run(split, m)
        run(chain)
        run(split)

    def alternate(*gens):
        gens = list(gens)
        while gens:
            for g in gens[:]:
                try:
                    next(g)
                except StopIteration:
                    gens.remove(g)

    class Norm:

        def __init__(self, x, g, hi, lo):
            self.x, self.g, self.hi, self.lo = x, g, hi, lo
            self.toks, self.d, self.done, self.rs = {}, {}, {}, {}

        def tok(self, k, t):
            return self.toks[k, t]

        def a_steps(self, t, *d):
            r, v = self.rs[t] = yield from rstd_steps(t, *d)
            yield
            self.d[t] = ts(DV, DIAG[:, t, :], IDENT, r, -0.5, ALU.mult, ALU.mult, v, diag_used[t])

        def a(self, t, *d):
            run(self.a_steps(t, *d))

        def b(self, t):
            self.done[t] = []
            for i in range(2):
                bk = 4 + 2 * t + i
                for q in range(4):
                    k = 4 * i + q
                    dn = mm(P[bk][:, q * 128:(q + 1) * 128], self.x[:, t, k * 128:(k + 1) * 128], DIAG[:, t, :],
                            True, True, self.d[t], pfree[bk], sig=(q == 3))
                self.done[t].append(dn)
            diag_used[t] = dn

        def c(self, t, *w):
            run(self.c_steps(t, *w))

        def c_steps(self, t, *w):
            ta = slice(t * 128, (t + 1) * 128)
            for i in range(2):
                bk = 4 + 2 * t + i
                hs = []
                for q in range(4):
                    k = 4 * i + q
                    hs.append(act(self.hi[:, k, ta], P[bk][:, q * 128:(q + 1) * 128], ACT.Copy, self.done[t][i], *w,
                                  scale=par(self.g, k)))
                    yield
                for q in range(4):
                    k = 4 * i + q
                    v = stt(DV, self.lo[:, k, ta], P[bk][:, q * 128:(q + 1) * 128], par(self.g, k), f(self.hi[:, k, ta]),
                            ALU.mult, ALU.subtract, hs[3], *w)
                    self.toks[k, t] = (hs[q], v)
                    if q == 3:
                        pfree[bk] = v
                    yield

    diag_used = [None, None]

    def finish():
        for E in (PE, AC, DV, PO):
            if E.n:
                SP.wait(E.last())
        for r in pool_sems:
            if r[1]:
                SP.wait((r[0], r[1]))
        for u in units.values():
            SP.wait(u[1])
        with nc.Block() as block:
            @block.sync
            def _(e):
                for g in SP.q:
                    g(e)

            @block.scalar
            def _(e):
                for g in AC.q:
                    g(e)

            @block.vector
            def _(e):
                for g in DV.q:
                    g(e)

            @block.gpsimd
            def _(e):
                for g in PO.q:
                    g(e)

            @block.tensor
            def _(e):
                for g in PE.q:
                    g(e)

    z = Region(Z, ZEND)
    KT = z("KT", [128, 8, 256])
    MEM = z("MEM", [128, 2, 1024], keep=False)
    VN = z("VN", [128, 2, 1024])
    IG = z("IG", [4, 2, 256])
    FG = z("FG", [4, 2, 256])
    RT1 = z("RT1", [4, 2, 256])
    NC = z("NC", [4, 2, 256])
    SI = z("SI", [4, 2, 128])
    KWR = z("KWR", [4, 2, 128])
    ONEROW = z("ONEROW", [4, 128])
    QP = z("QP", [128, 2, 260])
    QK = z("QK", [128, 8, 256])
    V1 = z("V1", [128, 2, 4, 130])
    SO = z("SO", [128, 2, 512])
    GV = z("GV", [128, 2, 512], keep=False)
    HS = z("HS", [128, 2, 512])
    GU = z("GU", [128, 4, 256])
    LNG = z("LNG", [128, 512])
    LNB = z("LNB", [128, 512])
    BS = z("BS", [1, 4, 128])
    WST = z("WST", [128, 4, 128])
    COLS = z("COLS", [128, 12, 4])
    MN = z("MN", [128, 2, 512])
    KW = z("KW", [128, 2, 2, 128])
    CA = z("CA", [128, 2, 2, 130])
    T1 = z("T1", [128, 2, 130])
    DN = z("DN", [128, 4])
    QX = at("QX", [128, 4, 256], Z + 16384)
    PX = at("PX", [128, 2, 2, 256], Z + 28672)
    PTX = at("PTX", [128, 2, 256], Z + 32768)
    K1_AT = ZEND - 8192
    WF_AT = Z + 34816

    def extra(name, off, until, own=None):
        return Slot(at(name, [128, 2048], off)[:, :], None, "s_" + name, until, own)

    ONCE = U_MOE + 12
    k1_slot, f2_slot = extra("ek1", K1_AT, U_MOE + 6 * UNITS_PER_GROUP), extra("ef2", WF_AT + 8192, U_MOE + 28)
    WR_AT = WF_AT + 16384
    f1_slot = extra("ef1", WF_AT, U_MOE + 28)
    wr_slot = extra("ewr", WR_AT, U_MOE + 28)
    assert WR_AT + 8192 <= K1_AT - 8192
    zslots = [k1_slot, extra("egs", Z + 20480, ONCE), extra("ez", K1_AT - 8192, U_B2), f2_slot, f1_slot]
    xslots = [extra("ext", Z + 8192, ONCE, own=U_MOE + 6)]
    hslots = [extra("eha", HA_AT, U_MOE + 28), extra("ela", LA_AT, U_MOE + 28)]

    i0 = CON["ident"]
    x_tok = [load(X[:, 0, :], A["x"][0])]
    i_tok = load(CONS[:, i0:i0 + 128], A["con"][:, i0:i0 + 128])
    p_tok = load(PARS[:, :], A["par"])
    load_units(1)
    x_tok.append(load(X[:, 1, :], A["x"][1]))
    load_units(2)
    mem_tok = [load(MEM[:, t, :], A["mem"][t]) for t in range(2)]
    load_units(1)
    assert i0 == 0
    c_tok = load(CONS[:, 128:], A["con"][:, 128:])
    load_units(R - 4)
    ln_tok = [load(LNG[:, :], A["ln_g"].partition_broadcast(128)), load(LNB[:, :], A["ln_b"].partition_broadcast(128))]
    bs_tok = load(BS[:, :, :], A["b_s"])
    wst_tok = load(WST[:, :, :], A["w_sT"])

    table("natural_log_exp_and_others")
    sm0 = memset(DV, SM[:, :], 0.0)
    qpz = memset(PO, QP[:, :, :], 0.0)
    v1one = memset(PO, V1[:, :, :, 128:130], 1.0)
    onerow = memset(PO, ONEROW[:, :], 1.0)
    AC.wait(sm0)
    DV.wait(sm0)

    nA = Norm(X, "g_mix", HA, LA)
    tA = nA.tok
    s0 = [ms(0, 0, X[:, 0, 0:512], x_tok[0]), ms(0, 1, X[:, 0, 512:1024], x_tok[0], E=DV)]
    DV.wait(i_tok)
    AC.wait(p_tok)
    nA.a(0, s0)
    nA.b(0)
    DV.wait(p_tok)
    c0 = nA.c_steps(0)
    split_chunks(1)
    run(c0, 8)
    s1 = [ms(1, 0, X[:, 1, 0:512], x_tok[1]), ms(1, 1, X[:, 1, 512:1024], x_tok[1], E=DV)]
    split_chunks(2)
    run(c0)
    split_chunks(LAHEAD)
    nA.a(1, s1)
    v_tok = [None, None]

    def v_evac(t, bank, done):
        v_tok[t] = act(V1[:, t, :, 0:128], bank[:, :].rearrange("p (h d) -> p h d", h=4), ACT.Copy, done)
        return v_tok[t]

    def v_mid():
        nA.b(1)
        nA.c(1)

    n_tiles(HA, LA, tA, v_evac, {(0, 3): v_mid})

    g_in = [None] * 4

    def gate_evac(bank, done):
        for kind in range(4):
            dst = (IG if kind < 2 else FG)[:, kind % 2, :]
            g_in[kind] = act(dst, bank[32 * kind:32 * kind + 4, 0:256], ACT.Identity, done,
                             bias=par("gate_b", p=4, p0=32 * kind))
        return g_in[3]

    t_out(HA, LA, tA, gate_evac)
    for E in (PE, AC, DV, PO):
        E.wait(c_tok)

    def order(d, t):
        return slice(t * 128, t * 128 + 128) if d == 0 else slice(t * 128 + 127, (t * 128 - 1) if t else None, -1)

    def at_end(ap, d, t):
        i = t * 128 + (127 if d == 0 else 0)
        return ap[:, d, i:i + 1]

    gt = {}

    def scan(out, a, b, init, op0, op1, *d):
        return DV(lambda e: e.tensor_tensor_scan(out, a, b, init, op0, op1), *d)

    def rows():
        a = act(RT1[:, :, :], FG[:, :, :], ACT.Abs, g_in[3])
        a = act(RT1[:, :, :], RT1[:, :, :], ACT.Exp, a, scale=-1.0)
        a = act(RT1[:, :, :], RT1[:, :, :], ACT.Ln, a, bias=1.0)
        yield
        lf = stt(DV, FG[:, :, :], FG[:, :, :], 0.0, RT1[:, :, :], ALU.min, ALU.subtract, a)
        yield
        bt = []
        for d in range(2):
            for t in range(2):
                o_ = order(d, t)
                bt.append(scan(RT1[:, d, o_], ONEROW[:, :], FG[:, d, o_], 0.0, ALU.mult, ALU.add, lf, onerow))
            yield
        gt["u"] = u_t = tt(DV, IG[:, :, :], IG[:, :, :], RT1[:, :, :], ALU.subtract, bt)
        yield
        mA = []
        for d in range(2):
            o_ = order(d, d)
            mA.append(scan(FG[:, d, o_], IG[:, d, o_], IG[:, d, o_], -3e38, ALU.max, ALU.max, u_t))
        yield
        mp_t = [tt(DV, SM[0:4, 16 + d:17 + d], at_end(FG, d, d), at_end(RT1, d, d), ALU.add, mA[d]) for d in range(2)]
        yield
        for d in range(2):
            o_ = order(d, 1 - d)
            mB = scan(FG[:, d, o_], IG[:, d, o_], IG[:, d, o_], SM[0:4, 16 + d:17 + d], ALU.max, ALU.max, mp_t[d])
        yield
        gt["nc"] = nc_t = ts(DV, NC[:, :, :], FG[:, :, :], -1.0, None, ALU.mult, None, mB)
        bc_t = tt(DV, RT1[:, :, :], RT1[:, :, :], FG[:, :, :], ALU.add, mB)
        yield
        for d in range(2):
            ta, tb = slice(d * 128, d * 128 + 128), slice((1 - d) * 128, (1 - d) * 128 + 128)
            kw_t = act(KWR[:, d, :], IG[:, d, ta], ACT.Exp, nc_t, bias=at_end(NC, d, d))
            si_t = act(SI[:, d, :], NC[:, d, tb], ACT.Exp, nc_t, bias=SM[0:4, 16 + d:17 + d])
        em_t = act(RT1[:, :, :], RT1[:, :, :], ACT.Exp, bc_t, scale=-1.0)
        for _ in range(5):
            yield
        src = [(IG, 0, 0), (IG, 0, 1), (IG, 1, 0), (IG, 1, 1), (RT1, 0, 0), (RT1, 0, 1), (RT1, 1, 1), (RT1, 1, 0)]
        for i, (a, d, t) in enumerate(src):
            done = tr(P[7][:, 4 * i:4 * i + 4], a[:, d, t * 128:(t + 1) * 128], u_t, em_t, pfree[7], n=4)
        for i, a in enumerate((SI, SI, KWR, KWR)):
            done = tr(P[7][:, 32 + 4 * i:36 + 4 * i], a[:, i % 2, :], sig=(i == 3), n=4)
        gt["cols"] = pfree[7] = cp(DV, COLS[:, :, :], P[7][:, 0:48].rearrange("p (k h) -> p k h", h=4), done)

    nB = Norm(MEM, "g_mem", HB, LB)
    tB = nB.tok

    def mem_norm():
        s = [[ms(t, n, MEM[:, t, n * 512:(n + 1) * 512], mem_tok[t]) for n in range(2)] for t in range(2)]
        yield
        nB.a(0, s[0])
        nB.a(1, s[1])
        yield
        yield
        nB.b(0)
        yield
        c = nB.c_steps(0)
        run(c, 8)
        nB.b(1)
        yield
        run(c)
        yield
        c = nB.c_steps(1)
        run(c, 8)
        yield
        run(c)

    qk_tok = [None] * 8
    qk_act = [None] * 8
    conv_tok = [None, None]

    def qk_evac(i):
        def ev(bank, done):
            r = i % 2
            t0 = act(QP[:, r, 2:258], bank[:, 0:256], ACT.Copy, done, qpz, conv_tok[r])
            acc = QK[:, i, :]
            v = t1 = act(acc, bank[:, 0:256], ACT.Identity, done, bias=par("conv_b", i), scale=par("conv_w", 16 + i))
            for j in (0, 1, 3, 4):
                v = stt(DV, acc, QP[:, r, j:j + 256], par("conv_w", 8 * j + i), acc, ALU.mult, ALU.add, v, t0)
            conv_tok[r] = qk_tok[i] = v
            return t1
        return ev

    so_t = [None, None]

    def o_evac(t, bank, done):
        so_t[t] = act(SO[:, t, :], bank[:, :], ACT.Copy, done)
        return so_t[t]

    kx_t = [None] * 8

    def kx_evac(i):
        def ev(bank, done):
            kx_t[i] = act(KT[:, i, :], bank[:, 0:256], ACT.Copy, done)
            return kx_t[i]
        return ev

    behind.append(mem_norm())
    st["bg"] = 1
    os_ = n_out(HA, LA, tA, o_evac)
    for i in range(4):
        t_out(HA, LA, tA, qk_evac(i))
        os_[i]()
    bg_all()
    behind.append(rows())
    st["bg"] = 2
    for i in range(4):
        t_out(HA, LA, tA, qk_evac(4 + i))
        t_out(HB, LB, tB, kx_evac(i))
    bg_all()

    so = []

    def activations():
        table("silu_and_others")
        for i in (0, 4, 2, 6):
            qk_act[i] = qk_act[i + 1] = act(QK[:, i:i + 2, :], QK[:, i:i + 2, :], ACT.Silu, qk_tok[i], qk_tok[i + 1])
            if i == 4:
                yield
        yield
        table("sigmoid_and_others")
        so.append(act(SO[:, :, :], SO[:, :, :], ACT.Sigmoid, so_t))
        table("gelu_apprx_tanh_and_others")

    gelu_t = [None, None]

    def gv_evac(t, bank, done):
        gelu_t[t] = act(GV[:, t, :], bank[:, :], ACT.Gelu_apprx_tanh, done)
        return gelu_t[t]

    gu_t = [None] * 4

    def gu_evac(i):
        def ev(bank, done):
            gu_t[i] = act(GU[:, i, :], bank[:, 0:256], ACT.Gelu_apprx_tanh, done)
            return gu_t[i]
        return ev

    def layer_norm():
        ln_done = []
        for t in range(2):
            b0 = DV(lambda e, t=t: e.bn_stats(SM[:, 32 + 6 * t:38 + 6 * t], GV[:, t, :]), gelu_t[t])
            ln_done.append(DV(lambda e, t=t: e.bn_aggr(SM[:, 24 + 2 * t:26 + 2 * t], SM[:, 32 + 6 * t:38 + 6 * t]), b0))
        yield
        r = cp(DV, SM[:, 2:4], SM[:, 25:29:2], ln_done)
        while gu_t[3] is None:
            yield
        table("natural_log_exp_and_others")
        r = rstd_of(SM[:, 2:4], 2, 1.0, 1e-5, r)
        yield
        for t in range(2):
            a = ts(DV, GV[:, t, :], GV[:, t, :], SM[:, 24 + 2 * t:25 + 2 * t], SM[:, 2 + t:3 + t],
                   ALU.subtract, ALU.mult, r)
            a = tt(PO, GV[:, t, :], GV[:, t, :], LNG[:, :], ALU.mult, a, ln_tok[0])
            gv_t[t] = tt(PO, GV[:, t, :], GV[:, t, :], LNB[:, :], ALU.add, a, ln_tok[1])
            yield

    gv_t = [None, None]
    behind.append(activations())
    st["bg"] = 1
    for s in n_out(HA, LA, tA, gv_evac):
        s()
    bg_all()
    behind.append(layer_norm())
    for i in range(4):
        t_out(HA, LA, tA, gu_evac(i))
    hA_free = PE.last()
    st["bg"] = 0

    SC = 128 ** -0.5
    hd = [{} for _ in range(4)]
    cols_t, nc_t = gt["cols"], gt["nc"]

    def col(kind, h):
        return COLS[:, kind, h:h + 1]

    def m1_products(h):
        s = hd[h]
        for t in range(2):
            ta = slice(t * 128, (t + 1) * 128)
            mm(P[4][:, ta], QK[:, 4 + h, ta], QK[:, h, ta], True, True, qk_act[h], qk_act[4 + h], pfree[4])
        for d in range(2):
            s["s"] = tr(P[4][:, 256 + d * 128:384 + d * 128], QK[:, 4 + h, d * 128:(d + 1) * 128], sig=(d == 1))
        for d in range(2):
            s["bc"] = mm(P[5][:, d * 256:(d + 1) * 256], con("onehot", h * 128, h * 128 + 128, p=4), NC[:, d, :],
                         True, True, nc_t, pfree[5], sig=(d == 1))

    def m2_weights(h):
        s, r = hd[h], h % 2
        a = []
        for d in range(2):
            for t in range(2):
                c = d * 256 + t * 128
                a.append(stt(DV, MN[:, r, c:c + 128], P[5][:, c:c + 128], col(2 * d + t, h),
                             con("mf" if d == 0 else "mb"), ALU.add, ALU.min, s["bc"], cols_t,
                             hd[h - 2]["num"] if h >= 2 else None))
        pfree[5] = a[3]
        x_ = act(MN[:, r, :], MN[:, r, :], ACT.Exp, a[3])
        for d in range(2):
            k_ = ts(DV, KW[:, r, d, :], P[4][:, 256 + d * 128:384 + d * 128], col(10 + d, h), None, ALU.mult, None,
                    s["s"], hd[h - 2]["caug"] if h >= 2 else None)
        s["kw"] = k_
        for d in range(2):
            c = slice(d * 256, d * 256 + 256)
            s["p"] = stt(DV, MN[:, r, c], P[4][:, 0:256], SC, MN[:, r, c], ALU.mult, ALU.mult, x_)
        pfree[4] = s["p"]

    def v_aug(t, h):
        return V1[:, t, h, 0:129]

    def m3_numerators(h):
        s, r, b = hd[h], h % 2, stream_bank()
        for d in range(2):
            s["caug"] = mm(P[b][:, d * 130:d * 130 + 129], KW[:, r, d, :], v_aug(d, h), True, True,
                           s["kw"], pfree[b], v_tok[d], v1one, sig=(d == 1))
        for i, (d, t) in enumerate(((0, 0), (0, 1), (1, 1))):
            s["x"] = mm(P[6][:, i * 130:i * 130 + 129], MN[:, r, d * 256 + t * 128:d * 256 + t * 128 + 128], v_aug(t, h),
                        True, True, s["p"], pfree[6], sig=(i == 2))
        s["num"] = mm(P[7][:, 0:129], MN[:, r, 256:384], v_aug(0, h), True, True, pfree[7], sig=True)
        pfree[b] = s["ca"] = act(CA[:, r, :, 0:129], P[b][:, 0:260].rearrange("p (d c) -> p d c", d=2)[:, :, 0:129],
                                 ACT.Copy, s["caug"], hd[h - 2]["int"] if h >= 2 else None, scale=SC)

    def m4_inter(h):
        s, r = hd[h], h % 2
        for d in range(2):
            tb = slice((1 - d) * 128, (1 - d) * 128 + 128)
            s["int"] = mm(P[7][:, 130 + d * 130:259 + d * 130], QK[:, h, tb], CA[:, r, d, 0:129], True, True, s["ca"],
                          sig=(d == 1))
        for d in range(2):
            a = act(T1[:, d, 0:129], P[7][:, 130 + d * 130:259 + d * 130], ACT.Copy, s["int"],
                    hd[h - 1]["out"] if h else None, scale=col(8 + d, h))
        b = act(DN[:, 0:3], P[6][:, 128:389:130], ACT.Abs, s["x"], hd[h - 1]["out"] if h else None)
        s["a"], s["b"] = a, b

    def m5_out(h):
        s = hd[h]
        f1 = tt(DV, T1[:, 0, 0:129], P[6][:, 130:259], T1[:, 0, 0:129], ALU.add, s["a"], s["b"])
        b0 = tt(DV, T1[:, 1, 0:129], P[7][:, 0:129], T1[:, 1, 0:129], ALU.add)
        pfree[7] = b0
        dn = stt(DV, DN[:, 1:4:2], T1[:, :, 128], -1.0, T1[:, :, 128], ALU.mult, ALU.max, b0)
        dn = tt(DV, DN[:, :], DN[:, :], COLS[:, 4:8, h], ALU.max, dn)
        dn = DV(lambda e: e.reciprocal(DN[:, :], DN[:, :]), dn)
        hs = [HS[:, t, h * 128:(h + 1) * 128] for t in range(2)]
        w = [gv_free[0], dn]
        a0 = ts(DV, hs[0], P[6][:, 0:128], DN[:, 0:1], None, ALU.mult, None, *w)
        a1 = ts(DV, hs[1], P[6][:, 260:388], DN[:, 2:3], None, ALU.mult, None)
        pfree[6] = a1
        a0 = stt(DV, hs[0], T1[:, 1, 0:128], DN[:, 3:4], hs[0], ALU.mult, ALU.add, a0)
        a1 = stt(DV, hs[1], T1[:, 0, 0:128], DN[:, 1:2], hs[1], ALU.mult, ALU.add, a1)
        s["out"] = a1
        for t in range(2):
            i = jnk[0] % 2
            jnk[0] += 1
            jnk[1][i] = s["ss"] = act(JNK[:, i, 0:128], hs[t], ACT.Square, a1, jnk[1][i],
                                      accum=SM[:, 4 + h * 2 + t:5 + h * 2 + t])

    ya = [[None] * 2 for _ in range(8)]

    def y_norm(p):
        r = rstd_of(SM[:, 4 + 4 * p:8 + 4 * p], 4, 1.0 / 128, EPS, hd[2 * p + 1]["ss"])
        for h in (2 * p, 2 * p + 1):
            for t in range(2):
                v = HS[:, t, h * 128:(h + 1) * 128]
                y_t = stt(DV, v, v, SM[:, 4 + h * 2 + t:5 + h * 2 + t], SO[:, t, h * 128:(h + 1) * 128],
                          ALU.mult, ALU.mult, r, so)
        hd[2 * p]["y"] = y_t

    def y_out(p):
        b = stream_bank()
        for h in (2 * p, 2 * p + 1):
            for t in range(2):
                v = HS[:, t, h * 128:(h + 1) * 128]
                done = tr(P[b][:, (h % 2) * 256 + t * 128:(h % 2) * 256 + t * 128 + 128], v, hd[2 * p]["y"], pfree[b],
                          sig=(t == 1))
        for q in (2 * p, 2 * p + 1):
            ya[q][0] = act(HA[:, q, :], P[b][:, (q % 2) * 256:(q % 2) * 256 + 256], ACT.Copy, done, hA_free,
                           scale=par("g_head", q))
        for q in (2 * p, 2 * p + 1):
            pfree[b] = ya[q][1] = stt(DV, LA[:, q, :], P[b][:, (q % 2) * 256:(q % 2) * 256 + 256], par("g_head", q),
                                      f(HA[:, q, :]), ALU.mult, ALU.subtract, ya[2 * p + 1][0])

    def spatial(half):
        b = stream_bank()
        for g in (2 * half, 2 * half + 1):
            for c in range(2):
                out = P[b][:, (g % 2) * 256 + c * 128:(g % 2) * 256 + c * 128 + 128]
                mm(out, GV[:, c, g * 128:(g + 1) * 128], WST[:, g, :], True, False, gv_t[c], wst_tok, pfree[b])
                done = mm(out, con("ones", p=1), BS[:, g, :], False, True, bs_tok, sig=True)
        gv_free[0] = done
        sp = []
        for g in (2 * half, 2 * half + 1):
            v = pfree[b] = tt(DV, GU[:, g, :], P[b][:, (g % 2) * 256:(g % 2) * 256 + 256], GU[:, g, :], ALU.mult, done, gu_t[g])
            sp.append(v)
        for g in (2 * half, 2 * half + 1):
            a = act(HA[:, 4 + g, :], GU[:, g, :], ACT.Copy, sp[g % 2], hA_free)
            ya[4 + g] = [a, tt(DV, LA[:, 4 + g, :], GU[:, g, :], f(HA[:, 4 + g, :]), ALU.subtract, a)]

    gv_free = [None]
    vx_t = [None] * 4

    def vx_evac(h):
        def ev(t, bank, done):
            vx_t[2 * h + t] = act(VN[:, t, h * 512:(h + 1) * 512], bank[:, :], ACT.Copy, done)
            return vx_t[2 * h + t]
        return ev

    def residual(half, x_t, nrm):
        def ev(t, bank, done):
            v = X[:, t, half * 512:(half + 1) * 512]
            a = tt(DV, v, bank[:, :], v, ALU.add, done)
            x_t[2 * t + half] = ms(t, half, v, a)
            if half == 1:
                nrm.a(t, x_t[2 * t:2 * t + 2])
            return a
        return ev

    x1 = [None] * 4
    nQ = Norm(X, "g_xattn", HA, LA)
    tY = lambda k, t: ya[k]
    WO = (2, 3, 0, 1)
    for i in range(4, 6):
        todo.append(lambda i=i: t_out(HB, LB, tB, kx_evac(i)))
    todo.extend(n_out(HB, LB, tB, vx_evac(0)))
    todo.extend(n_out(HB, LB, tB, vx_evac(1)))
    todo.extend(n_out(HA, LA, tY, residual(0, x1, nQ), pairs=WO))
    m1_products(0)
    m2_weights(0)
    bg_all()
    fill(1)
    m1_products(1)
    m2_weights(1)
    m3_numerators(0)
    fill(1)
    m1_products(2)
    spatial(0)
    m4_inter(0)
    m5_out(0)
    spatial(1)
    m2_weights(2)
    fill(1)
    m3_numerators(1)
    fill(1)
    m1_products(3)
    m4_inter(1)
    m5_out(1)
    m2_weights(3)
    fill(1)
    m3_numerators(2)
    fill(1)
    m4_inter(2)
    m5_out(2)
    y_norm(0)
    fill(1)
    m3_numerators(3)
    fill(1)
    y_out(0)
    m4_inter(3)
    m5_out(3)
    y_norm(1)
    fill(4)
    y_out(1)
    while todo:
        fill(1)

    t0_done = [None]

    def r1(t, bank, done, ev=residual(1, x1, nQ)):
        if t == 0:
            t0_done[0] = done
        v = ev(t, bank, done)
        if t == 1:
            nQ.c(0, t0_done[0])
        return v

    n_tiles(HA, LA, tY, r1, {(1, 3): lambda: nQ.b(0)}, pairs=WO)
    wo_done = PE.last()
    prev = now()
    z = Region(Z, K1_AT - 8192)
    XT_AT = z.o
    XT = z("XT", [128, 2, 8, 256])
    SWT = z("SWT", [128, 2, 2, 256])
    GS_AT = z.o
    GS = z("GS", [128, 512])
    HT = z("HT", [128, 4, 128])
    YS = z("YS", [128, 1024])
    SS = z("SS", [128, 2, 256], F32R)
    SW = z("SW", [128, 2, 256])
    RS = z("RS", [128, 7, 64])
    MB = z("MB", [128, 2, 32], BF16)
    assert z.o <= WF_AT
    z.o = WF_AT
    GF2 = z("GF2", [128, 1024], keep=False)
    HF = z("HF", [128, 2, 2, 512])
    HBI = z("HBI", [1, 512])
    XTMP = z("XTMP", [128, 512])
    W3 = z("W3", [64, 1024])
    assert z.o == WR_AT
    ZP = z("ZP", [33, 256])
    W1 = z("W1", [33, 64])
    W2 = z("W2", [64, 64])
    FA = z("FA", [64, 256])
    FB = z("FB", [64, 256])
    GR = z("GR", [1, 1024])
    zr = Region(WR_AT, z.end)
    WR = zr("WR", [128, 8, 36])
    WRH = zr("WRH", [128, 8, 36], F32R)
    WRL = zr("WRL", [128, 8, 36], F32R)
    LGT = zr("LGT", [36, 256])
    LG = zr("LG", [128, 2, 36])
    BRB = zr("BRB", [128, 36])
    BRD = zr("BRD", [36, 36])
    LTB = zr("LTB", [128, 128], BF16)
    ONB = zr("ONB", [128, 128], BF16)
    wr_t = load(WR[:, :, :], A["wr"], prev)
    vacant.extend((s_, prev) for s_ in zslots)
    load_units()

    g_, g1 = (PARS[:, PAR[n]:PAR[n] + 8] for n in ("gfin", "mix_pre0"))
    tt(DV, g_, g_, g1, ALU.mult, p_tok)
    t_out(HB, LB, tB, kx_evac(6))
    nQ.b(1)
    brd = ts(DV, BRD[:, :], con("ident", 0, 36, p=36), par("br", p=36), None, ALU.mult, None, prev)
    nQ.c(1, wo_done)
    t_out(HB, LB, tB, kx_evac(7))
    bk = stream_bank()
    brd = mm(P[bk][:, 0:36], con("ones", p=36), BRD[:, :], True, True, brd, pfree[bk], sig=True)
    brb = pfree[bk] = cp(DV, BRB[:, :], P[bk][:, 0:36], brd)
    q_t = [None] * 8
    hB_free = PE.last()

    def qx_evac(i):
        def ev(bank, done):
            q_t[i] = act(QX[:, i % 4, :], bank[:, 0:256], ACT.Copy, done, prev, xa[i // 2 - 2].get("s") if i > 3 else None)
            return q_t[i]
        return ev

    XS = 256 ** -0.5
    xa = [{} for _ in range(4)]
    yx = [None] * 8

    def a1_scores(h):
        s, b = xa[h], 4 + h % 2
        for t in range(2):
            for k in range(2):
                s["s"] = mm(P[b][:, t * 256:(t + 1) * 256], QX[:, (2 * h + k) % 4, t * 128:(t + 1) * 128], KT[:, 2 * h + k, :],
                            k == 0, k == 1, q_t[2 * h + k], kx_t[2 * h + k], pfree[b], sig=(t == 1 and k == 1))

    def a2_softmax(h):
        s, b, r = xa[h], 4 + h % 2, h % 2
        sm = SM[:, 160 + 8 * r:168 + 8 * r]
        m = DV(lambda e: e.tensor_reduce(sm[:, 0:2], P[b][:, :].rearrange("p (t m) -> p t m", t=2), AX.X, ALU.max),
               s["s"], xa[h - 2]["p"] if h >= 2 else None)
        m = ts(DV, sm[:, 2:4], sm[:, 0:2], -XS, None, ALU.mult, None, m)
        for t in range(2):
            e_ = act(PX[:, r, t, :], P[b][:, t * 256:(t + 1) * 256], ACT.Exp, m,
                     xa[h - 2]["tr"] if h >= 2 else prev, bias=sm[:, 2 + t:3 + t], scale=XS, accum=sm[:, 4 + t:5 + t])
        pfree[b] = e_
        m = DV(lambda e: e.reciprocal(sm[:, 6:8], sm[:, 4:6]), e_)
        for t in range(2):
            s["p"] = ts(DV, PX[:, r, t, :], PX[:, r, t, :], sm[:, 6 + t:7 + t], None, ALU.mult, None, m)

    def a3_transpose(h):
        s, r = xa[h], h % 2
        for m in range(2):
            for t in range(2):
                s["tr"] = tr(P[6][:, m * 256 + t * 128:m * 256 + t * 128 + 128], PX[:, r, t, m * 128:(m + 1) * 128],
                             s["p"], pfree[6], sig=(m == 1 and t == 1))
        pfree[6] = s["pt"] = cp(DV, PTX[:, :, :], P[6][:, :].rearrange("p (m t) -> p m t", m=2), s["tr"],
                                xa[h - 1]["o"] if h else prev)

    def a4_out(h):
        s, r = xa[h], h % 2
        for k in range(2):
            for m in range(2):
                s["o"] = mm(P[7][:, k * 256:(k + 1) * 256], VN[:, m, h * 256 + k * 128:h * 256 + k * 128 + 128],
                            PTX[:, m, :], m == 0, m == 1, s["pt"], vx_t, pfree[7], sig=(k == 1 and m == 1))
        a = [act(HB[:, 2 * h + k, :], P[7][:, k * 256:(k + 1) * 256], ACT.Copy, s["o"], hB_free) for k in range(2)]
        for k in range(2):
            l = tt(DV, LB[:, 2 * h + k, :], P[7][:, k * 256:(k + 1) * 256], f(HB[:, 2 * h + k, :]), ALU.subtract, a[1])
            yx[2 * h + k] = [a[k], l]
        pfree[7] = l

    t_out(HA, LA, nQ.tok, qx_evac(0))
    t_out(HA, LA, nQ.tok, qx_evac(1))
    for h in range(4):
        a1_scores(h)
        a2_softmax(h)
        if h:
            a4_out(h - 1)
        if h < 3:
            t_out(HA, LA, nQ.tok, qx_evac(2 * h + 2))
            a3_transpose(h)
            t_out(HA, LA, nQ.tok, qx_evac(2 * h + 3))
    vacant.extend((s_, PE.last()) for s_ in hslots)
    load_units()
    wrh = act(WRH[:, :, :], WR[:, :, :], ACT.Copy, wr_t)
    wrl = tt(DV, WRL[:, :, :], WR[:, :, :], f(WRH[:, :, :]), ALU.subtract, wrh)
    ltb = act(LTB[:, :], con("lt"), ACT.Copy, prev)
    onb = act(ONB[:, :], con("ones"), ACT.Copy)
    x2 = [None] * 4
    tX = lambda k, t: yx[k]
    steps = n_out(HB, LB, tX, residual(0, x2, None))
    steps[0]()
    a3_transpose(3)
    steps[1]()
    a4_out(3)
    vacant.extend((s_, [PE.last(), DV.last(), AC.last()]) for s_ in xslots)
    load_units()
    steps[2]()
    steps[3]()
    attn_done = now()

    NHI = at("NHI", [128, 2, 1024], HB_AT, F32R)
    NLO = at("NLO", [128, 2, 1024], LB_AT, F32R)
    XN2 = at("XN2", [128, 2, 1024], WF_AT + 4096)
    H32 = at("H32", [128, 8, 256], XT_AT)
    WF = at("WF", [128, 4, 1024], WF_AT + 4096)
    assert WF_AT + 4096 + 16384 <= K1_AT - 8192
    GF = at("GF", [128, 2, 512], GS_AT)
    HTF = at("HTF", [128, 4, 256], GS_AT + 4096)
    CAP = 64

    nh, nl = [None, None], [None, None]
    rc, xa_t = [None, None], [None, None]
    C_ = [SM[:, 12 + t:13 + t] for t in range(2)]
    RXH = at("RXH", [128, 4, 256], Z + 16384, F32R)
    RXL = at("RXL", [128, 4, 256], Z + 28672, F32R)
    XN = at("XN", [128, 1024], Z + 28672)
    RUH = at("RUH", [128, 4, 256], Z, F32R)
    RUL = at("RUL", [128, 4, 256], Z + 4096, F32R)
    rx = {}

    def scale_of(t):
        r, v = yield from rstd_steps(t, x2[2 * t:2 * t + 2])
        yield
        rc[t] = ts(DV, C_[t], r, -0.5, None, ALU.mult, None, v)

    def lower_half():
        for i in range(2):
            bk = 4 + i
            for q in range(2):
                for t in range(2):
                    k = 2 * i + q
                    d = tr(P[bk][:, q * 256 + t * 128:q * 256 + t * 128 + 128], X[:, t, k * 128:(k + 1) * 128],
                           x2[0], x2[2], pfree[bk], sig=(q == 1 and t == 1))
            for q in range(2):
                k = 2 * i + q
                h = act(RXH[:, k, :], P[bk][:, q * 256:(q + 1) * 256], ACT.Copy, d, attn_done, scale=par("g_moe", k))
            for q in range(2):
                k = 2 * i + q
                rx[k] = pfree[bk] = stt(DV, RXL[:, k, :], P[bk][:, q * 256:(q + 1) * 256], par("g_moe", k),
                                        f(RXH[:, k, :]), ALU.mult, ALU.subtract, h)

    def upper_half(t):
        ta = slice(t * 128, (t + 1) * 128)
        bks = (6 - 2 * t, 7 - 2 * t)
        for i in range(2):
            for q in range(2):
                k = 4 + 2 * i + q
                d = tr(P[bks[i]][:, q * 128:(q + 1) * 128], X[:, t, k * 128:(k + 1) * 128], xa_t[t], pfree[bks[i]], sig=True)
        yield
        h = {}
        for i in range(2):
            for q in range(2):
                k = 4 + 2 * i + q
                h[i] = act(RUH[:, k - 4, ta], P[bks[i]][:, q * 128:(q + 1) * 128], ACT.Copy, d, attn_done, scale=par("g_moe", k))
                yield
        for i in range(2):
            for q in range(2):
                k = 4 + 2 * i + q
                rx[k, t] = pfree[bks[i]] = stt(DV, RUL[:, k - 4, ta], P[bks[i]][:, q * 128:(q + 1) * 128], par("g_moe", k),
                                               f(RUH[:, k - 4, ta]), ALU.mult, ALU.subtract, h[i])
                yield

    def r2(t, bank, done):
        v = X[:, t, 512:1024]
        a = xa_t[t] = tt(DV, v, bank[:, :], v, ALU.add, done)
        x2[2 * t + 1] = ms(t, 1, v, a)
        if t == 0:
            run(scale_of(0))
        return a

    def ox_mid():
        lower_half()
        free = [his.pop(0)[1], his.pop(0)[1]]
        assert not his
        vacant.append((wslots[0], free))
        load_units()

    def own_parts(t):
        nh[t] = act(NHI[:, t, :], X[:, t, :], ACT.Copy, rc[t], ox_done, scale=C_[t])
        if t == 0:
            nl[t] = stt(DV, NLO[:, t, :], X[:, t, :], C_[t], f(NHI[:, t, :]), ALU.mult, ALU.subtract, nh[t])
        else:
            xn = tt(PO, XN[:, :], X[:, t, :], C_[t].broadcast_to([128, 1024]), ALU.mult, rc[t], lower_done)
            nl[t] = tt(PO, NLO[:, t, :], XN[:, :], f(NHI[:, t, :]), ALU.subtract, nh[t], xn)

    wslots = [extra(f"ew{i}", WH_AT + 8192 * i, U_B2) for i in range(NH // 2)]
    n_tiles(HB, LB, tX, r2, {(0, 3): ox_mid, (1, 2): lambda: run(upper_half(0))})
    ox_done = PE.last()
    vacant.extend((w_, ox_done) for w_ in wslots[1:])
    load_units()

    rb = stream_bank()
    assert rb != 1

    def logits(k, hi, lo, *d):
        out = P[rb][0:36, 0:256]
        mm(out, WRH[:, k, :], hi, k == 0, False, *d, wrl, pfree[rb])
        mm(out, WRL[:, k, :], hi, False, False)
        return mm(out, WRH[:, k, :], lo, False, k == 7, sig=(k % 4 == 3))

    for k in range(4):
        lower_done = logits(k, RXH[:, k, :], RXL[:, k, :], rx[k])
    up = upper_half(1)
    run(up, 1)
    weave(scale_of(1), up, ((1, 2), (1, 1), (1, 1), (0, 4)))
    own_parts(0)
    for k in range(4, 8):
        done = logits(k, RUH[:, k - 4, :], RUL[:, k - 4, :], rx[k, 0], rx[k, 1])
    lg = pfree[rb] = act(LGT[:, :], P[rb][0:36, 0:256], ACT.Copy, done)
    for t in range(2):
        done = tr(P[1][:, t * 36:(t + 1) * 36], LGT[:, t * 128:(t + 1) * 128], lg, pfree[1], n=36, sig=(t == 1))

    RT = at("RT", [128, 5, 64], Z + 16384)

    def rs(i, n=64, w=None):
        a = RS[:, i, 0:n] if i < 7 else RT[:, i - 7, 0:n]
        return a if w is None else a.rearrange("p (t c) -> p t c", t=2)

    def bc(ap, *shape):
        return ap.unsqueeze(len(ap.shape)).broadcast_to(list(shape))

    def red(out, a, op, *d):
        return DV(lambda e: e.tensor_reduce(out, a, AX.X, op), *d)

    def first_max(a, mx, ne, ix, oh, tmp, v):
        v = red(mx, a, ALU.max, v)
        yield
        v = tt(DV, ne, a, bc(mx, *a.shape), ALU.not_equal, v)
        yield
        shape = list(tmp.shape)
        io = con("iota", 0, shape[2]).unsqueeze(1).broadcast_to(shape)
        v = stt(DV, tmp, tmp, 100.0, io, ALU.mult, ALU.add, v)
        yield
        v = red(ix, tmp, ALU.min, v)
        yield
        return tt(DV, oh, io, bc(ix, *shape), ALU.is_equal, v)

    for t in range(2):
        lg_t = pfree[1] = stt(DV, LG[:, t, :], P[1][:, t * 36:(t + 1) * 36], C_[t], BRB[:, :], ALU.mult, ALU.add, done, rc, brb)
    own_parts(1)
    LGG, LGE = LG[:, :, 0:4], LG[:, :, 4:36].rearrange("p t (g e) -> p t g e", g=4)
    g4 = lambda i: rs(i, 64).rearrange("p (t g e) -> p t g e", t=2, g=4)
    small = lambda i, o, n: rs(i, o + n)[:, o:o + n].rearrange("p (t c) -> p t c", t=2)
    g8 = lambda i: rs(i, 64).rearrange("p (r e) -> p r e", e=8)
    g32 = lambda i: rs(i, 64, 1)
    gm, gx = rs(0, 2), rs(0, 4)[:, 2:4]
    max1, max2, ohg, tmg, tm = (small(4, 8 * i, 8) for i in range(5))
    eix = rs(4, 48)[:, 40:48]
    all4 = (128, 2, 4, 8)
    ends = {}

    OH1, NE, OH2, ONE, TWO = range(7, 12)

    def best_group():
        v = ends["ohg"] = yield from first_max(LGG, gm, tm, gx, ohg, tm, lg_t)
        yield
        v = tt(DV, tmg, LGG, bc(gm, 128, 2, 4), ALU.subtract)
        ends["tg"] = act(tmg, tmg, ACT.Exp, v)

    def best_experts():
        v = yield from first_max(LGE, max1, g4(NE), eix, g8(OH1), g8(NE), lg_t)
        yield
        oh1 = v
        v = stt(DV, g32(5), g32(OH1), -3e38, LG[:, :, 4:36], ALU.mult, ALU.add, v)
        yield
        ends["one"] = tt(DV, g4(ONE), bc(ohg, *all4), g4(OH1), ALU.mult, oh1, ends["ohg"])
        ends["oh"] = yield from first_max(g8(5), max2.rearrange("p t g -> p (t g)"), g8(NE), eix, g8(OH2), g8(NE), v)

    alternate(best_group(), best_experts())
    tg = ends["tg"]
    v = tt(DV, g4(TWO), bc(ohg, *all4), g4(OH2), ALU.mult, ends["oh"], ends["ohg"])
    one, two = g32(ONE), g32(TWO)
    W_, POS, WOV = g32(5), g32(1), g32(2)
    m_t = v = tt(DV, MB[:, :, :], one, two, ALU.add, v, ends["one"], ox_done)
    mm(P[1][:, 128:160], LTB[:, :], MB[:, 0, :], True, True, m_t, ltb, onb, pfree[1])
    mm(P[1][:, 160:192], LTB[:, :], MB[:, 1, :], True, False)
    mm(P[1][:, 160:192], ONB[:, :], MB[:, 0, :], False, True)
    mm(P[1][:, 192:224], ONB[:, :], MB[:, 0, :], True, False)
    done = mm(P[1][:, 192:224], ONB[:, :], MB[:, 1, :], False, True, sig=True)
    v = ts(DV, POS, MB[:, :, :], 1000.0, -1000.0, ALU.mult, ALU.add, v)
    v = tt(DV, POS, P[1][:, 128:192].rearrange("p (t c) -> p t c", t=2), POS, ALU.add, v, done)
    pos_t = v
    vacant.append((wr_slot, [done, v]))
    load_units()
    w_t = []

    def weights():
        pt, qd, w1, w2 = rs(3, 2), rs(3, 4)[:, 2:4], rs(3, 6)[:, 4:6], rs(3, 8)[:, 6:8]
        u = tt(DV, tm, max2, max1, ALU.subtract)
        u = tt(DV, tm, tm, ohg, ALU.mult, u)
        u = red(qd, tm, ALU.add, u)
        u = act(qd, qd, ACT.Exp, u)
        p_ = red(pt, tmg, ALU.add, tg)
        p_ = DV(lambda e: e.reciprocal(pt, pt), p_)
        u = ts(DV, w1, qd, 1.0, None, ALU.add, None, u)
        u = DV(lambda e: e.reciprocal(w1, w1), u)
        u = tt(DV, w1, w1, pt, ALU.mult, u, p_)
        u = tt(DV, w2, w1, qd, ALU.mult, u)
        for t in range(2):
            u = ts(DV, W_[:, t, :], one[:, t, :], w1[:, t:t + 1], None, ALU.mult, None, u)
            u = stt(DV, W_[:, t, :], two[:, t, :], w2[:, t:t + 1], W_[:, t, :], ALU.mult, ALU.add, u)
        w_t.append(stt(DV, WOV, POS, float(CAP), W_, ALU.is_ge, ALU.mult, u, pos_t))

    engines = (PE, AC, DV, PO, SP)
    fsem = [sem(f"s_f{n}") for n in range(6)]

    def general_path():
        fd = [0]
        entry = now()
        held = [(E.sem, E.n, E.q, E.seen) for E in engines]
        for E, s in zip(engines, fsem):
            E.sem, E.n, E.q, E.seen = s, 0, [], dict(E.seen)
            E.wait(entry)

        def fload(out, src, *d):
            SP.wait(*d)
            fd[0] += 16
            SP.q.append(lambda e: e.dma_start(out, src).then_inc(fsem[5], 16))
            return (fsem[5], fd[0])

        assert all(s_.freed for s_ in (f1_slot, f2_slot))
        for t in range(2):
            x_ = tt(DV, XN2[:, t, :], f(NHI[:, t, :]), f(NLO[:, t, :]), ALU.add)
        for k in range(8):
            for t in range(2):
                d = tr(P[k // 2][:, (k % 2) * 256 + t * 128:(k % 2) * 256 + t * 128 + 128], XN2[:, t, k * 128:(k + 1) * 128],
                       x_, sig=(t == 1))
        for k in range(8):
            h_t = act(H32[:, k, :], P[k // 2][:, (k % 2) * 256:(k % 2) * 256 + 256], ACT.Copy, d, scale=par("g_moe", k))
        free = h_t
        y_t = None
        for ex in range(32):
            u = U_MOE + (ex // 2) * UNITS_PER_GROUP
            parts = A["ws"][u:u + 12].rearrange("k p (e c) -> p k e c", e=2)[:, :, ex % 2, :]
            for m in range(2):
                w_t = fload(WF[:, :, :], parts[:, 4 * m:4 * m + 4, :], free)
                for t in range(2):
                    for k in range(8):
                        free = mm(P[2 * m + t][:, :], H32[:, k, t * 128:(t + 1) * 128],
                                  WF[:, k // 2, (k % 2) * 512:(k % 2) * 512 + 512], k == 0, k == 7,
                                  w_t, h_t, y_t, sig=(k == 7))
            g_t = [act(GF[:, t, :], P[t][:, :], ACT.Silu, free, y_t) for t in range(2)]
            hh = [tt(DV, GF[:, t, :], P[2 + t][:, :], GF[:, t, :], ALU.mult, g_t[t]) for t in range(2)]
            for k in range(4):
                for t in range(2):
                    d = tr(P[4 + k // 2][:, (k % 2) * 256 + t * 128:(k % 2) * 256 + t * 128 + 128],
                           GF[:, t, k * 128:(k + 1) * 128], hh, y_t, sig=(k == 3 and t == 1))
            for i in range(2):
                ht = cp(DV, HTF[:, 2 * i:2 * i + 2, :], P[4 + i][:, :].rearrange("p (k t) -> p k t", k=2), d)
            w_t = fload(WF[:, :, :], parts[:, 8:12, :], free)
            for t in range(2):
                for n in range(2):
                    for k in range(4):
                        free = mm(P[2 * t + n][:, :], HTF[:, k, t * 128:(t + 1) * 128],
                                  WF[:, k, n * 512:(n + 1) * 512], k == 0, k == 3, w_t, ht, sig=(k == 3))
            for t in range(2):
                for n in range(2):
                    v = X[:, t, n * 512:(n + 1) * 512]
                    y_t = stt(DV, v, P[2 * t + n][:, :], WOV[:, t, ex:ex + 1], v, ALU.mult, ALU.add, free)
        ends = [(E.sem, E.n) for E in engines if E.n]
        for E, (s_, n_, q_, seen_) in zip(engines, held):
            E.wait(ends)
            body = E.q
            E.sem, E.n, E.q, E.seen = s_, n_, q_, seen_
            E.wait(cnt_t)

            def branch(e, body=body):
                c = e.value_load(CNT[0:1, 0:1], min_val=0, max_val=512)
                with e.If(c > CAP):
                    for g in body:
                        g(e)
            E.q.append(branch)

    mbank = [0]

    def misc_bank():
        mbank[0] += 1
        return 4 + mbank[0] % 4

    ex_st = {"ht": None}
    grp = [{} for _ in range(GROUPS + 1)]
    four = [{} for _ in range(GROUPS // 2)]

    def prepare(G):
        s, r = four[G], G % 2
        back, back2 = (four[G - 1] if G else {}), (four[G - 2] if G >= 2 else {})
        e_ = slice(4 * G, 4 * G + 4)
        a = [tt(DV, SS[:, t, :].rearrange("p (e c) -> p e c", e=4), con("iota").unsqueeze(1).broadcast_to([128, 4, 64]),
                bc(POS[:, t, e_], 128, 4, 64), ALU.is_equal, pos_t, back.get("xt_mm"), back.get("ss"), nl) for t in range(2)]
        yield
        for q in range(4):
            bk = misc_bank()
            for k in (2 * q, 2 * q + 1):
                out = P[bk][:, (k % 2) * 256:(k % 2) * 256 + 256]
                kc = slice(k * 128, (k + 1) * 128)
                for t in range(2):
                    mm(out, NHI[:, t, kc], SS[:, t, :], t == 0, False, a[t], nh, pfree[bk])
                    s["xt_mm"] = mm(out, NLO[:, t, kc], SS[:, t, :], False, t == 1, nl, sig=(k % 2 == 1 and t == 1))
            s["xt", q] = tt(DV, XT[:, r, 2 * q:2 * q + 2, :], P[bk][:, :].rearrange("p (k s) -> p k s", k=2),
                         bc(PARS[:, PAR["g_moe"] + 2 * q:PAR["g_moe"] + 2 * q + 2], 128, 2, 256),
                         ALU.mult, s["xt_mm"], back2.get("up"), xslots[0].freed if r else None)
            pfree[bk] = s["xt", q]
            yield
        b = s["ss"] = tt(DV, SW[:, :, :].rearrange("p t (e c) -> p t e c", e=4),
                         f(SS[:, :, :]).rearrange("p t (e c) -> p t e c", e=4), bc(W_[:, :, e_], 128, 2, 4, 64),
                         ALU.mult, back.get("sw_mm"), w_t, a)
        yield
        for p in range(2):
            bk = misc_bank()
            for t in range(2):
                s["sw_mm"] = tr(P[bk][:, t * 128:(t + 1) * 128], SW[:, t, p * 128:(p + 1) * 128], b, pfree[bk],
                                sig=(t == 1))
            pfree[bk] = s["swt"] = act(SWT[:, r, p, :], P[bk][:, 0:256], ACT.Copy, s["sw_mm"], back2.get("comb"))
            yield

    preps = []

    def prep(n=1):
        while preps and n:
            try:
                next(preps[0])
                n -= 1
            except StopIteration:
                preps.pop(0)

    unit = [U_MOE]

    def in_products(g, bank, name):
        G, r, p = four[g // 2], (g // 2) % 2, g % 2
        for kp in range(4):
            u = unit[0]
            unit[0] += 1
            w, wt = units[u][0].raw, units[u][1]
            for q in range(2):
                k = 2 * kp + q
                for e_ in range(2):
                    c = p * 128 + e_ * 64
                    done = mm(P[bank][e_ * 64:(e_ + 1) * 64, :], XT[:, r, k, c:c + 64],
                              w[:, e_ * 1024 + q * 512:e_ * 1024 + q * 512 + 512], k == 0, k == 7,
                              wt, G["xt", kp], pfree[bank], sig=(q == 1 and e_ == 1))
            free_unit(u, done)
            if kp % 2 or g == 0:
                if g == 0 and name == "gate" and kp == 3:
                    continue
                prep()
            else:
                bg()
            if g == 0 and name == "gate" and kp == 1:
                weights()
                table("silu_and_others")
        grp[g][name] = G[name] = done

    def hidden(g):
        s = grp[g]
        a = pfree[0] = act(GS[:, :], P[0][:, :], ACT.Silu, s["gate"], ex_st["ht"])
        a = pfree[1] = tt(DV, GS[:, :], P[1][:, :], GS[:, :], ALU.mult, a, s["up"])
        if g == 0:
            prep(2)
        elif g < GROUPS - 1:
            combine(g - 1)
        bk = misc_bank()
        for k in range(4):
            d = tr(P[bk][:, k * 128:(k + 1) * 128], GS[:, k * 128:(k + 1) * 128], a, pfree[bk], sig=(k == 3))
        ex_st["ht"] = d
        pfree[bk] = s["ht"] = act(HT[:, :, :], P[bk][:, :].rearrange("p (k s) -> p k s", k=4), ACT.Copy, d,
                                  grp[g - 1].get("down"))

    def down(g):
        s = grp[g]
        prep()
        for k in range(4):
            u = unit[0]
            unit[0] += 1
            w, wt = units[u][0].raw, units[u][1]
            for n in range(2):
                for e_ in range(2):
                    done = mm(P[2 + n][e_ * 64:(e_ + 1) * 64, :], HT[:, k, e_ * 64:(e_ + 1) * 64],
                              w[:, e_ * 1024 + n * 512:e_ * 1024 + n * 512 + 512], k == 0, k == 3,
                              wt, s["ht"], pfree[2 + n], sig=(n == 1 and e_ == 1))
            free_unit(u, done)
            if k % 2:
                bg()
        s["down"] = done
        s["y"] = [act(YS[:, 0:512], P[2][:, :], ACT.Copy, done, grp[g - 1].get("comb")),
                  cp(DV, YS[:, 512:1024], P[3][:, :], done, grp[g - 1].get("comb"))]
        pfree[2], pfree[3] = s["y"]

    def combine(g, after=None):
        s, r = grp[g], (g // 2) % 2
        for t in range(2):
            for n in range(2):
                bk = misc_bank()
                s["comb"] = mm(P[bk][:, :], SWT[:, r, g % 2, t * 128:(t + 1) * 128], YS[:, n * 512:(n + 1) * 512], True, True,
                               four[g // 2]["swt"], s["y"][n], pfree[bk], sig=True)
                v = X[:, t, n * 512:(n + 1) * 512]
                pfree[bk] = v = tt(DV, v, P[bk][:, :], v, ALU.add, s["comb"])
                if after:
                    after(t, n, v)
        four[g // 2]["comb"] = s["comb"]

    K0W = at("K0W", [128, 2, 2, 512], HA_AT)
    K0 = at("K0", [128, 2, 2, 512], HB_AT)
    z = Region(LA_AT, LA_AT + 8192)
    TF = z("TF", [128, 2, 2, 256])
    DEC = z("DEC", [128, 2, 512])
    K1 = at("K1", [128, 2, 2, 512], K1_AT)
    KS_ = (K0, K1)
    k_done = [None, None]
    MAGIC = 1.5 * 2.0 ** 23
    C1, C2 = 6.28125, float(np.float32(2 * np.pi - 6.28125))
    C3 = float(np.float32(2 * np.pi - 6.28125 - np.float64(np.float32(C2))))
    PI_LO = float(np.nextafter(np.float32(np.pi), np.float32(0)))
    fs = {}

    def filters():
        nl_done = nl[1]
        assert f1_slot.freed and f2_slot.freed and wr_slot.freed and hslots[1].freed
        prev = now()
        prev.append(hslots[1].freed)
        fs["tf"] = load(TF[:, :, :, :], A["dft"][:, 0:1024], prev)
        fs["dec"] = load(DEC[:, :, :], A["decay"], prev)
        gf = load(GR[:, :], A["g_final"].unsqueeze(0), prev)
        fs["zp"] = load(ZP[:, :], A["zpos"], prev)
        for l in range(2):
            w = prev if l == 0 else fs["end"]
            fs["w1"] = load(W1[:, :], A["hw1"][l], w)
            fs["w2"] = load(W2[:, :], A["hw2"][l], w)
            fs["w3"] = load(W3[:, :], A["hw3"][l], w)
            fs["bias"] = load(HBI[:, :], A["hbias"][l].unsqueeze(0), w)
            for _ in range(12 if l else 4):
                yield
            hp = lambda i: PARS[0:64, PAR[f"hf{l}"] + i:PAR[f"hf{l}"] + i + 1]
            bk = misc_bank()
            d = mm(P[bk][0:64, 0:256], W1[:, :], ZP[:, :], True, True, fs["w1"], fs["zp"], pfree[bk], sig=True)
            yield from sine(bk, hp(0), hp(1), d)
            yield
            bk = misc_bank()
            d = mm(P[bk][0:64, 0:256], W2[:, :], FA[:, :], True, True, fs["w2"], fs["sin"], pfree[bk], sig=True)
            yield from sine(bk, hp(2), hp(3), d)
            yield
            for t in range(2):
                for n in range(2):
                    bk = misc_bank()
                    d = mm(P[bk][:, :], FA[:, t * 128:(t + 1) * 128], W3[:, n * 512:(n + 1) * 512], True, True,
                           fs["sin"], fs["w3"], pfree[bk], sig=True)
                    a = tt(DV, HF[:, n, t, :], P[bk][:, :], DEC[:, t, :], ALU.mult, d, fs["dec"])
                    pfree[bk] = a
                    yield
            z0 = memset(DV, HF[0:1, 1, 0, :], 0.0, a)
            for t in range(2):
                c = tt(DV, XTMP[:, :], HF[:, 0, t, :], HF[:, 1, t, :], ALU.add, z0, fs.get("c"))
                b_ = tt(DV, HF[:, 1, t, :], HF[:, 0, t, :], HF[:, 1, t, :], ALU.subtract, z0)
                fs["c"] = cp(DV, HF[:, 0, t, :], XTMP[:, :], c, b_)
                yield
            dst = K1 if l else K0W
            for kind in range(2):
                for m in range(2):
                    bk = misc_bank()
                    for t in range(2):
                        d = mm(P[bk][:, :], TF[:, kind, t, m * 128:(m + 1) * 128], HF[:, kind, t, :], t == 0,
                               t == 1 and kind == 1, fs["c"], fs["tf"], pfree[bk], sig=(t == 1))
                    if kind == 0:
                        d = mm(P[bk][:, :], con("ones", p=1), HBI[:, :], False, True, fs["bias"], sig=True)
                    w = [prev, hslots[0].freed if l == 0 else k1_slot.freed]
                    e_ = act(dst[:, kind, m, :], P[bk][:, :], ACT.Copy, d, w)
                    pfree[bk] = e_
                    yield
                fs["e", kind] = e_
            k_done[l] = fs["end"] = [d, fs["e", 0], e_]
        for n in range(2):
            yield
            w = slice(n * 512, (n + 1) * 512)
            bk = misc_bank()
            d = mm(P[bk][:, :], con("ones", p=1), GR[:, w], True, True, gf, fs["end"], pfree[bk], sig=True)
            fs["gf"] = pfree[bk] = ts(DV, GF2[:, w], P[bk][:, :], -0.5, None, ALU.mult, None, d)

    def sine(bk, b, fr, d):
        v = ts(DV, FA[:, :], P[bk][0:64, 0:256], b, fr, ALU.add, ALU.mult, d, fs.get("end"))
        pfree[bk] = v
        yield
        v = ts(DV, FB[:, :], FA[:, :], 1.0 / (2 * np.pi), MAGIC, ALU.mult, ALU.add, v)
        yield
        v = ts(DV, FB[:, :], FB[:, :], -MAGIC, None, ALU.add, None, v)
        for c in (C1, C2, C3):
            yield
            v = stt(DV, FA[:, :], FB[:, :], -c, FA[:, :], ALU.mult, ALU.add, v)
        yield
        v = ts(DV, FA[:, :], FA[:, :], PI_LO, -PI_LO, ALU.min, ALU.max, v)
        fs["sin"] = act(FA[:, :], FA[:, :], ACT.Sin, v)
        yield

    def until_out(*gens):
        for g in gens:
            for _ in g:
                pass

    preps.append(prepare(0))
    prep(1)
    cmax = rs(6, 1)
    cnt_t = red(cmax, P[1][:, 192:224], ALU.max, done)
    pfree[1] = cnt_t = cp(DV, CNT[:, 0:1], cmax, cnt_t)
    prep(2)
    for g in range(GROUPS):
        if g % 2 == 0 and 0 < g < GROUPS - 2:
            preps.append(prepare(g // 2 + 1))
        in_products(g, 0, "gate")
        if g == 0:
            preps.append(prepare(1))
        in_products(g, 1, "up")
        hidden(g)
        if g % 2:
            prep(20)
        down(g)
        if g == 2:
            behind.append(filters())
        if g == GROUPS - 2:
            combine(g)
            bg_all()
            general_path()
            k_done[0] = cp(PO, K0[:, :, :, :], K0W[:, :, :, :], k_done[0], now())
    b2 = Region(Z, K1_AT)
    MG = b2("MG", [128, 4, 512])
    GSB = b2("GSB", [128, 2, 2, 256])
    X0 = b2("X0", [128, 4, 256])
    ZV = b2("ZV", [128, 4, 256])
    QPC = b2("QPC", [128, 2, 260])
    CVT = b2("CVT", [128, 2, 256])
    QT_AT = b2.o
    QT = b2("QT", [128, 4, 256])
    KT_AT = b2.o
    KTT = b2("KTT", [128, 4, 256])
    VV_AT = b2.o
    VV = b2("VV", [128, 2, 512])
    LAB_AT = b2.o
    LAB = b2("LAB", [128, 2, 2, 512])
    QE_AT = b2.o
    QE = b2("QE", [128, 2, 2, 130])
    KE = b2("KE", [128, 2, 2, 128])
    QE2_AT = b2.o
    QE2 = b2("QE2", [128, 2, 2, 130])
    KE2 = b2("KE2", [128, 2, 2, 128])
    OO_AT = b2.o
    OO = b2("OO", [128, 2, 512])
    SM_AT = b2.o
    QI = b2("QI", [128, 2, 128])
    ATT = b2("ATT", [128, 2, 128])
    AT2 = b2("AT2", [128, 2, 64])
    PW = b2("PW", [128, 4, 128], keep=False)
    KN = b2("KN", [128, 2, 128])
    UU = b2("UU", [128, 2, 128])
    W2A = b2("W2A", [128, 512])
    LRT = b2("LRT", [128, 256])
    CVT4 = at("CVT4", [128, 8, 128], LAB_AT)
    SGT = at("SGT", [128, 2, 512], KT_AT)
    PXP = at("PXP", [128, 4, 272], QE_AT)
    PSA = at("PSA", [128, 7, 272], LAB_AT)
    PH = at("PH", [128, 4, 256], LB_AT, F32R)
    PL = at("PL", [128, 4, 256], LB_AT + 4096, F32R)
    GO = OO
    GH = at("GH", [128, 4, 256], LAB_AT, F32R)
    GL = at("GL", [128, 4, 256], LAB_AT + 4096, F32R)
    ZVN = at("ZVN", [128, 2, 512], KT_AT)
    TMP = at("TMP", [128, 2, 512], VV_AT)
    TAB = at("TAB", [128, 4, 2, 256], QE_AT)
    YY = at("YY", [128, 2, 2, 512], SM_AT)
    assert SM_AT + 8192 <= K1_AT
    HH = at("HH", [128, 4, 256], OO_AT, F32R)
    HL = at("HL", [128, 4, 256], QT_AT, F32R)
    GB = at("GB", [128, 1024], LAB_AT)
    YB = at("YB", [128, 2, 1024], Z)
    FH = at("FH", [128, 4, 256], HB_AT, F32R)
    FL = at("FL", [128, 4, 256], HB_AT + 4096, F32R)
    GEL = at("GEL", [128, 2, 256], QT_AT)
    BN = at("BN", [128, 2, 512], SM_AT)
    BT = at("BT", [128, 4, 256], SM_AT + 4096)

    po = {}

    def post_piece(t, n, psum, done, *w):
        q = square(AC, psum, SM[:, 224 + 2 * t + n:225 + 2 * t + n], 1.0 / D, done, *w)

        def y():
            po[t, n] = (q, tt(DV, YB[:, t, n * 512:(n + 1) * 512], psum, GB[:, n * 512:(n + 1) * 512], ALU.mult, q,
                              po["gb"], *w))
            return po[t, n][1]

        po[t, n], po["y", t] = (q, None), y
        return y() if n == 0 else None

    def post_tile(t):
        rstd = rstd_steps(t, po[t, 0][0], po[t, 1][0], base=224)
        run(rstd, 1)
        po["y", t]()
        r, v = yield from rstd
        for n in range(2):
            yield
            x = X[:, t, n * 512:(n + 1) * 512]
            po["x", t, n] = stt(DV, x, YB[:, t, n * 512:(n + 1) * 512], r, x, ALU.mult, ALU.add, v, po[t, n][1])

    def load_gain(src, *d):
        po["ld"] = load(GB[:, :], src.partition_broadcast(128), *d)

    def halve_gain():
        po["gb"] = ts(DV, GB[:, :], GB[:, :], -0.5, None, ALU.mult, None, po["ld"])

    class Raw:

        def __init__(self, hi_at, lo_at, gain, name):
            self.hi = at(name + "h", [128, 8, 256], hi_at, F32R)
            self.lo = at(name + "l", [128, 8, 256], lo_at, F32R)
            self.g, self.toks, self.done, self.scale, self.part = gain, {}, [None, None], [None, None], {}

        def tok(self, k, t):
            return self.toks[k, t]

        def b(self, t, *d):
            for i in range(2):
                bk = 4 + 2 * t + i
                for q in range(4):
                    k = 4 * i + q
                    self.done[t] = tr(P[bk][:, q * 128:(q + 1) * 128], X[:, t, k * 128:(k + 1) * 128], d[i], pfree[bk], sig=True)
                self.part[t, i] = self.done[t]

        def c(self, t, *w):
            ta = slice(t * 128, (t + 1) * 128)
            for i in range(2):
                bk = 4 + 2 * t + i
                for q in range(4):
                    k = 4 * i + q
                    h = act(self.hi[:, k, ta], P[bk][:, q * 128:(q + 1) * 128], ACT.Copy, self.part[t, i], *w, scale=par(self.g, k))
                for q in range(4):
                    k = 4 * i + q
                    v = pfree[bk] = stt(DV, self.lo[:, k, ta], P[bk][:, q * 128:(q + 1) * 128], par(self.g, k),
                                        f(self.hi[:, k, ta]), ALU.mult, ALU.subtract, h, *w)
                    self.toks[k, t] = (h, v)

    def second_layer(l, nL, raw, start, second, nxt):
        KF = KS_[l]
        prev = start
        w2_t = load(W2A[0:49, :], A["gw2"][l], prev)
        pw_t = load(PW[:, :, :], A["pool_w"][l], prev)
        z2 = memset(PO, ATT[:, :, :], 0.0, prev)
        z0 = memset(PO, PXP[:, :, 0:8], 0.0, prev)
        z1 = memset(PO, PXP[:, :, 264:272], 0.0)
        tA = nL.tok
        v_t = [None] * 2

        def v_evac(t, bank, done):
            v_t[t] = act(VV[:, t, :], bank[:, :], ACT.Copy, done, prev, raw.scale, scale=C_[t])
            return v_t[t]

        n_tiles(raw.hi, raw.lo, raw.tok, v_evac, {(0, 3 if l else 1): second})
        go = [None, None]

        def g_evac(t, bank, done):
            go[t] = act(GO[:, t, :], bank[:, :], ACT.Copy, done, prev, raw.scale, scale=C_[t])
            return go[t]

        steps = n_out(raw.hi, raw.lo, raw.tok, g_evac)
        for t in range(2):
            steps[t]()
            nL.b(t)
            nL.c(t, prev)
        steps[2]()
        steps[3]()
        qz = memset(PO, QPC[:, :, :], 0.0, prev, PE.last())
        table("sigmoid_and_others")
        so = act(SGT[:, :, :], GO[:, :, :], ACT.Sigmoid, go, prev)
        so = tt(DV, GO[:, :, :], GO[:, :, :], SGT[:, :, :], ALU.mult, so)

        def px_evac(i):
            def ev(bank, done):
                px[i] = act(PXP[:, i, 8:264], bank[:, 0:256], ACT.Copy, done, prev)
                return px[i]
            return ev

        px = [None] * 4
        for i in range(4):
            t_out(HA, LA, tA, px_evac(i))
        pd, pw = [], {}

        def pool_difference(g):
            ws, c, v = pw[g]
            pd.append(stt(DV, PXP[:, g, 8:264], ws, c, PXP[:, g, 8:264], ALU.mult, ALU.subtract, v))

        for g in range(4):
            step = 1
            v = [px[g], z0, z1]
            n = 272
            b0 = max(0, 2 * g - 1)
            src = PXP[:, g, :]
            for i in range(g + 1):
                n -= step
                dst = PSA[:, b0 + i % 2, :]
                v = tt(PO, dst[:, 0:n], src[:, 0:n], src[:, step:step + n], ALU.add, v)
                src = dst
                step *= 2
            w = 2 << g
            ws = src[:, 8 - w // 2:8 - w // 2 + 256]
            for e0, c0 in ((0, 0), (248, 8)):
                v = tt(PO, ws[:, e0:e0 + 8], ws[:, e0:e0 + 8], con("edge", 16 * g + c0, 16 * g + c0 + 8), ALU.mult, v)
            pw[g] = (ws, 1.0 / w, v)

        q_t, k_t = [None] * 4, [None] * 4

        def q_evac(i):
            def ev(bank, done):
                q_t[i] = act(QT[:, i, :], bank[:, 0:256], ACT.Copy, done, prev, scale=128 ** -0.5)
                return q_t[i]
            return ev

        def k_evac(i):
            def ev(bank, done):
                k_t[i] = act(KTT[:, i, :], bank[:, 0:256], ACT.Copy, done, so)
                return k_t[i]
            return ev

        lr = {}

        def lr_evac(bank, done):
            lr["t"] = act(LRT[:, :], bank[:, 0:256], ACT.Identity, done, bias=con("lrone"))
            return lr["t"]

        t_out(HA, LA, tA, q_evac(0))
        pool_difference(0)
        t_out(HA, LA, tA, k_evac(0))
        pool_difference(1)
        pool_difference(2)
        t_out(HA, LA, tA, lr_evac)
        pool_difference(3)

        ph = [None] * 4
        for i in range(2):
            for g in (2 * i, 2 * i + 1):
                d = mm(P[6 + i][:, (g % 2) * 256:(g % 2) * 256 + 256], PW[:, g, :], PXP[:, g, 8:264], True, True,
                       pw_t, pd[g], pfree[6 + i], sig=(g % 2 == 1))
            for g in (2 * i, 2 * i + 1):
                a = act(PH[:, g, :], P[6 + i][:, (g % 2) * 256:(g % 2) * 256 + 256], ACT.Copy, d, prev,
                        scale=par(f"pool_s{l}", g))
                ph[g] = [a, None]
            for g in (2 * i, 2 * i + 1):
                pfree[6 + i] = ph[g][1] = stt(DV, PL[:, g, :], P[6 + i][:, (g % 2) * 256:(g % 2) * 256 + 256],
                                              par(f"pool_s{l}", g), f(PH[:, g, :]), ALU.mult, ALU.subtract, a)

        hy = {}

        def hy_evac(i):
            def ev(bank, done):
                r = i % 2
                t0 = act(QPC[:, r, 2:258], bank[:, 0:256], ACT.Copy, done, qz, hy.get(("c", i - 2)))
                out = X0[:, i, :] if i < 4 else ZV[:, i - 4, :] if i < 8 else CVT[:, r, :]
                v = t1 = act(out, bank[:, 0:256], ACT.Identity, prev, hy.get(("m", i - 2)), bias=par(f"hcb{l}", i),
                             scale=par(f"hcw{l}", 12 + i))
                for j in (0, 2):
                    v = stt(DV, out, QPC[:, r, j + 1:j + 257], par(f"hcw{l}", 12 * j + i), out, ALU.mult, ALU.add, v, t0)
                hy[("c", i)] = v
                if i >= 8:
                    v = tt(DV, ZV[:, i - 8, :], ZV[:, i - 8, :], out, ALU.mult, v)
                    hy[("m", i)] = v
                return t1
            return ev

        for i in range(1, 4):
            todo.append(lambda i=i: t_out(HA, LA, tA, q_evac(i)))
            todo.append(lambda i=i: t_out(HA, LA, tA, k_evac(i)))
        for i in range(12):
            todo.append(lambda i=i: t_out(HA, LA, tA, hy_evac(i)))
        table("natural_log_exp_and_others")
        la, mx = [None] * 2, [None] * 2

        def decay_products(t):
            for d in range(2):
                b = 4 + 2 * t + d
                dn = mm(P[b][:, :], LRT[32 * d:32 * d + 17, t * 128:(t + 1) * 128], W2A[32 * d:32 * d + 17, :], True, True,
                        lr["t"], w2_t, pfree[b], sig=True)
                pfree[b] = mx[t] = ts(DV, LAB[:, t, d, :], P[b][:, :], -20.0, None, ALU.max, None, dn, prev, pd)

        decay_products(0)
        fill(1)
        decay_products(1)
        for t in range(2):
            v = act(LAB[:, t, :, :], LAB[:, t, :, :], ACT.Exp, mx[t], scale=-1.0)
            v = act(LAB[:, t, :, :], LAB[:, t, :, :], ACT.Ln, v, bias=1.0)
            la[t] = ts(DV, LAB[:, t, :, :], LAB[:, t, :, :], -1.0 / 16.0, -1.0, ALU.mult, ALU.max, v)
        fill(2)

        ATM = {"o": ph[3][1], "s": None, "u": ph[3][1]}
        bufs = ((QE, KE), (QE2, KE2))
        for h in range(4):
            qe, ke = bufs[h % 2]
            hc = slice(h * 128, (h + 1) * 128)
            old = hy.get(("h", h - 2))
            for d in range(2):
                b = 4 + d
                for t in range(2):
                    dn = mm(P[b][:, t * 130:t * 130 + 130], LAB[:, t, d, hc], con("cf" if d == 0 else "cb"), True, True,
                            la[t], pfree[b], sig=(t == 1))
                pv = P[b][:, 0:260].rearrange("p (t c) -> p t c", t=2)
                e1 = act(qe[:, d, :, :], pv, ACT.Exp, dn, old, pd, ph[3][1])
                e2 = act(ke[:, d, :, :], pv[:, :, 0:128], ACT.Exp, dn, scale=-1.0)
                pfree[b] = e2
            for d in range(2):
                e1 = tt(DV, qe[:, d, :, 0:128], qe[:, d, :, 0:128], QT[:, h, :].rearrange("p (t c) -> p t c", t=2),
                        ALU.mult, e2, q_t[h])
                e2 = tt(DV, ke[:, d, :, :], ke[:, d, :, :], KTT[:, h, :].rearrange("p (t c) -> p t c", t=2),
                        ALU.mult, k_t[h])
            for d in range(2):
                e1 = ts(DV, QI[:, d, :], qe[:, d, 1 - d, 0:128], qe[:, d, 1 - d, 128:129], None, ALU.mult, None, e1,
                        ATM["o"])
            fill(1)
            for d in range(2):
                dn = tr(P[5][:, d * 128:(d + 1) * 128], ke[:, d, d, :], e2, pfree[5], sig=(d == 1))
            kn = act(KN[:, :, :], P[5][:, 0:256].rearrange("p (d c) -> p d c", d=2), ACT.Copy, dn, ATM["u"])
            for t in range(2):
                c0 = t * 192
                kf, kb, qf, qb = ke[:, 0, t, :], ke[:, 1, t, :], qe[:, 0, t, 0:128], qe[:, 1, t, 0:128]
                mm(P[4][0:64, c0:c0 + 128], kf[:, 0:64], qf, True, True, e1, e2, pfree[4])
                mm(P[4][64:128, c0 + 64:c0 + 128], kf[:, 64:128], qf[:, 64:128], True, True)
                mm(P[4][64:128, c0:c0 + 64], kb[:, 64:128], qb[:, 0:64], True, True)
                mm(P[4][0:64, c0 + 128:c0 + 192], kb[:, 0:64], qb[:, 0:64], True, True)
                dn = mm(P[4][64:128, c0 + 128:c0 + 192], kb[:, 64:128], qb[:, 64:128], True, True, sig=(t == 1))
            hy[("h", h)] = dn
            sv = P[4][:, 0:384].rearrange("p (t c) -> p t c", t=2)
            a1 = tt(DV, ATT[:, :, :], sv[:, :, 0:128], con("m1").unsqueeze(1).broadcast_to([128, 2, 128]), ALU.mult, dn,
                    ATM["o"], z2)
            a2 = tt(DV, AT2[:, :, :], sv[:, :, 128:192], con("m2").unsqueeze(1).broadcast_to([128, 2, 64]), ALU.mult,
                    ATM["s"])
            pfree[4] = a2
            for lo in (0, 64):
                ATM["s"] = tt(DV, ATT[lo:lo + 64, :, lo:lo + 64], ATT[lo:lo + 64, :, lo:lo + 64], AT2[lo:lo + 64, :, :],
                              ALU.add, a1, a2)
            fill(1)
            for d in range(2):
                dn = mm(P[5][:, 256 + d * 128:384 + d * 128], KN[:, d, :], VV[:, d, hc], True, True, kn, v_t[d],
                        sig=(d == 1))
            ATM["u"] = dn
            for d in range(2):
                u_ = act(UU[:, d, :], P[5][:, 256 + d * 128:384 + d * 128], ACT.Copy, dn, ATM["o"],
                         scale=qe[:, d, d, 129:130])
            pfree[5] = u_
            fill(1)
            for t in range(2):
                mm(P[6 + t][:, hc], ATT[:, t, :], VV[:, t, hc], True, False, ATM["s"], pfree[6 + t])
                ATM["o"] = mm(P[6 + t][:, hc], QI[:, 1 - t, :], UU[:, 1 - t, :], False, True, u_, sig=True)
            fill(1)
        hd_free = [ATM["o"], u_, ATM["s"]]
        r = None
        for t in range(2):
            for h in range(4):
                r = act(CVT4[:, 4 * t + h, :], P[6 + t][:, h * 128:(h + 1) * 128], ACT.Square, ATM["o"],
                        accum=SM[:, 4 + 4 * t + h:5 + 4 * t + h])
        fill(1)
        r = rstd_of(SM[:, 4:12], 8, 1.0 / 128, EPS, r)
        while todo:
            fill(1)
        tab_t = load(TAB[:, :, :, :], A["dft"], hd_free, now())
        table("sigmoid_and_others")

        mg = [None] * 4
        gs = {}
        state = {"last": None}

        def gate_evac(i, p):
            def ev(bank, done):
                gs[i] = act(GSB[:, p % 2, i % 2, :], bank[:, 0:256], ACT.Sigmoid, done, mg_used[p % 2], prev)
                return gs[i]
            return ev

        mg_used = [None, None]

        def br_evac(p, which):
            def ev(bank, done):
                g_ = GSB[:, p % 2, :, :].rearrange("p a b -> p (a b)")
                if which == 0:
                    mg[p] = mg_used[p % 2] = tt(DV, MG[:, p, :], bank[:, :], g_, ALU.mult, done, gs[2 * p + 1], prev)
                    return mg[p]
                v = tt(DV, g_, bank[:, :], g_, ALU.mult, done, gs[2 * p + 1])
                mg[p] = mg_used[p % 2] = tt(DV, MG[:, p, :], MG[:, p, :], g_, ALU.add, v)
                if which == 2:
                    for k in (2 * p, 2 * p + 1):
                        src = MG[:, p, (k % 2) * 256:(k % 2) * 256 + 256]
                        a = act(HB[:, k, :], src, ACT.Copy, mg[p], hy["k"])
                        ym[k] = [a, tt(DV, LB[:, k, :], src, f(HB[:, k, :]), ALU.subtract, a, state["last"])]
                return v
            return ev

        ym = [None] * 8

        def branch_steps(which, hi, lo, tok):
            out = []
            for p in range(4):
                for i in (2 * p, 2 * p + 1):
                    out.append(lambda i=i, p=p: t_out(HA, LA, tA, gate_evac(i, p)))
                out.append(lambda p=p: t_out(hi, lo, tok, br_evac(p, which), kt=4, parts=2))
            return out

        todo.extend(branch_steps(0, PH, PL, lambda k, t: ph[k]))
        yg = [None] * 4
        for t in range(2):
            for h in range(4):
                o_ = GO[:, t, h * 128:(h + 1) * 128]
                y_ = stt(DV, o_, P[6 + t][:, h * 128:(h + 1) * 128], SM[:, 4 + 4 * t + h:5 + 4 * t + h], o_,
                         ALU.mult, ALU.mult, r, so)
            pfree[6 + t] = y_
        fill(2)
        for t in range(2):
            for c in range(4):
                dn = tr(P[4 + t][:, c * 128:(c + 1) * 128], ZV[:, c, t * 128:(t + 1) * 128], hy[("m", 8 + c)],
                        pfree[4 + t], sig=(c == 3))
            pfree[4 + t] = zn = act(ZVN[:, t, :], P[4 + t][:, :], ACT.Copy, dn, hd_free)
        for i in range(2):
            for h in (2 * i, 2 * i + 1):
                for t in range(2):
                    dn = tr(P[6 + i][:, (h % 2) * 256 + t * 128:(h % 2) * 256 + t * 128 + 128],
                            GO[:, t, h * 128:(h + 1) * 128], y_, pfree[6 + i], sig=(t == 1))
            for h in (2 * i, 2 * i + 1):
                a = act(GH[:, h, :], P[6 + i][:, (h % 2) * 256:(h % 2) * 256 + 256], ACT.Copy, dn, hd_free,
                        scale=par(f"gla_norm{l}"))
                yg[h] = [a, None]
            for h in (2 * i, 2 * i + 1):
                pfree[6 + i] = yg[h][1] = stt(DV, GL[:, h, :], P[6 + i][:, (h % 2) * 256:(h % 2) * 256 + 256],
                                              par(f"gla_norm{l}"), f(GH[:, h, :]), ALU.mult, ALU.subtract, a)
        go_free = dn
        while len(todo):
            fill(1)
        todo.extend(branch_steps(1, GH, GL, lambda k, t: yg[k]))
        yv = None
        for m in range(2):
            mc = slice(m * 128, (m + 1) * 128)
            zb = []
            for kind in range(2):
                b = 4 + 2 * m + kind
                for t in range(2):
                    dn = mm(P[b][:, :], TAB[:, kind, t, mc], ZVN[:, t, :], t == 0, t == 1, tab_t, zn, pfree[b],
                            sig=(t == 1))
                zb.append(dn)
            zr, zs = P[4 + 2 * m][:, :], P[5 + 2 * m][:, :]
            a = tt(DV, YY[:, 0, m, :], zr, KF[:, 0, m, :], ALU.mult, zb[0], hd_free, k_done[l])
            b_ = tt(DV, TMP[:, 0, :], zs, KF[:, 1, m, :], ALU.mult, zb[1], yv)
            c_ = tt(DV, YY[:, 1, m, :], zs, KF[:, 0, m, :], ALU.mult)
            pfree[5 + 2 * m] = c_
            d_ = tt(DV, TMP[:, 1, :], zr, KF[:, 1, m, :], ALU.mult)
            pfree[4 + 2 * m] = d_
            y1 = tt(PO, YY[:, 0, m, :], YY[:, 0, m, :], TMP[:, 0, :], ALU.subtract, a, b_)
            yv = tt(PO, YY[:, 1, m, :], YY[:, 1, m, :], TMP[:, 1, :], ALU.add, c_, d_)
            fill(2)
        hy["k"] = d_
        fill(4)
        yh = [None] * 4
        for i in range(2):
            for c in (2 * i, 2 * i + 1):
                out = P[4 + i][:, (c % 2) * 256:(c % 2) * 256 + 256]
                for kind in range(2):
                    for m in range(2):
                        dn = mm(out, YY[:, kind, m, c * 128:(c + 1) * 128], TAB[:, 2 + kind, m, :],
                                kind == 0 and m == 0, kind == 1 and m == 1, yv, pfree[4 + i],
                                sig=(kind == 1 and m == 1))
            x0 = X0[:, 2 * i:2 * i + 2, :].rearrange("p a b -> p (a b)")
            v = tt(DV, x0, P[4 + i][:, :], x0, ALU.mult, dn)
            pfree[4 + i] = v
            for c in (2 * i, 2 * i + 1):
                a = act(HH[:, c, :], X0[:, c, :], ACT.Copy, v, go_free, hd_free)
                yh[c] = [a, tt(DV, HL[:, c, :], X0[:, c, :], f(HH[:, c, :]), ALU.subtract, a)]
        while todo:
            fill(1)
        state["last"] = PE.last()
        load_gain(A["post"][l, 0], state["last"], DV.last())
        todo.extend(branch_steps(2, HH, HL, lambda k, t: yh[k]))
        while todo:
            fill(1)

        halve_gain()
        prev = now()
        table("natural_log_exp_and_others")
        nF = Norm(X, f"ffn_pre{l}", HA, LA)
        tM = lambda k, t: ym[k]
        for s in n_out(HB, LB, tM, lambda t, bank, done: post_piece(t, 0, bank[:, :], done, prev)):
            s()

        rawF = Raw(QE_AT, Z + 8192, f"ffn_pre{l}", f"rawf{l}")

        def y_evac(t, bank, done):
            post_piece(t, 1, bank[:, :], done, prev)
            if t == 0:
                run(post_tile(0))
            else:
                run(post_tile(1))
                run(norm_scale(nF, rawF, 0))
            return po[t, 1][1]

        def raw_step(t):
            rawF.b(t, po["x", t, 0], po["x", t, 1])
            rawF.c(t, prev)

        def y_mid():
            raw_step(0)

        n_tiles(HB, LB, tM, y_evac, {(1, 2): lambda: split_chunks(st["chunk"] + 4), (1, 3): y_mid}, ahead=0)

        load_gain(A["post"][l, 1], po[1, 1][1])
        before, prev = prev, now()
        qz = memset(PO, QPC[:, :, :], 0.0, prev)
        tA = nF.tok
        ff = {}
        bn = [None, None]
        tb = [stream_bank(True), stream_bank(True)]

        def bn_evac(t, bank, done):
            bn[t] = act(BN[:, t, :], bank[:, :], ACT.Copy, done, prev, rawF.scale[t], scale=C_[t])
            return bn[t]

        def bn_transposes(t):
            for i in range(4):
                out = P[tb[i // 2]][:, (i % 2) * 256 + t * 128:(i % 2) * 256 + t * 128 + 128]
                dn = tr(out, BN[:, t, i * 128:(i + 1) * 128], bn[t], pfree[tb[i // 2]] if t == 0 else None, sig=(i % 2 == 1))
                if i % 2:
                    ff["bt", i // 2] = dn

        def tile_1():
            raw_step(1)
            run(norm_scale(nF, rawF, 1))
            split_chunks(st["chunk"] + 1)

        def normed_0():
            nF.b(0)
            nF.c(0, before)
            split_chunks(st["chunk"] + 2)

        def norm_1():
            nF.b(1)
            nF.c(1, before)

        n_tiles(rawF.hi, rawF.lo, rawF.tok, bn_evac,
                {(0, 3): tile_1, (1, 1): normed_0, (1, 2): norm_1, (1, 3): lambda: bn_transposes(0)}, ahead=0, split=False)
        split_chunks(st["chunk"] + 2)

        def bn_end():
            bn_transposes(1)
            for j in range(2):
                held.discard(tb[j])
                pfree[tb[j]] = ff["bs", j] = act(BT[:, 2 * j:2 * j + 2, :],
                                                 P[tb[j]][:, :].rearrange("p (k t) -> p k t", k=2), ACT.Copy, ff["bt", j])

        def a_evac(i):
            def ev(bank, done):
                if i == 0:
                    bn_end()
                r = i % 2
                t0 = act(QPC[:, r, 2:258], bank[:, 0:256], ACT.Copy, done, qz, ff.get(("c", i - 2)))
                out = CVT[:, r, :]
                v = t1 = act(out, bank[:, 0:256], ACT.Identity, ff.get(("g", i - 2)), bias=par(f"fcb{l}", i),
                             scale=par(f"fcw{l}", 22 + i))
                if i == 0:
                    table("gelu_and_others")
                for j in (0, 2):
                    v = stt(DV, out, QPC[:, r, j + 1:j + 257], par(f"fcw{l}", 22 * j + i), out, ALU.mult, ALU.add, v, t0)
                ff[("c", i)] = v
                ff[("g", i)] = act(GEL[:, r, :], out, ACT.Gelu, v, ff.get(("b", i - 2)), prev)
                return t1
            return ev

        def b_evac(i):
            def ev(bank, done):
                r = i % 2
                g_ = GEL[:, r, :]
                v = tt(DV, g_, bank[:, 0:256], g_, ALU.mult, done, ff[("g", i)])
                a = act(FH[:, i % 4, :], g_, ACT.Copy, v, ff.get(("d", i - 4)), prev)
                ff[("b", i)] = tt(DV, FL[:, i % 4, :], g_, f(FH[:, i % 4, :]), ALU.subtract, a)
                ff[("y", i)] = [a, ff[("b", i)]]
                return v
            return ev

        def down(i, parts, tiles):
            hi, lo, t1, t2 = parts
            y = ff[("y", i)]
            for t in tiles:
                ta = slice(t * 128, (t + 1) * 128)
                for n in range(2):
                    out = P[4 + 2 * t + n][:, :]
                    w = slice(n * 512, (n + 1) * 512)
                    mm(out, FH[:, i % 4, ta], hi[:, w], i == 0, False, t1, y[0], pfree[4 + 2 * t + n] if i == 0 else None)
                    mm(out, FL[:, i % 4, ta], hi[:, w], False, False, y[1])
                    dn = mm(out, FH[:, i % 4, ta], lo[:, w], False, i == 21, t2, sig=(n == 1 or i == 21))
                    ff["n", n] = dn
            return dn

        for i in range(22):
            t_out(HA, LA, tA, a_evac(i))
            if i < 4:
                b_evac(i)(BT[:, i, :], ff["bs", i // 2])
            else:
                t_out(HA, LA, tA, b_evac(i), split=False)
            if i == 3:
                halve_gain()
            if 1 < i < 20:
                c, parts = take()
                ff[("d", i - 2)] = down(i - 2, parts, (0, 1))
                give(c, ff[("d", i - 2)])
        split_chunks(st["chunk"] + 4)
        table("natural_log_exp_and_others")
        got = [take(False) for _ in range(4)]
        start = now()
        raw = Raw(Z + 8192, Z + 16384, f"mix_pre{l + 1}", "rawb") if nxt else None

        for t, j in ((0, 0), (0, 1), (0, 2), (1, 0), (0, 3), (1, 1), (1, 2), (1, 3)):
            c, parts = got[j]
            dn = down(18 + j, parts, (t,))
            if t == 1:
                give(c, dn)
            if j == 3:
                for n in range(2):
                    pfree[4 + 2 * t + n] = post_piece(t, n, P[4 + 2 * t + n][:, :], ff["n", n], prev)
                if t and raw:
                    raw.b(0, po["x", 0, 0], po["x", 0, 1])
                    raw.c(0, start)
                    split_chunks(st["chunk"] + LAHEAD)
                run(post_tile(t))
                pfree[5 + 2 * t] = po[t, 1][1]
                if t == 0:
                    split_chunks(st["chunk"] + 2)

        def second():
            raw.b(1, po["x", 1, 0], po["x", 1, 1])
            raw.c(1, start)
            alternate(*[norm_scale(nxt, raw, t) for t in range(2)])

        return raw, start, second

    nL = [Norm(X, "mix_pre0", HA, LA), Norm(X, "mix_pre1", HA, LA), None]
    bg_all()
    table("natural_log_exp_and_others")
    sq = {}

    def norm_scale(nrm, raw, t):
        s_ = [ms(t, n, X[:, t, n * 512:(n + 1) * 512], po["x", t, n]) for n in range(2)]
        yield
        yield from nrm.a_steps(t, s_)
        yield
        raw.scale[t] = ts(DV, C_[t], nrm.rs[t][0], -0.5, None, ALU.mult, None, nrm.rs[t][1])

    def last_norm(t):
        s_ = [ms(t, n, X[:, t, n * 512:(n + 1) * 512], sq[t, n]) for n in range(2)]
        yield
        r, v = yield from rstd_steps(t, s_)
        yield
        c3 = ts(DV, SM[:, 14 + t:15 + t], r, -0.5, None, ALU.mult, None, v)
        s_ = []
        for m in range(2):
            yield
            x = X[:, t, m * 512:(m + 1) * 512]
            a = po["x", t, m] = stt(DV, x, x, r, GF2[:, m * 512:(m + 1) * 512], ALU.mult, ALU.mult, v, fs["gf"],
                                    raw.done[t])
            s_.append(ms(t, m, x, a))
        yield
        yield from nL[0].a_steps(t, s_)
        yield
        raw.scale[t] = stt(DV, C_[t], nL[0].rs[t][0], -0.5, SM[:, 14 + t:15 + t], ALU.mult, ALU.mult, nL[0].rs[t][1], c3)

    assert all(w_.freed for w_ in wslots)
    his[:] = [(WH[:, i, :], wslots[i // 2].freed) for i in range(NH)]
    st["split"] = st["chunk"] = 2 * U_B2
    st["end"] = 2 * U_B2 + 2 * L_CHUNKS
    raw = Raw(Z, Z + 8192, "gfin", "rawa")
    start = now()
    mbank[0] = 3

    def between(t, n, v):
        sq[t, n] = v
        if (t, n) == (1, 0):
            raw.b(0, sq[0, 0], sq[0, 1])
            split_chunks(2 * U_B2 + 2)

    combine(GROUPS - 1, between)
    raw.c(0, start)
    split_chunks(2 * U_B2 + LAHEAD)

    def second():
        raw.b(1, sq[1, 0], sq[1, 1])
        raw.c(1, start)
        alternate(last_norm(0), last_norm(1))

    for l in range(2):
        raw, start, second = second_layer(l, nL[l], raw, start, second, nL[l + 1])
    s_out = sem("s_out")
    for t in range(2):
        for n in range(2):
            w = slice(n * 512, (n + 1) * 512)
            SP.wait(po["x", t, n])
            SP.q.append(lambda e, t=t, w=w: e.dma_start(A["out"][0, t * 128:(t + 1) * 128, w], X[:, t, w]).then_inc(s_out, 16))
    SP.q.append(lambda e: e.wait_ge(s_out, 64))
    return finish()


def host_arrays(I):
    ws = np.zeros((N_UNITS, 128, 2048), np.float32)
    flat = ws.reshape(N_UNITS, 128, 2, 1024)

    def put(c, a):
        flat[c // 2, :, c % 2, :] = a.reshape(128, 1024)

    def kt(w):
        return w.reshape(-1, 128, w.shape[1]).transpose(1, 0, 2)

    def t_cols(c, w, col, n):
        for i in range(n):
            put(c + i, kt(w[:, col + 128 * i:col + 128 * i + 128]))

    def n_cols(c, w, col, pairs=(0, 1, 2, 3)):
        a = kt(w[:, col:col + 512])
        for i, j in enumerate(pairs):
            put(c + i, a[:, 2 * j:2 * j + 2])

    w, kvx = I["w_in"][0], I["w_kv_x"][0]
    gates = np.zeros((1024, 128), np.float32)
    for i, kind in enumerate((0, 2, 1, 3)):
        gates[:, 32 * i:32 * i + 4] = w[:, 2048 + 4 * kind:2052 + 4 * kind]
    n_cols(0, w, 1024)
    t_cols(4, gates, 0, 1)
    for i in range(4):
        t_cols(5 + 2 * i, w, 128 * i, 1)
        put(6 + 2 * i, kt(w[:, 1536:2048])[:, 2 * i:2 * i + 2])
        t_cols(13 + 2 * i, w, 512 + 128 * i, 1)
        t_cols(14 + 2 * i, kvx, 128 * i, 1)
    n_cols(21, w, 2064 + 512)
    t_cols(25, w, 2064, 4)
    t_cols(29, kvx, 512, 2)
    for h in range(2):
        n_cols(31 + 4 * h, kvx, 1024 + 512 * h)
        n_cols(39 + 4 * h, I["w_out"][0], 512 * h, (2, 3, 0, 1))
        n_cols(57 + 4 * h, I["w_o_x"][0], 512 * h)
    t_cols(47, kvx, 768, 2)
    t_cols(49, I["w_q_x"][0], 0, 8)

    for g in range(GROUPS):
        u = U_MOE + g * UNITS_PER_GROUP
        for m, name in enumerate(("w_gate", "w_up")):
            a = I[name][0][2 * g:2 * g + 2].reshape(2, 4, 2, 128, 512)
            ws[u + 4 * m:u + 4 * m + 4] = a.transpose(1, 3, 0, 2, 4).reshape(4, 128, 2048)
        a = I["w_down"][0][2 * g:2 * g + 2].reshape(2, 4, 128, 1024)
        ws[u + 8:u + 12] = a.transpose(1, 2, 0, 3).reshape(4, 128, 2048)

    for l in range(2):
        c0 = 2 * U_B2 + l * L_CHUNKS
        at = lambda n: c0 + L_AT[n]
        w2 = I["w_in_2"][l]
        t_cols(at("pool"), w2, 3616, 4)
        for h in range(4):
            for m in range(2):
                t_cols((at("qk") + 2 * (h - 1) if h else at("qk0")) + m, w2, 1536 + 512 * m + 128 * h, 1)
        n_cols(at("v"), w2, 2560)
        n_cols(at("g"), w2, 3072)
        lr = np.zeros((1024, 128), np.float32)
        lr[:, 0:16] = w2[:, 3584:3600]
        lr[:, 32:48] = w2[:, 3600:3616]
        t_cols(at("lr"), lr, 0, 1)
        t_cols(at("hy"), w2, 0, 12)
        for b, (n, src) in enumerate((("pb", "pool"), ("gb", "gla"), ("hb", "hyena"))):
            gate0 = 4128 + 1024 * {"hyena": 0, "gla": 1, "pool": 2}[src]
            br = I[f"w_br_{src}_2"][l]
            for p in range(4):
                t_cols(at(n) + 3 * p, w2, gate0 + 256 * p, 2)
                put(at(n) + 3 * p + 2, np.stack([kt(br[:, 256 * p + 128 * i:256 * p + 128 * i + 128]) for i in range(2)], axis=1))
        for h in range(2):
            n_cols(at("wo") + 4 * h, I["w_out_2"][l], 512 * h)
        up, dn = I["ffn_w_up_2"][l], kt(I["ffn_w_down_2"][l])
        c = at("ffn")
        n_cols(c, up, 2816)
        c += 4
        for i in range(22):
            t_cols(c, up, 128 * i, 1)
            c += 1
            if i > 3:
                t_cols(c, up, 2816 + 128 * i, 1)
                c += 1
            if 1 < i < 20:
                put(c, dn[:, i - 2])
                c += 1
        for i in range(4):
            put(c + i, dn[:, 18 + i])

    gw2 = np.zeros((2, 49, 512), np.float32)
    for l in range(2):
        for d in range(2):
            gw2[l, 32 * d:32 * d + 16] = I["gla_gate_w2_2"][l, d]
            gw2[l, 32 * d + 16] = I["gla_gate_b_2"][l, d]

    par = np.zeros((128, N_PAR), np.float32)

    def vec(name, v):
        v = v.reshape(-1, 128).T if v.size >= 128 else v.reshape(-1, 1)
        par[:v.shape[0], PAR[name]:PAR[name] + v.shape[1]] = v

    for n in ("g_mix", "g_mem", "g_xattn", "g_moe", "g_head", "conv_w", "conv_b"):
        vec(n, I[n][0])
    for i, kind in enumerate((0, 2, 1, 3)):
        par[32 * i:32 * i + 4, PAR["gate_b"]] = I["gate_b"][0][4 * kind:4 * kind + 4]
    par[0:36, PAR["br"]] = np.concatenate([I["b_rg"][0], I["b_re"][0]])
    vec("gfin", I["g_final"])
    for l in range(2):
        vec(f"mix_pre{l}", I["norm_mix_pre_2"][l])
        vec(f"ffn_pre{l}", I["norm_ffn_pre_2"][l])
        vec(f"hcw{l}", I["hy_conv_w_2"][l])
        vec(f"hcb{l}", I["hy_conv_b_2"][l])
        for i, n in enumerate(("b1", "freq1", "b2", "freq2")):
            par[0:64, PAR[f"hf{l}"] + i] = I[f"hy_filt_{n}_2"][l]
        vec(f"gla_norm{l}", I["gla_norm_2"][l])
        vec(f"pool_s{l}", I["pool_scale_2"][l])
        vec(f"fcw{l}", I["ffn_conv_w_2"][l])
        vec(f"fcb{l}", I["ffn_conv_b_2"][l])
    out = {
        "x": I["x"][0].reshape(2, 128, 1024), "mem": I["mem"][0].reshape(2, 128, 1024), "ws": ws, "par": par,
        "con": constants(), "ln_g": I["ln_v_g"][0], "ln_b": I["ln_v_b"][0], "b_s": I["b_s"],
        "w_sT": I["w_s"][0].transpose(2, 0, 1),
        "wr": kt(np.concatenate([I["w_rg"][0], I["w_re"][0]], axis=1)),
        "gw2": gw2, "pool_w": I["pool_w_2"].transpose(0, 2, 1, 3), "g_final": I["g_final"],
        "post": np.stack([I["norm_mix_post_2"], I["norm_ffn_post_2"]], axis=1),
        "dft": dft_tables(), "decay": filter_tables()[1], "zpos": filter_tables()[0],
        "hw1": I["hy_filt_w1_2"], "hw2": I["hy_filt_w2_2"], "hw3": I["hy_filt_w3_2"], "hbias": I["hy_bias_2"],
    }
    return {k: np.ascontiguousarray(v) for k, v in out.items()}


def kernel(**inputs):
    import numpy as _np
    import concourse.bacc as _bacc
    from concourse import mybir as _mybir
    from concourse.bass_utils import run_bass_kernel_spmd as _run

    nc = _bacc.Bacc("TRN2", target_bir_lowering=False, num_devices=1)
    arrays, args = {}, {}
    for name, a in host_arrays({k: _np.asarray(v) for k, v in inputs.items()}).items():
        arrays[f"in_{name}_dram"] = a
        args[name] = nc.dram_tensor(f"in_{name}_dram", a.shape, _mybir.dt.from_np(a.dtype), kind="ExternalInput").ap()
    args["out"] = nc.dram_tensor("out_0_dram", (1, 256, 1024), _mybir.dt.float32, kind="ExternalOutput").ap()
    program(nc, args)
    r = _run(nc, [arrays], core_ids=[0])
    return r.results[0]["out_0_dram"]
```
